# Optimizing a Trainium2 kernel written in Bass

```python
import jax
import jax.numpy as jnp
from jax import lax
import numpy as np
import jax, jax.numpy as jnp

D_MODEL = 1024
BATCH = 1
SEQ = 256
DEPTH = 2

CTX_LEN = 256
GRID_W = 64
CONV_DIM = 512
CONV_K = 31
NA_HEADS = 8
HEAD_DIM = 64
NA_DIM = NA_HEADS * HEAD_DIM
NA_KH_MAX = 8
NA_KW = 16
ROPE_THETA = 10000.0
FFN_DIM = 2816
FFN_CONV_K = 3
N_BRANCH = 2
EPS = 1e-6
GLU_END = 2 * CONV_DIM
QKV_END = GLU_END + 3 * NA_DIM
IN_DIM = QKV_END + N_BRANCH * D_MODEL


def rmsnorm(x, g):
    xf = x.astype(jnp.float32)
    y = xf * lax.rsqrt(jnp.mean(xf * xf, axis=-1, keepdims=True) + EPS)
    return (y * g.astype(jnp.float32)).astype(x.dtype)

def layernorm(x, g, b):
    xf = x.astype(jnp.float32)
    mu = jnp.mean(xf, axis=-1, keepdims=True)
    var = jnp.mean(jnp.square(xf - mu), axis=-1, keepdims=True)
    y = (xf - mu) * lax.rsqrt(var + EPS)
    return (y * g.astype(jnp.float32) + b.astype(jnp.float32)).astype(x.dtype)

def modulate(h, shift, scale):
    return h * (1 + scale) + shift

def dwconv1d(x, w, b):
    k, ch = w.shape
    y = lax.conv_general_dilated(
        x, w.astype(x.dtype)[:, None, :], window_strides=(1,),
        padding=[(k // 2, k // 2)],
        dimension_numbers=("NWC", "WIO", "NWC"),
        feature_group_count=ch)
    return y + b

def split_heads(t):
    b, l, _ = t.shape
    return t.reshape(b, l, NA_HEADS, HEAD_DIM).transpose(0, 2, 1, 3)

def merge_heads(t):
    b, h, l, d = t.shape
    return t.transpose(0, 2, 1, 3).reshape(b, l, h * d)

def rope_2d(x, pos_row, pos_col):
    half = HEAD_DIM // 2
    inv_freq = ROPE_THETA ** (-jnp.arange(0, half, 2, dtype=jnp.float32) / half)

    def rot(xa, pos):
        ang = pos[:, None] * inv_freq[None, :]
        cos, sin = jnp.cos(ang), jnp.sin(ang)
        x1, x2 = jnp.split(xa.astype(jnp.float32), 2, axis=-1)
        return jnp.concatenate([x1 * cos - x2 * sin, x1 * sin + x2 * cos], axis=-1)

    out = jnp.concatenate([rot(x[..., :half], pos_row), rot(x[..., half:], pos_col)], axis=-1)
    return out.astype(x.dtype)

def conv_branch(p_glu, dw, dw_b, ln_g, ln_b, w_o):
    a, g = jnp.split(p_glu, 2, axis=-1)
    u = a * jax.nn.sigmoid(g)
    u = dwconv1d(u, dw, dw_b)
    u = jax.nn.silu(layernorm(u, ln_g, ln_b))
    return u @ w_o

def neighbourhood_attention(q, k, v, k_ctx, v_ctx, rpb):
    b, h, l, dh = q.shape
    rows = l // GRID_W
    kh = min(NA_KH_MAX, rows)
    n_win = kh * NA_KW
    qg = q.reshape(b, h, rows, GRID_W, dh)
    kg = k.reshape(b, h, rows, GRID_W, dh)
    vg = v.reshape(b, h, rows, GRID_W, dh)
    cols = jnp.arange(GRID_W)
    col_start = jnp.clip(cols - NA_KW // 2, 0, GRID_W - NA_KW)
    col_idx = col_start[:, None] + jnp.arange(NA_KW)[None, :]
    dc_idx = col_idx - cols[:, None] + (NA_KW - 1)
    scale = HEAD_DIM ** -0.5

    def row_block(r):
        row_start = jnp.clip(r - kh // 2, 0, rows - kh)
        q_r = lax.dynamic_index_in_dim(qg, r, axis=2, keepdims=False)
        k_band = lax.dynamic_slice_in_dim(kg, row_start, kh, axis=2)
        v_band = lax.dynamic_slice_in_dim(vg, row_start, kh, axis=2)
        k_win = k_band[:, :, :, col_idx]
        v_win = v_band[:, :, :, col_idx]
        s_win = jnp.einsum("bhqd,bhiqjd->bhqij", q_r, k_win,
                           preferred_element_type=jnp.float32) * scale
        dr_idx = row_start + jnp.arange(kh) - r + (NA_KH_MAX - 1)
        bias = rpb[:, dr_idx[None, :, None], dc_idx[:, None, :]]
        s_win = s_win + bias[None].astype(jnp.float32)
        s_ctx = jnp.einsum("bhqd,bhcd->bhqc", q_r, k_ctx,
                           preferred_element_type=jnp.float32) * scale
        s = jnp.concatenate([s_win.reshape(b, h, GRID_W, n_win), s_ctx], axis=-1)
        p = jax.nn.softmax(s, axis=-1).astype(v.dtype)
        p_win = p[..., :n_win].reshape(b, h, GRID_W, kh, NA_KW)
        p_ctx = p[..., n_win:]
        return (jnp.einsum("bhqij,bhiqjd->bhqd", p_win, v_win)
                + jnp.einsum("bhqc,bhcd->bhqd", p_ctx, v_ctx))

    out = lax.map(row_block, jnp.arange(rows))
    return out.transpose(1, 2, 0, 3, 4).reshape(b, h, l, dh)

def context_attention(q, k, v):
    s = jnp.einsum("bhqd,bhkd->bhqk", q, k, preferred_element_type=jnp.float32) * (HEAD_DIM ** -0.5)
    p = jax.nn.softmax(s, axis=-1).astype(v.dtype)
    return jnp.einsum("bhqk,bhkd->bhqd", p, v)

def gated_merge(p_gate, y_conv, y_attn, w_o):
    g_conv, g_attn = jnp.split(jax.nn.sigmoid(p_gate), 2, axis=-1)
    return (g_conv * y_conv + g_attn * y_attn) @ w_o

def conv_ffn(h, w_up, dw, dw_b, w_down):
    u = dwconv1d(h @ w_up, dw, dw_b)
    a, g = jnp.split(u, 2, axis=-1)
    return (jax.nn.silu(g) * a) @ w_down

def first_inputs(seed: int = 0) -> dict:
    key = jax.random.key(seed)
    ks = jax.random.split(key, 24)
    n = jax.random.normal
    f32 = jnp.float32
    D = D_MODEL
    return {
        "x": n(ks[0], (BATCH, SEQ, D), f32),
        "c": n(ks[1], (BATCH, D), f32),
        "ctx": n(ks[2], (BATCH, CTX_LEN, D), f32),
        "c_ctx": n(ks[3], (D,), f32),
        "w_ada": n(ks[4], (DEPTH, D, 6 * D), f32) * (0.5 * D ** -0.5),
        "b_ada": n(ks[5], (DEPTH, 6 * D), f32) * 0.02,
        "norm1_g": 1.0 + 0.02 * n(ks[6], (DEPTH, D), f32),
        "w_in": n(ks[7], (DEPTH, D, IN_DIM), f32) * D ** -0.5,
        "conv_dw": n(ks[8], (DEPTH, CONV_K, CONV_DIM), f32) * CONV_K ** -0.5,
        "conv_dw_b": n(ks[9], (DEPTH, CONV_DIM), f32) * 0.02,
        "conv_ln_g": 1.0 + 0.02 * n(ks[10], (DEPTH, CONV_DIM), f32),
        "conv_ln_b": n(ks[11], (DEPTH, CONV_DIM), f32) * 0.02,
        "w_conv_out": n(ks[12], (DEPTH, CONV_DIM, D), f32) * CONV_DIM ** -0.5,
        "na_rpb": n(ks[13], (DEPTH, NA_HEADS, 2 * NA_KH_MAX - 1, 2 * NA_KW - 1), f32) * 0.1,
        "w_na_out": n(ks[14], (DEPTH, NA_DIM, D), f32) * NA_DIM ** -0.5,
        "w_out": n(ks[15], (DEPTH, D, D), f32) * D ** -0.5,
        "norm2_g": 1.0 + 0.02 * n(ks[16], (DEPTH, D), f32),
        "w_up": n(ks[17], (DEPTH, D, 2 * FFN_DIM), f32) * D ** -0.5,
        "ffn_dw": n(ks[18], (DEPTH, FFN_CONV_K, 2 * FFN_DIM), f32) * FFN_CONV_K ** -0.5,
        "ffn_dw_b": n(ks[19], (DEPTH, 2 * FFN_DIM), f32) * 0.02,
        "w_down": n(ks[20], (DEPTH, FFN_DIM, D), f32) * FFN_DIM ** -0.5,
        "final_norm_g": 1.0 + 0.02 * n(ks[21], (D,), f32),
    }

def first_block(x, c, ctx, c_ctx, w_ada, b_ada, norm1_g, w_in, conv_dw, conv_dw_b, conv_ln_g,
              conv_ln_b, w_conv_out, na_rpb, w_na_out, w_out, norm2_g, w_up, ffn_dw, ffn_dw_b,
              w_down, final_norm_g):
    L = x.shape[1]
    t = jnp.arange(L)
    pos_row = (t // GRID_W).astype(jnp.float32)
    pos_col = (t % GRID_W).astype(jnp.float32)
    xc = ctx
    s_lat = jax.nn.silu(c)
    s_ctx = jax.nn.silu(c_ctx)
    for l in range(DEPTH):
        last = l == DEPTH - 1
        mod = (s_lat @ w_ada[l] + b_ada[l])[:, None, :]
        sh1, sc1, g1, sh2, sc2, g2 = jnp.split(mod, 6, axis=-1)
        mod_c = s_ctx @ w_ada[l] + b_ada[l]
        csh1, csc1, cg1, csh2, csc2, cg2 = jnp.split(mod_c, 6, axis=-1)

        h = modulate(rmsnorm(x, norm1_g[l]), sh1, sc1)
        hc = modulate(rmsnorm(xc, norm1_g[l]), csh1, csc1)
        p = h @ w_in[l]
        if last:
            kv_c = hc @ w_in[l][:, GLU_END + NA_DIM:QKV_END]
            k_c, v_c = (split_heads(u) for u in jnp.split(kv_c, 2, axis=-1))
        else:
            pc = hc @ w_in[l]
            q_c, k_c, v_c = (split_heads(u) for u in jnp.split(pc[..., GLU_END:QKV_END], 3, axis=-1))

        q, k, v = (split_heads(u) for u in jnp.split(p[..., GLU_END:QKV_END], 3, axis=-1))
        q = rope_2d(q, pos_row, pos_col)
        k = rope_2d(k, pos_row, pos_col)
        y_conv = conv_branch(p[..., :GLU_END], conv_dw[l], conv_dw_b[l], conv_ln_g[l],
                             conv_ln_b[l], w_conv_out[l])
        y_attn = merge_heads(neighbourhood_attention(q, k, v, k_c, v_c, na_rpb[l])) @ w_na_out[l]
        x = x + g1 * gated_merge(p[..., QKV_END:], y_conv, y_attn, w_out[l])

        h2 = modulate(rmsnorm(x, norm2_g[l]), sh2, sc2)
        x = x + g2 * conv_ffn(h2, w_up[l], ffn_dw[l], ffn_dw_b[l], w_down[l])

        if not last:
            yc_conv = conv_branch(pc[..., :GLU_END], conv_dw[l], conv_dw_b[l], conv_ln_g[l],
                                  conv_ln_b[l], w_conv_out[l])
            yc_attn = merge_heads(context_attention(q_c, k_c, v_c)) @ w_na_out[l]
            xc = xc + cg1 * gated_merge(pc[..., QKV_END:], yc_conv, yc_attn, w_out[l])
            hc2 = modulate(rmsnorm(xc, norm2_g[l]), csh2, csc2)
            xc = xc + cg2 * conv_ffn(hc2, w_up[l], ffn_dw[l], ffn_dw_b[l], w_down[l])
    return rmsnorm(x, final_norm_g)


N_MIXERS = 2
SB_HEADS = 16
SB_HEAD_DIM = D_MODEL // SB_HEADS
Q_BLOCK = 128
D_RNN = (D_MODEL * 5) // 4
LRU_BLOCKS = 10
LRU_BLOCK_W = D_RNN // LRU_BLOCKS
CONV_W = 4
LRU_C = 8.0
D_FF = ((8 * D_MODEL // 3 + 127) // 128) * 128
N_SUB = 3
MACARON_W = 0.5
N_SB_LAYERS = (DEPTH + 1) // 2
N_LRU_LAYERS = DEPTH // 2


def rmsnorm_2(x, g):
    xf = x.astype(jnp.float32)
    inv = lax.rsqrt(jnp.mean(xf * xf, axis=-1, keepdims=True) + EPS)
    return (xf * inv).astype(x.dtype) * g

def sublayer_input(x, g, mod_j):
    shift, scale, gate = mod_j[:, 0], mod_j[:, 1], mod_j[:, 2]
    h = rmsnorm_2(x, g) * (1 + scale[:, None, :]) + shift[:, None, :]
    return h, (1 + gate)[:, None, :]

def swiglu(h, w_gu, w_down):
    g, u = jnp.split(h @ w_gu, 2, axis=-1)
    return (jax.nn.silu(g) * u) @ w_down

def stick_breaking_attention(h, w_qkv, w_o):
    B, S, _ = h.shape
    qkv = (h @ w_qkv).reshape(B, S, 3, SB_HEADS, SB_HEAD_DIM)
    qkv = jnp.transpose(qkv, (2, 0, 3, 1, 4)).astype(jnp.float32)
    q = qkv[0] * (SB_HEAD_DIM ** -0.5)
    k, v = qkv[1], qkv[2]
    outs = []
    for blk in range(S // Q_BLOCK):
        t0 = blk * Q_BLOCK
        L = t0 + Q_BLOCK
        z = jnp.einsum('bhqd,bhkd->bhqk', q[:, :, t0:L], k[:, :, :L])
        t_idx = t0 + jnp.arange(Q_BLOCK)
        s_idx = jnp.arange(L)
        mask = s_idx[None, :] < t_idx[:, None]
        log_keep = jnp.where(mask, jax.nn.log_sigmoid(-z), 0.0)
        later = lax.cumsum(log_keep, axis=3, reverse=True) - log_keep
        w = jnp.where(mask, jnp.exp(jax.nn.log_sigmoid(z) + later), 0.0)
        outs.append(jnp.einsum('bhqk,bhkd->bhqd', w, v[:, :, :L]))
    o = jnp.concatenate(outs, axis=2)
    o = jnp.transpose(o, (0, 2, 1, 3)).reshape(B, S, D_MODEL).astype(h.dtype)
    return o @ w_o

def _lin_rec_combine(left, right):
    a1, b1 = left
    a2, b2 = right
    return a1 * a2, a2 * b1 + b2

def rglru_block(h, w_in, conv_w, conv_b, w_r, b_r, w_i, b_i, lam, w_out):
    B, S, _ = h.shape
    gate, xb = jnp.split(h @ w_in, 2, axis=-1)
    xp = jnp.pad(xb, ((0, 0), (CONV_W - 1, 0), (0, 0)))
    xc = conv_b + xp[:, 0:S] * conv_w[0]
    for tap in range(1, CONV_W):
        xc = xc + xp[:, tap:tap + S] * conv_w[tap]
    xblk = xc.reshape(B, S, LRU_BLOCKS, LRU_BLOCK_W)
    r = jax.nn.sigmoid(jnp.einsum('bsnk,nkj->bsnj', xblk, w_r).reshape(B, S, D_RNN) + b_r)
    i = jax.nn.sigmoid(jnp.einsum('bsnk,nkj->bsnj', xblk, w_i).reshape(B, S, D_RNN) + b_i)
    log_a = -LRU_C * r.astype(jnp.float32) * jax.nn.softplus(-lam.astype(jnp.float32))
    a = jnp.exp(log_a)
    b = jnp.sqrt(-jnp.expm1(2.0 * log_a)) * (i * xc).astype(jnp.float32)
    _, hs = lax.associative_scan(_lin_rec_combine, (a, b), axis=1)
    y = jax.nn.gelu(gate) * hs.astype(h.dtype)
    return y @ w_out

def second_inputs(seed: int = 0) -> dict:
    key = jax.random.key(seed)
    ks = jax.random.split(key, 24)
    D = D_MODEL
    f32 = jnp.float32
    nrm = lambda k, shape, s: jax.random.normal(k, shape, f32) * s
    x = nrm(ks[0], (BATCH, SEQ, D), 1.0)
    c = nrm(ks[1], (BATCH, D), 1.0)
    mod_w = nrm(ks[2], (DEPTH, D, N_SUB * 3 * D), 0.2 * D ** -0.5)
    mod_b = nrm(ks[3], (DEPTH, N_SUB * 3 * D), 0.05)
    norm_g = 1.0 + nrm(ks[4], (DEPTH, N_SUB, D), 0.02)
    ffn_w_gu = nrm(ks[5], (DEPTH, 2, D, 2 * D_FF), D ** -0.5)
    ffn_w_down = nrm(ks[6], (DEPTH, 2, D_FF, D), D_FF ** -0.5)
    sb_w_qkv = nrm(ks[7], (N_SB_LAYERS, D, 3 * D), D ** -0.5)
    sb_w_o = nrm(ks[8], (N_SB_LAYERS, D, D), D ** -0.5)
    lru_w_in = nrm(ks[9], (N_LRU_LAYERS, D, 2 * D_RNN), D ** -0.5)
    lru_conv_w = nrm(ks[10], (N_LRU_LAYERS, CONV_W, D_RNN), CONV_W ** -0.5)
    lru_conv_b = nrm(ks[11], (N_LRU_LAYERS, D_RNN), 0.02)
    lru_w_r = nrm(ks[12], (N_LRU_LAYERS, LRU_BLOCKS, LRU_BLOCK_W, LRU_BLOCK_W), LRU_BLOCK_W ** -0.5)
    lru_b_r = nrm(ks[13], (N_LRU_LAYERS, D_RNN), 0.1)
    lru_w_i = nrm(ks[14], (N_LRU_LAYERS, LRU_BLOCKS, LRU_BLOCK_W, LRU_BLOCK_W), LRU_BLOCK_W ** -0.5)
    lru_b_i = nrm(ks[15], (N_LRU_LAYERS, D_RNN), 0.1)
    a_c = jax.random.uniform(ks[16], (N_LRU_LAYERS, D_RNN), f32, 0.9, 0.999)
    a0 = a_c ** (1.0 / LRU_C)
    lru_lambda = jnp.log(a0) - jnp.log1p(-a0)
    lru_w_out = nrm(ks[17], (N_LRU_LAYERS, D_RNN, D), D_RNN ** -0.5)
    final_norm_g = 1.0 + nrm(ks[18], (D,), 0.02)
    return {"x": x, "c": c, "mod_w": mod_w, "mod_b": mod_b, "norm_g": norm_g,
            "ffn_w_gu": ffn_w_gu, "ffn_w_down": ffn_w_down,
            "sb_w_qkv": sb_w_qkv, "sb_w_o": sb_w_o,
            "lru_w_in": lru_w_in, "lru_conv_w": lru_conv_w, "lru_conv_b": lru_conv_b,
            "lru_w_r": lru_w_r, "lru_b_r": lru_b_r, "lru_w_i": lru_w_i, "lru_b_i": lru_b_i,
            "lru_lambda": lru_lambda, "lru_w_out": lru_w_out, "final_norm_g": final_norm_g}

def second_block(x, c, mod_w, mod_b, norm_g, ffn_w_gu, ffn_w_down, sb_w_qkv, sb_w_o,
              lru_w_in, lru_conv_w, lru_conv_b, lru_w_r, lru_b_r, lru_w_i, lru_b_i,
              lru_lambda, lru_w_out, final_norm_g):
    B = x.shape[0]
    c_act = jax.nn.silu(c)
    for layer in range(DEPTH):
        mod = (c_act @ mod_w[layer] + mod_b[layer]).reshape(B, N_SUB, 3, D_MODEL)
        h, g = sublayer_input(x, norm_g[layer, 0], mod[:, 0])
        x = x + MACARON_W * g * swiglu(h, ffn_w_gu[layer, 0], ffn_w_down[layer, 0])
        h, g = sublayer_input(x, norm_g[layer, 1], mod[:, 1])
        j = layer // N_MIXERS
        if layer % N_MIXERS == 0:
            y = stick_breaking_attention(h, sb_w_qkv[j], sb_w_o[j])
        else:
            y = rglru_block(h, lru_w_in[j], lru_conv_w[j], lru_conv_b[j], lru_w_r[j], lru_b_r[j],
                            lru_w_i[j], lru_b_i[j], lru_lambda[j], lru_w_out[j])
        x = x + g * y
        h, g = sublayer_input(x, norm_g[layer, 2], mod[:, 2])
        x = x + MACARON_W * g * swiglu(h, ffn_w_gu[layer, 1], ffn_w_down[layer, 1])
    return rmsnorm_2(x, final_norm_g)


def setup_inputs(seed=0):
    out = dict(first_inputs(seed))
    for name, value in second_inputs(seed + 1).items():
        if name != "x":
            out[name + "_2"] = value
    return out


def reference(
    x, c, ctx, c_ctx, w_ada, b_ada, norm1_g, w_in, conv_dw, conv_dw_b, conv_ln_g, conv_ln_b,
    w_conv_out, na_rpb, w_na_out, w_out, norm2_g, w_up, ffn_dw, ffn_dw_b, w_down, final_norm_g,
    c_2, mod_w_2, mod_b_2, norm_g_2, ffn_w_gu_2, ffn_w_down_2, sb_w_qkv_2, sb_w_o_2, lru_w_in_2,
    lru_conv_w_2, lru_conv_b_2, lru_w_r_2, lru_b_r_2, lru_w_i_2, lru_b_i_2, lru_lambda_2,
    lru_w_out_2, final_norm_g_2,
):
    x = first_block(
        x, c, ctx, c_ctx, w_ada, b_ada, norm1_g, w_in, conv_dw, conv_dw_b, conv_ln_g, conv_ln_b,
        w_conv_out, na_rpb, w_na_out, w_out, norm2_g, w_up, ffn_dw, ffn_dw_b, w_down,
        final_norm_g,
    )
    return second_block(
        x, c_2, mod_w_2, mod_b_2, norm_g_2, ffn_w_gu_2, ffn_w_down_2, sb_w_qkv_2, sb_w_o_2,
        lru_w_in_2, lru_conv_w_2, lru_conv_b_2, lru_w_r_2, lru_b_r_2, lru_w_i_2, lru_b_i_2,
        lru_lambda_2, lru_w_out_2, final_norm_g_2,
    )


_drawn_inputs = setup_inputs


def setup_inputs(seed=0):
    import zlib

    import numpy as np

    out = dict(_drawn_inputs(seed))
    spreads = {}
    factors = {'norm1_g': 8.0,
     'conv_dw_b': 6.096,
     'conv_ln_g': 8.0,
     'conv_ln_b': 8.0,
     'na_rpb': 8.0,
     'norm2_g': 5.443,
     'ffn_dw_b': 4.849,
     'lru_b_r_2': 7.524,
     'lru_b_i_2': 3.331,
     'final_norm_g_2': 2.803}
    for name, (base, spread) in spreads.items():
        noise = np.random.default_rng([zlib.crc32(name.encode()), seed]).standard_normal(out[name].shape)
        drawn = base * np.exp(spread * noise) if base else spread * noise
        out[name] = jnp.asarray(drawn.astype(out[name].dtype))
    for name, factor in factors.items():
        out[name] = (out[name] * factor).astype(out[name].dtype)
    return out
```

```python
from contextlib import ExitStack
from dataclasses import dataclass

import numpy as np
import concourse.bass as bass
from concourse import mybir

P = 128
D = 1024
T = 256
DC = D // P
GRID_W = 64
CONV_C, CONV_K = 4, 31
PAD = CONV_K // 2
UW = T + 2 * PAD + 2
HD = 64
NA_H, NA_C = 8, 4
SB_H = 16
FC = 22
FA = 12
RC = 10
SLAB = 16 * P
EPS = 1e-6
N_MOD_A, N_MOD_B = 6 * D // 256, 9 * D // 256
N_MOD = 2 * N_MOD_A + 2 * N_MOD_B
N_FIRST = 8
N_DOUBLE = N_MOD_A + 8
SERIES = 10

F32 = mybir.dt.float32
F32R = mybir.dt.float32r
ALU = mybir.AluOpType
ACT = mybir.ActivationFunctionType
RADD = bass.bass_isa.ReduceOp.add
AXX = mybir.AxisListType.X


def param_columns():
    at, n = {}, 0
    sizes = [("cvec", 24)]
    for l in range(2):
        sizes += [(f"b_ada{l}", 48), (f"norm1{l}", 8), (f"norm2{l}", 8), (f"conv_w{l}", CONV_C * CONV_K),
                  (f"conv_b{l}", 4), (f"ln_g{l}", 4), (f"ln_b{l}", 4), (f"ffn_w{l}", 3 * 44), (f"ffn_b{l}", 44),
                  (f"mod_b{l}", 72), (f"norm_b{l}", 24)]
    sizes += [("final_a", 8), ("final_b", 8), ("lru_w", 40), ("lru_b", 10), ("lru_br", 10), ("lru_bi", 10),
              ("lru_lam", 10)]
    for name, k in sizes:
        at[name] = (n, k)
        n += k
    return at, n


PCOL, NPARAM = param_columns()
TCOL = {"ident": (0, 128), "ones": (128, 128), "ntri": (256, 128), "nones": (384, 128), "cos": (512, 256),
        "sin": (768, 256), "keep": (1024, 384), "drop": (1408, 384)}
NTAB = 1792


@dataclass
class Stage:
    kind: str
    src: tuple
    width: tuple
    bodies: int
    kc: int = 8
    mods: int = 0
    arg: object = None
    g0: int = 0
    m0: int = 0
    e0: int = 0
    x0: int = 0
    nxt: object = None


def build(nc, a):
    plan = []

    def stage(kind, src, width, bodies, **kw):
        src = src if isinstance(src, tuple) else (src, src)
        width = width if isinstance(width, tuple) else (width, width)
        plan.append(("slabs", Stage(kind, src, width, bodies, **kw)))

    def norm(x, kind, l, v, need, dest="h"):
        plan.append(("norm", dict(x=x, kind=kind, l=l, v=v, need=need, dest=dest)))

    def layer_a(l, x):
        dbl = l == 0 and x == "ctx"
        norm(x, "a", l, 0, l * N_MOD_A + 8)
        stage("glu", a[f"w_glu{l}"], SLAB, 2, mods=2)
        rope = x == "x"
        qk = "qr" if rope else "q"
        stage(qk, a[f"w_q{l}"], SLAB, 1, arg=dict(dst="q", rope=rope, scale=HD ** -0.5, conv=(l, 0, 2)))
        stage(qk, a[f"w_k{l}"], SLAB, 1, arg=dict(dst="k" if rope else "kc", rope=rope, scale=1.0, conv=(l, 2, 4)))
        stage("v", a[f"w_v{l}"], SLAB, 1, arg=dict(dst="v" if rope else "vc", conv=(l, 4, 6), heads=NA_H))
        plan.append(("ln", dict(l=l)))
        plan.append(("attn", dict(l=l, ctx=x == "ctx")))
        stage("gm", (a[f"w_gate{l}"], a[f"w_merge{l}"]), (SLAB, 1024), 8, mods=1)
        stage("out", a[f"w_out{l}"], SLAB, 2, mods=2,
              arg=dict(x=x, kind="a", l=l, v=2, need=l * N_MOD_A + 12))
        norm(x, "a", l, 3, l * N_MOD_A + 20)
        stage("upa", a[f"w_up{l}"], SLAB, FC // 2, arg=dict(l=l))
        for part in range(2):
            stage("down", a[f"w_down{l}{part}"], (FA, FC - FA)[part] * P, 4, kc=(FA, FC - FA)[part], mods=1,
                  arg=dict(x=x, kind="a", l=l, v=5, need=(l + 1) * N_MOD_A, part=part))

    def ffn_b(l, f, sub, mods):
        base = 2 * N_MOD_A + l * N_MOD_B + 12 * sub
        norm("x", "b", l, 3 * sub, base + 8)
        stage("upb", a[f"w_gu{l}{f}"], SLAB, FC // 2, mods=mods[0])
        for part in range(2):
            stage("down", a[f"w_dn{l}{f}{part}"], (FA, FC - FA)[part] * P, 4, kc=(FA, FC - FA)[part], mods=mods[1],
                  arg=dict(x="x", kind="b", l=l, v=3 * sub + 2, need=base + 12, part=part, half=True))

    layer_a(0, "ctx")
    layer_a(0, "x")
    norm("ctx", "a", 1, 0, N_MOD_A + 8)
    stage("q", a["w_k1"], SLAB, 1, arg=dict(dst="kc", rope=False, scale=1.0, conv=None))
    stage("v", a["w_v1"], SLAB, 1, arg=dict(dst="vc", conv=None, heads=NA_H))
    layer_a(1, "x")
    norm("x", "fa", 0, 0, 0, dest="x")
    ffn_b(0, 0, 0, (1, 1))
    norm("x", "b", 0, 3, 2 * N_MOD_A + 20)
    stage("q", a["w_sbq"], SLAB, 2, mods=1, arg=dict(dst="sbq", rope=False, scale=HD ** -0.5, conv=None))
    stage("q", a["w_sbk"], SLAB, 2, mods=1, arg=dict(dst="sbk", rope=False, scale=1.0, conv=None))
    stage("v", a["w_sbv"], SLAB, 2, mods=1, arg=dict(dst="sbv", conv=None, heads=SB_H))
    plan.append(("stick", {}))
    stage("out", a["w_sbo"], SLAB, 2, mods=2, arg=dict(x="x", kind="b", l=0, v=5, need=2 * N_MOD_A + 24))
    ffn_b(0, 1, 2, (1, 0))
    ffn_b(1, 0, 0, (0, 0))
    norm("x", "b", 1, 3, 2 * N_MOD_A + N_MOD_B + 20)
    stage("lin", a["w_lin"], SLAB, RC // 2)
    stage("lgate", a["w_lg"], 2 * P, RC // 2, kc=1)
    plan.append(("lru", {}))
    stage("down", a["w_lout"], RC * P, 4, kc=RC,
          arg=dict(x="x", kind="b", l=1, v=5, need=2 * N_MOD_A + N_MOD_B + 24, part=2))
    ffn_b(1, 1, 2, (0, 0))
    norm("x", "fb", 0, 0, 0, dest="y")

    if a.get("cut"):
        plan = plan[:a["cut"]]

    g = xn = 0
    m = N_FIRST
    of_kind, seen, before, n_h, n_bias, had_x = {}, {}, None, 0, 0, False
    for what, s in plan:
        if what == "slabs":
            s.g0, s.m0, s.e0, s.x0 = g, m, of_kind.get(s.kind, 0), xn
            n = 2 * s.bodies
            g += n
            m += s.mods * s.bodies
            of_kind[s.kind] = s.e0 + n
            if s.kind == "out":
                xn += 2 * n
            if s.kind == "down":
                xn += n
            if before is not None:
                before.nxt = s
            before = s
        else:
            s["i"] = seen.get(what, 0)
            seen[what] = s["i"] + 1
            s["x0"] = xn
            s["had"] = dict(of_kind)
            if what == "norm":
                s["ih"] = n_h
                n_h += s["dest"] == "h"
                s["first_x"] = s["x"] == "x" and not had_x
                had_x = had_x or s["x"] == "x"
            if what == "attn":
                s["n_bias"] = n_bias
                n_bias += not s["ctx"]
    n_mod = m
    assert n_mod <= N_MOD
    first = next(s for what, s in plan if what == "slabs")

    with ExitStack() as ctx:
        def sb(name, shape, dt=F32):
            return ctx.enter_context(nc.sbuf_tensor(name, shape, dt))

        def sem(name):
            return ctx.enter_context(nc.semaphore(name))

        raw = sb("raw", [P, 2, SLAB])
        w_hi = sb("w_hi", [P, 2, SLAB], F32R)
        w_lo = sb("w_lo", [P, 2, SLAB], F32R)
        res = {"x": sb("x_res", [P, DC, T]), "ctx": sb("ctx_res", [P, DC, T])}
        h_hi = sb("h_hi", [P, DC, T], F32R)
        h_lo = sb("h_lo", [P, DC, T], F32R)
        e_hi = sb("e_hi", [P, FC, T], F32R)
        e_lo = sb("e_lo", [P, FC, T], F32R)
        modraw = sb("modraw", [P, DC, 256])
        modacc = sb("modacc", [P, 2, 2, 256])
        modred = sb("modred", [P, 256])
        moddiag = sb("moddiag", [P, 2, P])
        modcol = sb("modcol", [P, 2, 2 * N_MOD])
        par = sb("par", [P, NPARAM])
        tab = sb("tab", [P, NTAB])
        cact = sb("cact", [P, 3, DC])
        cols = sb("cols", [P, 4, 8])
        small = sb("small", [P, 8, RC])
        arena = sb("arena", [P, 13312])
        bias = sb("bias", [P, 2, 2, 256])

        def view(at, *shape):
            n = int(np.prod(shape))
            v = arena[:, at:at + n]
            if len(shape) == 2:
                return v.rearrange("p (b c) -> p b c", b=shape[0])
            if len(shape) == 3:
                return v.rearrange("p (b c d) -> p b c d", b=shape[0], c=shape[1])
            return v

        dst = {"q": view(0, NA_C, T), "k": view(1024, NA_C, T), "kc": view(3072, NA_C, T),
               "v": view(2048, 2, 512), "vc": view(4096, 2, 512),
               "sbq": view(0, DC, T), "sbk": view(2048, DC, T), "sbv": view(4096, 2, D)}
        u_pad = view(5120, CONV_C, UW)
        cy = view(5120 + CONV_C * UW, CONV_C, T)
        free0 = 5120 + CONV_C * (UW + T)
        att_p = view(free0, 2, 2, 512)
        att_pt = view(free0 + 2048, 2, 4, T)
        ln_r = view(free0, 5, T)
        ln_y = view(free0 + 2048, CONV_C, T)
        scr = view(free0, 2, 2, T)
        scr2 = view(free0 + 1024, 2, 2, T)
        nsq = view(0, DC, T)
        nrm = view(2048, 4, T)
        sb_z = view(8192, 2, 3, 384)
        l_gate, l_x, l_r, l_i, l_t = (view(RC * T * k, RC, T) for k in range(5))
        assert free0 + 4096 <= 13312 and 5 * RC * T <= 13312 and 8192 + 2304 <= 13312
        mod_first = [arena[:, k * SLAB:(k + 1) * SLAB].rearrange("p (k n) -> p k n", k=DC) for k in range(6)]

        pb = [ctx.enter_context(nc.psum_tensor(f"bank_pair{k}", [P, 2, 512], F32)) for k in range(2)]
        ps_t = ctx.enter_context(nc.psum_tensor("ps_t", [P, 2, 512], F32))
        ps_o = ctx.enter_context(nc.psum_tensor("ps_o", [P, 2, 512], F32))

        def pcol(name, k=0, n=1):
            at = PCOL[name][0] + k
            return par[:, at:at + n]

        def pview(name, k):
            at, n = PCOL[name]
            return par[:, at:at + n].rearrange("p (c k) -> p c k", k=k)

        def table(name):
            at, n = TCOL[name]
            return tab[:, at:at + n]

        raw_in = [sem("raw_in0"), sem("raw_in1")]
        hi_ready, lo_ready = sem("hi_ready"), sem("lo_ready")
        slab_done = sem("slab_done")
        setup_in = [sem(f"setup_in{k}") for k in range(4)]
        first_in = [sem(f"first_in{k}") for k in range(N_FIRST)]
        mod_in, mod_chain = sem("mod_in"), sem("mod_chain")
        mod_summed, mod_done, pool_chain = sem("mod_summed"), sem("mod_done"), sem("pool_chain")
        c_ready, zeroed = sem("c_ready"), sem("zeroed")
        dve_chain, act_chain = sem("dve_chain"), sem("act_chain")
        updated = sem("updated")
        sq_ready, sum_ready, ms_ready, std_ready = (sem(k) for k in ("sq_ready", "sum_ready", "ms_ready", "std_ready"))
        norm_ready, hn_hi, hn_lo = sem("norm_ready"), sem("hn_hi"), sem("hn_lo")
        glu_sig, glu_mul = sem("glu_sig"), sem("glu_mul")
        q_copied, r_copied, q_roped, v_copied = (sem(k) for k in ("q_copied", "r_copied", "q_roped", "v_copied"))
        conv_tap = sem("conv_tap")
        ln_sum, ln_centred, ln_sq, ln_var, ln_ms, ln_std = (sem(f"ln_{k}") for k in
                                                            ("sum", "centred", "sq", "var", "ms", "std"))
        ln_scaled, ln_hi, ln_lo = sem("ln_scaled"), sem("ln_hi"), sem("ln_lo")
        bias_in = [sem("bias_in0"), sem("bias_in1")]
        att_s, att_max, att_exp, att_prob = sem("att_s"), sem("att_max"), sem("att_exp"), sem("att_prob")
        att_t, att_tc, att_o, att_hi, att_lo = (sem(f"att_{k}") for k in ("t", "tc", "o", "hi", "lo"))
        gm_sig, gm_mul, gm_sum, gm_hi, gm_lo = (sem(f"gm_{k}") for k in ("sig", "mul", "sum", "hi", "lo"))
        up_lin, up_tap, up_silu, up_mul, up_hi, up_lo = (sem(f"up_{k}") for k in
                                                         ("lin", "tap", "silu", "mul", "hi", "lo"))
        upb_silu, upb_mul, upb_hi, upb_lo = (sem(f"upb_{k}") for k in ("silu", "mul", "hi", "lo"))
        st_z, st_ln, st_sp, st_r, st_v, st_w, st_o, st_hi, st_lo = (
            sem(f"st_{k}") for k in ("z", "ln", "sp", "r", "v", "w", "o", "hi", "lo"))
        lin_lin, lin_tap, lin_hi, lin_lo = (sem(f"lin_{k}") for k in ("lin", "tap", "hi", "lo"))
        lru_gates, lru_sq, lru_root, lru_y, lru_hi, lru_lo = (sem(f"lru_{k}") for k in
                                                              ("gates", "sq", "root", "y", "hi", "lo"))
        stored = sem("stored")

        block = ctx.enter_context(nc.Block())

        def sweep(eng, s, body):
            n = s.bodies
            if n <= 3 or s.kind == "lgate":
                for b in range(n):
                    body(b, b == 0, b == n - 1)
            else:
                body(0, True, False)
                with eng.Fori(1, n - 1) as b:
                    body(b, False, False)
                body(n - 1, False, True)

        def following(s, b, p, last):
            if p == 0:
                return s, b, 1
            if last:
                return (s.nxt, 0, 0) if s.nxt is not None else None
            return s, b + 1, 0

        def wait_up(eng, s, value):
            if not isinstance(value, int) or value > 0:
                eng.wait_ge(s, value)

        @block.sync
        def _(sp):
            sp.dma_start(par[:], a["params"]).then_inc(setup_in[0], 16)
            for k in range(6):
                sp.dma_start(mod_first[k], a["w_mod"][k].rearrange("p (k n) -> p k n", k=DC)).then_inc(first_in[k], 16)
                if k == 0:
                    sp.dma_start(tab[:], a["tables"]).then_inc(setup_in[1], 16)
                if k == 3:
                    sp.dma_start(res["ctx"][:], a["ctx"]).then_inc(setup_in[2], 16)

            def load(s, b, p):
                g = s.g0 + 2 * b + p
                wait_up(sp, lo_ready, g - 1)
                j = b if s.kind == "gm" else 2 * b + p
                sp.dma_start(raw[:, p, 0:s.width[p]], s.src[p][j]).then_inc(raw_in[p], 16)

            load(first, 0, 0)
            load(first, 0, 1)
            for k in (6, 7):
                sp.wait_ge(mod_summed, k - 5)
                sp.dma_start(mod_first[k - 6], a["w_mod"][k].rearrange("p (k n) -> p k n", k=DC))\
                  .then_inc(first_in[k], 16)
            sp.dma_start(res["x"][:], a["x"]).then_inc(setup_in[3], 16)
            for what, s in plan:
                if what != "slabs":
                    continue

                def body(b, is_first, last, s=s):
                    for p in range(2):
                        if not (s is first and is_first):
                            load(s, b, p)
                sweep(sp, s, body)
            out_norms = [s for what, s in plan if what == "norm" and s["dest"] == "y"]
            if out_norms:
                sp.wait_ge(norm_ready, 2 * (out_norms[0]["i"] + 1))
                sp.dma_start(a["y"], nsq).then_inc(stored, 16)
            else:
                sp.wait_ge(updated, xn)
                sp.dma_start(a["y"], res[a["cut_out"]][:]).then_inc(stored, 16)
            sp.wait_ge(stored, 16)

        @block.gpsimd
        def _(pool):
            ident2 = table("ident").unsqueeze(1).broadcast_to([P, 2, P])
            
            def load_mod(m):
                nc.gpsimd.dma_start(modraw[:], a["w_mod"][m].rearrange("p (k n) -> p k n", k=DC)).then_inc(mod_in, 16)

            def reduce_to_columns(m, passes, slot, c0, more=True):
                pool.wait_ge(mod_summed, m + 1)
                if more:
                    load_mod(m + 1)
                for v in range(passes):
                    k = c0 + 9 * v
                    nc.gpsimd.partition_all_reduce(modred[:], modacc[:, slot, v, :], P, RADD).then_inc(pool_chain, 1)
                    pool.wait_ge(pool_chain, k + 1)
                    nc.gpsimd.tensor_tensor(moddiag[:], modred[:].rearrange("p (c n) -> p c n", c=2), ident2,
                                            ALU.mult).then_inc(pool_chain, 1)
                    pool.wait_ge(pool_chain, k + 2)
                    for n in range(7):
                        w = P >> (n + 1)
                        nc.gpsimd.tensor_tensor(moddiag[:, :, 0:w], moddiag[:, :, 0:w], moddiag[:, :, w:2 * w], ALU.add)\
                          .then_inc(pool_chain, 1)
                        pool.wait_ge(pool_chain, k + 3 + n)
                    ins = nc.gpsimd.tensor_copy(modcol[:, v, bass.ds(2 * m, 2)], moddiag[:, :, 0])
                ins.then_inc(mod_done, 1)

            pool.wait_ge(setup_in[1], 16)
            for m in range(N_FIRST):
                reduce_to_columns(m, 2, m % 2, 18 * m, more=False)
            load_mod(N_FIRST)
            top = min(N_DOUBLE, n_mod - 1)
            with pool.Fori(N_FIRST, top) as m:
                reduce_to_columns(m, 2, 0, 18 * m)
            if n_mod > N_DOUBLE:
                with pool.Fori(N_DOUBLE, n_mod - 1) as m:
                    reduce_to_columns(m, 1, 0, 18 * N_DOUBLE + 9 * (m - N_DOUBLE))
                reduce_to_columns(n_mod - 1, 1, 0, 18 * N_DOUBLE + 9 * (n_mod - 1 - N_DOUBLE), more=False)
            else:
                reduce_to_columns(n_mod - 1, 2, 0, 18 * (n_mod - 1), more=False)

        @block.scalar
        def _(act):
            chain = [0]

            def link(ins):
                chain[0] += 1
                ins.then_inc(act_chain, 1)
                act.wait_ge(act_chain, chain[0])

            def split_hi(nx):
                if nx is None:
                    return
                s, b, p = nx
                g = s.g0 + 2 * b + p
                act.wait_ge(raw_in[p], 16 * (s.g0 // 2) + 16 + 16 * b)
                wait_up(act, slab_done, g - 1)
                w = s.width[p]
                nc.scalar.activation(w_hi[:, p, 0:w], raw[:, p, 0:w], ACT.Copy).then_inc(hi_ready, 1)

            act.wait_ge(setup_in[0], 16)
            at = PCOL["cvec"][0]
            nc.scalar.activation(cact[:].rearrange("p a b -> p (a b)"), par[:, at:at + 24], ACT.Silu)\
                .then_inc(c_ready, 1)
            lam = pcol("lru_lam", 0, RC)
            link(nc.scalar.activation(small[:, 0, :], lam, ACT.Abs))
            nc.scalar.activation(small[:, 1, :], small[:, 0, :], ACT.Exp, scale=-1.0).then_inc(c_ready, 1)
            split_hi((first, 0, 0))

            def do_norm(n):
                i, x = n["i"], res[n["x"]]
                if i == 0:
                    act.wait_ge(setup_in[2], 16)
                    act.wait_ge(mod_summed, N_FIRST)
                if n["first_x"]:
                    act.wait_ge(setup_in[3], 16)
                wait_up(act, updated, n["x0"])
                wait_up(act, norm_ready, 2 * i)
                for k in range(4):
                    nc.scalar.activation(nsq[:, 2 * k:2 * k + 2, :], x[:, 2 * k:2 * k + 2, :], ACT.Square)\
                        .then_inc(sq_ready, 1)
                act.wait_ge(ms_ready, i + 1)
                nc.scalar.activation(nrm[:, 1, :], nrm[:, 0, :], ACT.Sqrt).then_inc(std_ready, 1)
                if n["dest"] == "h":
                    for f in range(2):
                        act.wait_ge(norm_ready, 2 * i + f + 1)
                        nc.scalar.activation(h_hi[:, 4 * f:4 * f + 4, :], nsq[:, 4 * f:4 * f + 4, :], ACT.Copy)\
                            .then_inc(hn_hi, 1)

            def do_glu(s):
                def body(b, is_first, last):
                    for p in range(2):
                        g, e = s.g0 + 2 * b + p, s.e0 + 2 * b + p
                        split_hi(following(s, b, p, last))
                        act.wait_ge(slab_done, g + 1)
                        wait_up(act, glu_mul, e - 1)
                        nc.scalar.activation(scr[:, p, 0, :], pb[p][:, 1, 0:T], ACT.Sigmoid).then_inc(glu_sig, 1)
                sweep(act, s, body)

            def do_q(s):
                r = s.arg
                def body(b, is_first, last):
                    for p in range(2):
                        g, e = s.g0 + 2 * b + p, s.e0 + 2 * b + p
                        j = 2 * (2 * b + p)
                        split_hi(following(s, b, p, last))
                        act.wait_ge(slab_done, g + 1)
                        if r["rope"]:
                            wait_up(act, q_roped, e - 1)
                            o = scr[:, p, :, :]
                        else:
                            o = dst[r["dst"]][:, j:j + 2, :]
                        nc.scalar.activation(o, pb[p][:, :, 0:T], ACT.Copy, scale=r["scale"])\
                            .then_inc(r_copied if r["rope"] else q_copied, 1)
                sweep(act, s, body)

            def do_v(s):
                def body(b, is_first, last):
                    for p in range(2):
                        g = s.g0 + 2 * b + p
                        j = 256 * (2 * b + p)
                        split_hi(following(s, b, p, last))
                        act.wait_ge(slab_done, g + 1)
                        nc.scalar.activation(dst[s.arg["dst"]][:, :, j:j + 256], pb[p][:, :, 0:T], ACT.Copy)\
                            .then_inc(v_copied, 1)
                sweep(act, s, body)

            def do_ln(n):
                i, l = n["i"], n["l"]
                for k in range(2):
                    act.wait_ge(ln_centred, 2 * i + k + 1)
                    nc.scalar.activation(ln_y[:, 2 * k:2 * k + 2, :], cy[:, 2 * k:2 * k + 2, :], ACT.Square)\
                        .then_inc(ln_sq, 1)
                act.wait_ge(ln_ms, i + 1)
                nc.scalar.activation(ln_r[:, 1, :], ln_r[:, 0, :], ACT.Sqrt).then_inc(ln_std, 1)
                for k in range(CONV_C):
                    act.wait_ge(ln_scaled, CONV_C * i + k + 1)
                    link(nc.scalar.activation(ln_y[:, k, :], cy[:, k, :], ACT.Silu, bias=pcol(f"ln_b{l}", k),
                                              scale=pcol(f"ln_g{l}", k)))
                nc.scalar.activation(e_hi[:, 0:CONV_C, :], ln_y, ACT.Copy).then_inc(ln_hi, 1)

            def load_bias(l, hd):
                nc.scalar.dma_start(bias[:, hd % 2, :, :], a["rel_bias"][l, hd]).then_inc(bias_in[hd % 2], 16)

            def do_attn(n):
                a0, keys = NA_H * n["i"], 256 if n["ctx"] else 512
                if not n["ctx"]:
                    wait_up(act, att_max, a0)
                    load_bias(n["l"], 0)
                    load_bias(n["l"], 1)
                for h in range(NA_H + 2):
                    if h < NA_H:
                        act.wait_ge(att_max, a0 + h + 1)
                        if not n["ctx"] and h + 2 < NA_H:
                            load_bias(n["l"], h + 2)
                        for t in range(2):
                            ins = nc.scalar.activation(att_p[:, h % 2, t, 0:keys], att_p[:, h % 2, t, 0:keys], ACT.Exp,
                                                       bias=small[:, 4 + h % 2, t:t + 1],
                                                       accum_out=small[:, 6 + h % 2, t:t + 1])
                        ins.then_inc(att_exp, 1)
                    if 1 <= h <= NA_H:
                        k = h - 1
                        act.wait_ge(att_t, a0 + k + 1)
                        wait_up(act, att_o, a0 + k - 1)
                        nk = keys // P
                        nc.scalar.activation(
                            att_pt[:, k % 2, 0:nk, :].rearrange("p k (t q) -> p t k q", t=2),
                            ps_t[:, :, 0:keys].rearrange("p t (k q) -> p t k q", q=P), ACT.Copy).then_inc(att_tc, 1)
                    if h >= 2:
                        k = h - 2
                        r = HD * (k % 2)
                        act.wait_ge(att_o, a0 + k + 1)
                        nc.scalar.activation(e_hi[r:r + HD, CONV_C + k // 2, :], ps_o[r:r + HD, k % 2, 0:T],
                                             ACT.Copy).then_inc(att_hi, 1)

            def do_gm(s):
                b0 = s.e0 // 2
                def body(b, is_first, last):
                    g = s.g0 + 2 * b
                    split_hi(following(s, b, 0, last))
                    act.wait_ge(slab_done, g + 1)
                    wait_up(act, gm_mul, b0 + b)
                    nc.scalar.activation(scr[:, 0, :, :], pb[0][:, :, 0:T], ACT.Sigmoid).then_inc(gm_sig, 1)
                    split_hi(following(s, b, 1, last))
                    act.wait_ge(gm_sum, b0 + b + 1)
                    nc.scalar.activation(e_hi[:, 8 + b, :], scr2[:, 0, 0, :], ACT.Copy).then_inc(gm_hi, 1)
                sweep(act, s, body)

            def do_splits_only(s):
                def body(b, is_first, last):
                    for p in range(2):
                        split_hi(following(s, b, p, last))
                sweep(act, s, body)

            def do_upa(s):
                l = s.arg["l"]
                taps, fb = pview(f"ffn_w{l}", 3), pview(f"ffn_b{l}", 1)

                def step(b, p, last, has_tail):
                    j = 2 * b + p
                    g, e = s.g0 + j, s.e0 + j
                    split_hi(following(s, b, p, last))
                    if has_tail:
                        act.wait_ge(up_tap, 4 * e)
                        nc.scalar.activation(scr[:, 1 - p, 1, :], scr[:, 1 - p, 1, :], ACT.Silu).then_inc(up_silu, 1)
                    act.wait_ge(slab_done, g + 1)
                    wait_up(act, up_lo, e - 1)
                    nc.scalar.activation(scr[:, p, 0, :], pb[p][:, 0, 0:T], ACT.Identity,
                                         bias=fb[:, j, :], scale=taps[:, j, 1:2])
                    nc.scalar.activation(scr[:, p, 1, :], pb[p][:, 1, 0:T], ACT.Identity,
                                         bias=fb[:, FC + j, :], scale=taps[:, FC + j, 1:2]).then_inc(up_lin, 1)
                    if has_tail:
                        act.wait_ge(up_mul, e)
                        nc.scalar.activation(e_hi[:, j - 1, :], scr[:, 1 - p, 0, :], ACT.Copy).then_inc(up_hi, 1)

                def body(b, is_first, last):
                    step(b, 0, last, not is_first)
                    step(b, 1, last, True)
                sweep(act, s, body)
                e = s.e0 + FC
                act.wait_ge(up_tap, 4 * e)
                nc.scalar.activation(scr[:, 1, 1, :], scr[:, 1, 1, :], ACT.Silu).then_inc(up_silu, 1)
                act.wait_ge(up_mul, e)
                nc.scalar.activation(e_hi[:, FC - 1, :], scr[:, 1, 0, :], ACT.Copy).then_inc(up_hi, 1)

            def do_upb(s):
                def step(b, p, last, has_tail):
                    j = 2 * b + p
                    g, e = s.g0 + j, s.e0 + j
                    split_hi(following(s, b, p, last))
                    if has_tail:
                        act.wait_ge(upb_mul, e)
                        nc.scalar.activation(e_hi[:, j - 1, :], scr[:, 1 - p, 1, :], ACT.Copy).then_inc(upb_hi, 1)
                    act.wait_ge(slab_done, g + 1)
                    nc.scalar.activation(scr[:, p, 0, :], pb[p][:, 0, 0:T], ACT.Silu).then_inc(upb_silu, 1)

                def body(b, is_first, last):
                    step(b, 0, last, not is_first)
                    step(b, 1, last, True)
                sweep(act, s, body)
                act.wait_ge(upb_mul, s.e0 + FC)
                nc.scalar.activation(e_hi[:, FC - 1, :], scr[:, 1, 1, :], ACT.Copy).then_inc(upb_hi, 1)

            def do_stick(n):
                act.preload_act_table_set("natural_log_exp_and_others")
                for h in range(SB_H + 2):
                    if h < SB_H:
                        act.wait_ge(st_z, h + 1)
                        z, w = pb[0][:, h % 2, 0:384], sb_z[:, h % 2, 0, :]
                        wait_up(act, st_sp, 3 * (h - 1))
                        if h >= 2:
                            act.wait_ge(st_r, h - 1)
                        link(nc.scalar.activation(w, z, ACT.Abs))
                        link(nc.scalar.activation(w, w, ACT.Exp, scale=-1.0))
                        nc.scalar.activation(w, w, ACT.Ln, bias=1.0).then_inc(st_ln, 1)
                    if 1 <= h <= SB_H:
                        k = h - 1
                        act.wait_ge(st_v, k + 1)
                        nc.scalar.activation(sb_z[:, k % 2, 2, :], sb_z[:, k % 2, 1, :], ACT.Exp).then_inc(st_w, 1)
                    if h >= 2:
                        k = h - 2
                        r = HD * (k % 2)
                        act.wait_ge(st_o, k + 1)
                        nc.scalar.activation(e_hi[r:r + HD, k // 2, :], ps_o[r:r + HD, k % 2, 0:T],
                                             ACT.Copy).then_inc(st_hi, 1)

            def do_lin(s):
                w = pview("lru_w", 4)

                def step(b, p, last, has_tail):
                    j = 2 * b + p
                    g, e = s.g0 + j, s.e0 + j
                    split_hi(following(s, b, p, last))
                    act.wait_ge(slab_done, g + 1)
                    nc.scalar.activation(l_gate[:, j, :], pb[p][:, 0, 0:T], ACT.Gelu_apprx_tanh)
                    nc.scalar.activation(l_x[:, j, :], pb[p][:, 1, 0:T], ACT.Identity,
                                         bias=pview("lru_b", 1)[:, j, :], scale=w[:, j, 3:4]).then_inc(lin_lin, 1)
                    if has_tail:
                        act.wait_ge(lin_tap, 3 * e)
                        nc.scalar.activation(e_hi[:, j - 1, :], l_x[:, j - 1, :], ACT.Copy).then_inc(lin_hi, 1)

                def body(b, is_first, last):
                    step(b, 0, last, not is_first)
                    step(b, 1, last, True)
                sweep(act, s, body)
                act.wait_ge(lin_tap, 3 * RC)
                nc.scalar.activation(e_hi[:, RC - 1, :], l_x[:, RC - 1, :], ACT.Copy).then_inc(lin_hi, 1)

            def do_lgate(s):
                def body(b, is_first, last):
                    for p in range(2):
                        j = 2 * b + p
                        split_hi(following(s, b, p, last))
                        act.wait_ge(slab_done, s.g0 + j + 1)
                        nc.scalar.activation(l_r[:, j, :], pb[p][:, 0, 0:T], ACT.Sigmoid, bias=pcol("lru_br", j))
                        nc.scalar.activation(l_i[:, j, :], pb[p][:, 1, 0:T], ACT.Sigmoid, bias=pcol("lru_bi", j))\
                            .then_inc(lru_gates, 1)
                sweep(act, s, body)

            def do_lru(n):
                act.wait_ge(lru_gates, RC)
                for j in range(RC):
                    nc.scalar.activation(l_t[:, j, :], l_r[:, j, :], ACT.Tanh, scale=small[:, 2, j:j + 1])
                    ins = nc.scalar.activation(l_r[:, j, :], l_r[:, j, :], ACT.Exp, scale=small[:, 3, j:j + 1])
                ins.then_inc(lru_sq, 1)
                act.wait_ge(lru_y, 1)
                nc.scalar.activation(l_t, l_t, ACT.Sqrt).then_inc(lru_root, 1)
                act.wait_ge(lru_y, 2)
                nc.scalar.activation(e_hi[:, 0:RC, :], l_gate, ACT.Copy).then_inc(lru_hi, 1)

            kinds = {"glu": do_glu, "q": do_q, "qr": do_q, "v": do_v, "gm": do_gm, "out": do_splits_only, "down": do_splits_only,
                     "upa": do_upa, "upb": do_upb, "lin": do_lin, "lgate": do_lgate}
            others = {"norm": do_norm, "ln": do_ln, "attn": do_attn, "stick": do_stick, "lru": do_lru}
            for what, s in plan:
                kinds[s.kind](s) if what == "slabs" else others[what](s)

        @block.vector
        def _(dve):
            chain = [0]

            def link(ins):
                chain[0] += 1
                ins.then_inc(dve_chain, 1)
                dve.wait_ge(dve_chain, chain[0])

            def split_lo(nx):
                if nx is None:
                    return
                s, b, p = nx
                g, w = s.g0 + 2 * b + p, s.width[p]
                dve.wait_ge(hi_ready, g + 1)
                nc.vector.tensor_tensor(w_lo[:, p, 0:w], raw[:, p, 0:w], w_hi[:, p, 0:w].bitcast(F32),
                                        ALU.subtract).then_inc(lo_ready, 1)

            def mod_step(m, tile, passes, slot, c0, vec, arrived, reduced):
                dve.wait_ge(*arrived)
                wait_up(dve, mod_done, reduced)
                for k in range(DC):
                    for v in range(passes):
                        n = passes * k + v
                        o, c = modacc[:, slot, v, :], cact[:, vec[v], k:k + 1]
                        if k == 0:
                            ins = nc.vector.tensor_scalar(o, tile[:, k, :], c, None, ALU.mult)
                        else:
                            dve.wait_ge(mod_chain, c0 + n - passes + 1)
                            ins = nc.vector.scalar_tensor_tensor(out=o, in0=tile[:, k, :], scalar=c, in1=o,
                                                                 op0=ALU.mult, op1=ALU.add)
                        ins.then_inc(mod_summed if n == DC * passes - 1 else mod_chain, 1)

            def mods(s, b):
                for q in range(s.mods):
                    m = s.m0 + s.mods * b + q
                    k0 = s.m0 + q
                    double = k0 < N_DOUBLE
                    c0 = 15 * m if double else 15 * N_DOUBLE + 7 * (m - N_DOUBLE)
                    vec = (0, 1) if double else ((0,) if k0 < 2 * N_MOD_A else (2,))
                    mod_step(m, modraw, 2 if double else 1, 0, c0, vec, (mod_in, 16 * (m - N_FIRST + 1)), m)

            def pad_edges():
                link(nc.vector.memset(u_pad[:, :, 0:PAD], 0.0))
                link(nc.vector.memset(u_pad[:, :, PAD + T:UW], 0.0))

            dve.wait_ge(c_ready, 1)
            for m in range(N_FIRST):
                mod_step(m, mod_first[m % 6], 2, m % 2, 15 * m, (0, 1), (first_in[m], 16), m - 1)
            dve.wait_ge(c_ready, 2)
            e_, u_, v_, p_ = small[:, 1, :], small[:, 2, :], small[:, 3, :], small[:, 0, :]
            link(nc.vector.tensor_scalar(v_, e_, 2.0, None, ALU.add))
            link(nc.vector.reciprocal(u_, v_))
            link(nc.vector.tensor_tensor(u_, u_, e_, ALU.mult))
            link(nc.vector.tensor_tensor(v_, u_, u_, ALU.mult))
            link(nc.vector.memset(p_, 1.0 / (2 * SERIES + 1)))
            for k in range(SERIES - 1, -1, -1):
                link(nc.vector.tensor_tensor(p_, p_, v_, ALU.mult))
                link(nc.vector.tensor_scalar(p_, p_, 1.0 / (2 * k + 1), None, ALU.add))
            link(nc.vector.scalar_tensor_tensor(out=p_, in0=p_, scalar=2.0, in1=u_, op0=ALU.mult, op1=ALU.mult))
            link(nc.vector.tensor_scalar(u_, pcol("lru_lam", 0, RC), -1.0, 0.0, ALU.mult, ALU.max))
            link(nc.vector.tensor_tensor(p_, p_, u_, ALU.add))
            link(nc.vector.tensor_scalar(small[:, 2, :], p_, 8.0, None, ALU.mult))
            link(nc.vector.tensor_scalar(small[:, 3, :], p_, -8.0, None, ALU.mult))
            split_lo((first, 0, 0))

            def mod_vector(r, v, out, plus):
                if r["kind"] == "a":
                    base, bcol, w = 48 * r["l"], pcol(f"b_ada{r['l']}", 8 * v, 8), 1 if r["x"] == "ctx" else 0
                else:
                    base, bcol, w = 96 + 72 * r["l"], pcol(f"mod_b{r['l']}", 8 * v, 8), 0
                dve.wait_ge(mod_done, r["need"])
                src = modcol[:, w, base + 8 * v:base + 8 * v + 8]
                link(nc.vector.scalar_tensor_tensor(out=cols[:, out, :], in0=src, scalar=plus, in1=bcol,
                                                    op0=ALU.add, op1=ALU.add))

            def newton_rsqrt(ms, std, t, r):
                link(nc.vector.reciprocal(r, std))
                link(nc.vector.tensor_tensor(t, ms, r, ALU.mult))
                link(nc.vector.tensor_tensor(t, t, r, ALU.mult))
                link(nc.vector.tensor_scalar(t, t, -0.5, 1.5, ALU.mult, ALU.add))
                link(nc.vector.tensor_tensor(r, r, t, ALU.mult))

            def do_norm(n):
                i, x, kind, l, v = n["i"], res[n["x"]], n["kind"], n["l"], n["v"]
                if kind in ("a", "b"):
                    mod_vector(n, v, 1, 0.0)
                    mod_vector(n, v + 1, 0, 1.0)
                    gain = {("a", 0): pcol(f"norm1{l}", 0, 8), ("a", 3): pcol(f"norm2{l}", 0, 8)}[(kind, v)] \
                        if kind == "a" else pcol(f"norm_b{l}", 8 * (v // 3), 8)
                    link(nc.vector.tensor_tensor(cols[:, 0, :], cols[:, 0, :], gain, ALU.mult))
                dve.wait_ge(sum_ready, i + 1)
                wait_up(dve, updated, n["x0"])
                wait_up(dve, norm_ready, 2 * i)
                nc.vector.tensor_scalar(nrm[:, 0, :], ps_t[:, 0, 0:T], 1.0 / D, EPS, ALU.mult, ALU.add)\
                    .then_inc(ms_ready, 1)
                dve.wait_ge(std_ready, i + 1)
                newton_rsqrt(nrm[:, 0, :], nrm[:, 1, :], nrm[:, 2, :], nrm[:, 3, :])
                r4 = nrm[:, 3, :].unsqueeze(1).broadcast_to([P, 4, T])
                for f in range(2):
                    link(nc.vector.tensor_tensor(nsq[:, 4 * f:4 * f + 4, :], x[:, 4 * f:4 * f + 4, :], r4, ALU.mult))
                    for k in range(4 * f, 4 * f + 4):
                        o = x[:, k, :] if n["dest"] == "x" else nsq[:, k, :]
                        if kind in ("a", "b"):
                            ins = nc.vector.tensor_scalar(o, nsq[:, k, :], cols[:, 0, k:k + 1], cols[:, 1, k:k + 1],
                                                          ALU.mult, ALU.add)
                        else:
                            ins = nc.vector.tensor_scalar(o, nsq[:, k, :], pcol(f"final_{kind[1]}", k), None, ALU.mult)
                    ins.then_inc(norm_ready, 1)
                if n["dest"] == "h":
                    for f in range(2):
                        dve.wait_ge(hn_hi, 2 * n["ih"] + f + 1)
                        nc.vector.tensor_tensor(h_lo[:, 4 * f:4 * f + 4, :], nsq[:, 4 * f:4 * f + 4, :],
                                                h_hi[:, 4 * f:4 * f + 4, :].bitcast(F32), ALU.subtract)\
                            .then_inc(hn_lo, 1)

            def do_glu(s):
                pad_edges()
                def body(b, is_first, last):
                    for p in range(2):
                        j = 2 * b + p
                        split_lo(following(s, b, p, last))
                        dve.wait_ge(glu_sig, s.e0 + j + 1)
                        nc.vector.tensor_tensor(u_pad[:, j, PAD:PAD + T], pb[p][:, 0, 0:T], scr[:, p, 0, :], ALU.mult)\
                            .then_inc(glu_mul, 1)
                    mods(s, b)
                sweep(dve, s, body)

            conv_n = CONV_C * CONV_K

            def conv_piece(piece, i):
                l, k0, _ = piece
                n0, n1 = conv_n * k0 // 6, conv_n * (k0 + 1) // 6
                w = pview(f"conv_w{l}", CONV_K)
                base = conv_n * i
                if k0 == 0:
                    dve.wait_ge(glu_mul, 4 * (i + 1))
                for n in range(n0, n1):
                    t, j = n // CONV_C, n % CONV_C
                    o, u = cy[:, j, :], u_pad[:, j, t:t + T]
                    if t == 0:
                        ins = nc.vector.tensor_scalar(o, u, w[:, j, 0:1], pcol(f"conv_b{l}", j), ALU.mult, ALU.add)
                    else:
                        dve.wait_ge(conv_tap, base + n - CONV_C + 1)
                        ins = nc.vector.scalar_tensor_tensor(out=o, in0=u, scalar=w[:, j, t:t + 1], in1=o,
                                                             op0=ALU.mult, op1=ALU.add)
                    ins.then_inc(conv_tap, 1)

            conv_i = [0]

            def do_q(s):
                r = s.arg
                def body(b, is_first, last):
                    for p in range(2):
                        j = 2 * (2 * b + p)
                        split_lo(following(s, b, p, last))
                        if r["rope"]:
                            dve.wait_ge(r_copied, s.e0 + 2 * b + p + 1)
                            q_in, q_sw, o = scr[:, p, :, :], scr2[:, p, :, :], dst[r["dst"]][:, j:j + 2, :]
                            both = lambda name: table(name).unsqueeze(1).broadcast_to([P, 2, T])
                            link(nc.vector.stream_shuffle(q_sw, q_in, [(k + 16) % 32 for k in range(32)]))
                            link(nc.vector.tensor_tensor(o, q_in, both("cos"), ALU.mult))
                            link(nc.vector.tensor_tensor(q_sw, q_sw, both("sin"), ALU.mult))
                            nc.vector.tensor_tensor(o, o, q_sw, ALU.add).then_inc(q_roped, 1)
                        if r["conv"]:
                            conv_piece((r["conv"][0], r["conv"][1] + p, 0), conv_i[0])
                    mods(s, b)
                sweep(dve, s, body)

            def do_v(s):
                def body(b, is_first, last):
                    for p in range(2):
                        split_lo(following(s, b, p, last))
                        if s.arg["conv"]:
                            conv_piece((s.arg["conv"][0], s.arg["conv"][1] + p, 0), conv_i[0])
                    mods(s, b)
                sweep(dve, s, body)
                if s.arg["conv"]:
                    conv_i[0] += 1

            def do_ln(n):
                i = n["i"]
                width = CONV_C * P
                dve.wait_ge(ln_sum, i + 1)
                dve.wait_ge(conv_tap, conv_n * (i + 1))
                link(nc.vector.tensor_scalar(ln_r[:, 4, :], ps_t[:, 0, 0:T], 1.0 / width, None, ALU.mult))
                mean = ln_r[:, 4, :].unsqueeze(1).broadcast_to([P, 2, T])
                for k in range(2):
                    nc.vector.tensor_tensor(cy[:, 2 * k:2 * k + 2, :], cy[:, 2 * k:2 * k + 2, :], mean, ALU.subtract)\
                        .then_inc(ln_centred, 1)
                dve.wait_ge(ln_var, i + 1)
                nc.vector.tensor_scalar(ln_r[:, 0, :], ps_t[:, 1, 0:T], 1.0 / width, EPS, ALU.mult, ALU.add)\
                    .then_inc(ln_ms, 1)
                dve.wait_ge(ln_std, i + 1)
                dve.wait_ge(ln_centred, 2 * (i + 1))
                newton_rsqrt(ln_r[:, 0, :], ln_r[:, 1, :], ln_r[:, 2, :], ln_r[:, 3, :])
                for k in range(CONV_C):
                    nc.vector.tensor_tensor(cy[:, k, :], cy[:, k, :], ln_r[:, 3, :], ALU.mult).then_inc(ln_scaled, 1)
                dve.wait_ge(ln_hi, i + 1)
                nc.vector.tensor_tensor(e_lo[:, 0:CONV_C, :], ln_y, e_hi[:, 0:CONV_C, :].bitcast(F32), ALU.subtract)\
                    .then_inc(ln_lo, 1)

            def do_attn(n):
                a0, is_ctx = NA_H * n["i"], n["ctx"]
                keys = 256 if is_ctx else 512
                for h in range(NA_H + 2):
                    if h < NA_H:
                        dve.wait_ge(att_s, a0 + h + 1)
                        wait_up(dve, att_t, a0 + h - 1)
                        s_ = pb[h % 2]
                        if is_ctx:
                            link(nc.vector.tensor_copy(att_p[:, h % 2, :, 0:256], s_[:, :, 0:256]))
                        else:
                            dve.wait_ge(bias_in[h % 2], 16 * (NA_H // 2 * n["n_bias"] + h // 2 + 1))
                            nc.vector.tensor_tensor(att_p[:, h % 2, :, 0:256], s_[:, :, 0:256], bias[:, h % 2, :, :],
                                                    ALU.add)
                            link(nc.vector.tensor_copy(att_p[:, h % 2, :, 256:512], s_[:, :, 256:512]))
                        link(nc.vector.tensor_reduce(small[:, 4 + h % 2, 2:4], att_p[:, h % 2, :, 0:keys], AXX, ALU.max))
                        nc.vector.tensor_scalar(small[:, 4 + h % 2, 0:2], small[:, 4 + h % 2, 2:4], -1.0, None,
                                                ALU.mult).then_inc(att_max, 1)
                    if 1 <= h <= NA_H:
                        k = h - 1
                        dve.wait_ge(att_exp, a0 + k + 1)
                        link(nc.vector.reciprocal(small[:, 6 + k % 2, 2:4], small[:, 6 + k % 2, 0:2]))
                        for t in range(2):
                            ins = nc.vector.tensor_scalar(att_p[:, k % 2, t, 0:keys], att_p[:, k % 2, t, 0:keys],
                                                          small[:, 6 + k % 2, 2 + t:3 + t], None, ALU.mult)
                        ins.then_inc(att_prob, 1)
                    if h >= 2:
                        k = h - 2
                        r = HD * (k % 2)
                        dve.wait_ge(att_hi, a0 + k + 1)
                        nc.vector.tensor_tensor(e_lo[r:r + HD, CONV_C + k // 2, :], ps_o[r:r + HD, k % 2, 0:T],
                                                e_hi[r:r + HD, CONV_C + k // 2, :].bitcast(F32), ALU.subtract)\
                            .then_inc(att_lo, 1)

            def do_gm(s):
                b0 = s.e0 // 2
                def body(b, is_first, last):
                    split_lo(following(s, b, 0, last))
                    split_lo(following(s, b, 1, last))
                    dve.wait_ge(slab_done, s.g0 + 2 * b + 2)
                    dve.wait_ge(gm_sig, b0 + b + 1)
                    wait_up(dve, gm_hi, b0 + b)
                    nc.vector.tensor_tensor(scr2[:, 1, :, :], pb[1][:, :, 0:T], scr[:, 0, :, :], ALU.mult)\
                        .then_inc(gm_mul, 1)
                    dve.wait_ge(gm_mul, b0 + b + 1)
                    nc.vector.tensor_tensor(scr2[:, 0, 0, :], scr2[:, 1, 0, :], scr2[:, 1, 1, :], ALU.add)\
                        .then_inc(gm_sum, 1)
                    dve.wait_ge(gm_hi, b0 + b + 1)
                    nc.vector.tensor_tensor(e_lo[:, 8 + b, :], scr2[:, 0, 0, :], e_hi[:, 8 + b, :].bitcast(F32),
                                            ALU.subtract).then_inc(gm_lo, 1)
                    mods(s, b)
                sweep(dve, s, body)

            def gate_columns(r, x0):
                half = r.get("half")
                wait_up(dve, updated, x0)
                mod_vector(r, r["v"], 2, 0.0 if r["kind"] == "a" else 1.0)
                if half:
                    link(nc.vector.tensor_scalar(cols[:, 2, :], cols[:, 2, :], 0.5, None, ALU.mult))

            def do_out(s):
                r = s.arg
                x = res[r["x"]]
                gate_columns(r, s.x0)

                def body(b, is_first, last):
                    for p in range(2):
                        g = s.g0 + 2 * b + p
                        split_lo(following(s, b, p, last))
                        dve.wait_ge(slab_done, g + 1)
                        for q in range(2):
                            k = 2 * (2 * b + p) + q
                            nc.vector.scalar_tensor_tensor(out=x[:, k, :], in0=pb[p][:, q, 0:T],
                                                           scalar=cols[:, 2, k:k + 1], in1=x[:, k, :],
                                                           op0=ALU.mult, op1=ALU.add).then_inc(updated, 1)
                    mods(s, b)
                sweep(dve, s, body)

            def do_down(s):
                r = s.arg
                x = res[r["x"]]
                if r["part"] != 1:
                    gate_columns(r, s.x0)
                gate = cols[:, 2, :].unsqueeze(2)
                def body(b, is_first, last):
                    for p in range(2):
                        j = 2 * b + p
                        split_lo(following(s, b, p, last))
                        dve.wait_ge(slab_done, s.g0 + j + 1)
                        if r["part"] == 1:
                            dve.wait_ge(updated, s.x0 - 8 + j + 1)
                        nc.vector.scalar_tensor_tensor(out=x[:, j, :], in0=pb[p][:, 0, 0:T], scalar=gate[:, j, :],
                                                       in1=x[:, j, :], op0=ALU.mult, op1=ALU.add)\
                            .then_inc(updated, 1)
                    mods(s, b)
                sweep(dve, s, body)

            def do_upa(s):
                taps = pview(f"ffn_w{s.arg['l']}", 3)

                def tail_mul(e, q):
                    dve.wait_ge(up_silu, e)
                    nc.vector.tensor_tensor(scr[:, q, 0, :], scr[:, q, 0, :], scr[:, q, 1, :], ALU.mult)\
                        .then_inc(up_mul, 1)

                def tail_lo(e, q, j):
                    dve.wait_ge(up_hi, e)
                    nc.vector.tensor_tensor(e_lo[:, j, :], scr[:, q, 0, :], e_hi[:, j, :].bitcast(F32), ALU.subtract)\
                        .then_inc(up_lo, 1)

                def step(b, p, last, has_tail):
                    j = 2 * b + p
                    e = s.e0 + j
                    split_lo(following(s, b, p, last))
                    if has_tail:
                        tail_mul(e, 1 - p)
                    dve.wait_ge(up_lin, e + 1)
                    for n, (q, left) in enumerate(((0, 1), (1, 1), (0, 0), (1, 0))):
                        o = scr[:, p, q, 1:T] if left else scr[:, p, q, 0:T - 1]
                        i_ = pb[p][:, q, 0:T - 1] if left else pb[p][:, q, 1:T]
                        if n >= 2:
                            dve.wait_ge(up_tap, 4 * e + n - 1)
                        nc.vector.scalar_tensor_tensor(out=o, in0=i_, scalar=taps[:, FC * q + j, 0:1] if left else
                                                       taps[:, FC * q + j, 2:3], in1=o, op0=ALU.mult, op1=ALU.add)\
                            .then_inc(up_tap, 1)
                    if has_tail:
                        tail_lo(e, 1 - p, j - 1)

                def body(b, is_first, last):
                    step(b, 0, last, not is_first)
                    step(b, 1, last, True)
                    mods(s, b)
                sweep(dve, s, body)
                tail_mul(s.e0 + FC, 1)
                tail_lo(s.e0 + FC, 1, FC - 1)

            def do_upb(s):
                def tail_lo(e, q, j):
                    dve.wait_ge(upb_hi, e)
                    nc.vector.tensor_tensor(e_lo[:, j, :], scr[:, q, 1, :], e_hi[:, j, :].bitcast(F32), ALU.subtract)\
                        .then_inc(upb_lo, 1)

                def step(b, p, last, has_tail):
                    j = 2 * b + p
                    e = s.e0 + j
                    split_lo(following(s, b, p, last))
                    if has_tail:
                        tail_lo(e, 1 - p, j - 1)
                    dve.wait_ge(upb_silu, e + 1)
                    nc.vector.tensor_tensor(scr[:, p, 1, :], pb[p][:, 1, 0:T], scr[:, p, 0, :], ALU.mult)\
                        .then_inc(upb_mul, 1)

                def body(b, is_first, last):
                    step(b, 0, last, not is_first)
                    step(b, 1, last, True)
                    mods(s, b)
                sweep(dve, s, body)
                tail_lo(s.e0 + FC, 1, FC - 1)

            def do_stick(n):
                for h in range(SB_H + 2):
                    if 1 <= h <= SB_H:
                        k = h - 1
                        dve.wait_ge(st_r, k + 1)
                        nc.vector.tensor_tensor(sb_z[:, k % 2, 1, :], pb[1][:, k % 2, 0:384], sb_z[:, k % 2, 1, :],
                                                ALU.add).then_inc(st_v, 1)
                    if h < SB_H:
                        z, w, zm = pb[0][:, h % 2, 0:384], sb_z[:, h % 2, 0, :], sb_z[:, h % 2, 1, :]
                        dve.wait_ge(st_ln, h + 1)
                        wait_up(dve, st_w, h - 1)
                        nc.vector.tensor_tensor(zm, z, table("drop"), ALU.add).then_inc(st_sp, 1)
                        nc.vector.scalar_tensor_tensor(out=w, in0=z, scalar=0.0, in1=w, op0=ALU.max, op1=ALU.add)\
                            .then_inc(st_sp, 1)
                        dve.wait_ge(st_sp, 3 * h + 2)
                        nc.vector.tensor_tensor(w, w, table("keep"), ALU.mult).then_inc(st_sp, 1)
                    if h >= 2:
                        k = h - 2
                        r = HD * (k % 2)
                        dve.wait_ge(st_hi, k + 1)
                        nc.vector.tensor_tensor(e_lo[r:r + HD, k // 2, :], ps_o[r:r + HD, k % 2, 0:T],
                                                e_hi[r:r + HD, k // 2, :].bitcast(F32), ALU.subtract)\
                            .then_inc(st_lo, 1)

            def do_lin(s):
                w = pview("lru_w", 4)

                def tail_lo(j):
                    dve.wait_ge(lin_hi, j + 1)
                    nc.vector.tensor_tensor(e_lo[:, j, :], l_x[:, j, :], e_hi[:, j, :].bitcast(F32), ALU.subtract)\
                        .then_inc(lin_lo, 1)

                def step(b, p, last, has_tail):
                    j = 2 * b + p
                    split_lo(following(s, b, p, last))
                    dve.wait_ge(lin_lin, j + 1)
                    for k in range(1, 4):
                        if k > 1:
                            dve.wait_ge(lin_tap, 3 * j + k - 1)
                        nc.vector.scalar_tensor_tensor(out=l_x[:, j, k:T], in0=pb[p][:, 1, 0:T - k],
                                                       scalar=w[:, j, 3 - k:4 - k], in1=l_x[:, j, k:T],
                                                       op0=ALU.mult, op1=ALU.add).then_inc(lin_tap, 1)
                    if has_tail:
                        tail_lo(j - 1)

                def body(b, is_first, last):
                    step(b, 0, last, not is_first)
                    step(b, 1, last, True)
                    mods(s, b)
                sweep(dve, s, body)
                tail_lo(RC - 1)

            def do_lgate(s):
                def body(b, is_first, last):
                    for p in range(2):
                        split_lo(following(s, b, p, last))
                sweep(dve, s, body)

            def do_lru(n):
                dve.wait_ge(lru_sq, 1)
                link(nc.vector.tensor_tensor(l_i, l_i, l_x, ALU.mult))
                link(nc.vector.tensor_tensor(l_x, l_r, l_r, ALU.mult))
                nc.vector.scalar_tensor_tensor(out=l_t, in0=l_x, scalar=1.0, in1=l_t, op0=ALU.add, op1=ALU.mult)\
                    .then_inc(lru_y, 1)
                dve.wait_ge(lru_root, 1)
                link(nc.vector.tensor_tensor(l_i, l_i, l_t, ALU.mult))
                for j in range(RC):
                    ins = nc.vector.tensor_tensor_scan(l_x[:, j, :], l_r[:, j, :], l_i[:, j, :], 0.0,
                                                       ALU.mult, ALU.add)
                link(ins)
                nc.vector.tensor_tensor(l_gate, l_gate, l_x, ALU.mult).then_inc(lru_y, 1)
                dve.wait_ge(lru_hi, 1)
                nc.vector.tensor_tensor(e_lo[:, 0:RC, :], l_gate, e_hi[:, 0:RC, :].bitcast(F32), ALU.subtract)\
                    .then_inc(lru_lo, 1)

            kinds = {"glu": do_glu, "q": do_q, "qr": do_q, "v": do_v, "gm": do_gm, "out": do_out, "down": do_down,
                     "upa": do_upa, "upb": do_upb, "lin": do_lin, "lgate": do_lgate}
            others = {"norm": do_norm, "ln": do_ln, "attn": do_attn, "stick": do_stick, "lru": do_lru}
            for what, s in plan:
                kinds[s.kind](s) if what == "slabs" else others[what](s)

        @block.tensor
        def _(pe):
            ones = table("ones")
            pe.wait_ge(setup_in[1], 16)

            def mm3(out, l, r, start, stop):
                nc.tensor.matmul(out, l[0], r[0], start=start, stop=False)
                nc.tensor.matmul(out, l[0], r[1], start=False, stop=False)
                return nc.tensor.matmul(out, l[1], r[0], start=False, stop=stop)

            def freed(s, b, p):
                j = 2 * b + p
                return {"glu": lambda: (glu_mul, s.e0 + j + 1), "q": lambda: (q_copied, s.e0 + j + 1),
                        "qr": lambda: (r_copied, s.e0 + j + 1), "v": lambda: (v_copied, s.e0 + j + 1),
                        "gm": lambda: ((gm_sig, gm_mul)[p], s.e0 // 2 + b + 1),
                        "out": lambda: (updated, s.x0 + 2 * j + 2), "down": lambda: (updated, s.x0 + j + 1),
                        "upa": lambda: (up_tap, 4 * (s.e0 + j + 1)), "upb": lambda: (upb_mul, s.e0 + j + 1),
                        "lin": lambda: (lin_tap, 3 * (j + 1)), "lgate": lambda: (lru_gates, j + 1)}[s.kind]()

            def chunks(s, b, p):
                part = (s.arg or {}).get("part") if isinstance(s.arg, dict) else None
                if s.kind == "gm" and p == 1:
                    return [[(e_hi[:, 4 * q + k, :], e_lo[:, 4 * q + k, :]) for k in range(4)] for q in range(2)]
                if s.kind == "out":
                    at = 8 if s.arg["kind"] == "a" else 0
                    return [[(e_hi[:, at + k, :], e_lo[:, at + k, :]) for k in range(DC)]] * 2
                if s.kind == "down":
                    at = FA if part == 1 else 0
                    return [[(e_hi[:, at + k, :], e_lo[:, at + k, :]) for k in range(s.kc)]]
                if s.kind == "lgate":
                    return [[(e_hi[:, 2 * b + p, :], e_lo[:, 2 * b + p, :])]] * 2
                return [[(h_hi[:, k, :], h_lo[:, k, :]) for k in range(DC)]] * 2

            def operands_ready(s, b, p, is_first):
                if s.kind == "gm" and p == 1 and is_first:
                    pe.wait_ge(ln_lo, s.e0 // 16 + 1)
                    pe.wait_ge(att_lo, NA_H * (s.e0 // 16 + 1))
                if s.kind == "out" and p == 0 and is_first:
                    if s.arg["kind"] == "a":
                        pe.wait_ge(gm_lo, gm_done[id(s)])
                    else:
                        pe.wait_ge(st_lo, SB_H)
                if s.kind == "down" and p == 0 and is_first:
                    part = s.arg["part"]
                    if part == 2:
                        pe.wait_ge(lru_lo, 1)
                    else:
                        pe.wait_ge(up_lo if s.arg["kind"] == "a" else upb_lo, up_done[id(s)] + (FA if part == 0 else FC))
                if s.kind == "lgate":
                    pe.wait_ge(lin_lo, 2 * b + p + 1)

            gm_done, up_done, had, prior = {}, {}, {}, {}
            before = None
            for what, s in plan:
                if what == "slabs":
                    gm_done[id(s)] = had.get("gm", 0) // 2
                    up_done[id(s)] = had.get("upa" if isinstance(s.arg, dict) and s.arg.get("kind") == "a" else "upb",
                                             0) - FC
                    had[s.kind] = s.e0 + 2 * s.bodies
                    prior[id(s)] = before
                    before = s

            def do_slabs(s):
                def body(b, is_first, last):
                    for p in range(2):
                        g = s.g0 + 2 * b + p
                        operands_ready(s, b, p, is_first)
                        pe.wait_ge(lo_ready, g + 1)
                        if not is_first:
                            pe.wait_ge(*freed(s, b - 1, p))
                        elif prior[id(s)] is not None:
                            q = prior[id(s)]
                            pe.wait_ge(*freed(q, q.bodies - 1, p))
                        if s.kind == "v":
                            for t in range(2):
                                for k in range(DC):
                                    x = [h[:, k, t * P:(t + 1) * P] for h in (h_hi, h_lo)]
                                    w = [v[:, p, 256 * k:256 * (k + 1)] for v in (w_hi, w_lo)]
                                    ins = mm3(pb[p][:, t, 0:256], x, w, k == 0, k == DC - 1)
                        else:
                            for q, xs in enumerate(chunks(s, b, p)):
                                n = len(xs)
                                for k, x in enumerate(xs):
                                    c = P * (n * q + k)
                                    w = (w_hi[:, p, c:c + P], w_lo[:, p, c:c + P])
                                    ins = mm3(pb[p][:, q, 0:T], w, x, k == 0, k == n - 1)
                        ins.then_inc(slab_done, 1)
                sweep(pe, s, body)

            def do_norm(n):
                i = n["i"]
                for k in range(DC):
                    pe.wait_ge(sq_ready, 4 * i + k // 2 + 1)
                    ins = nc.tensor.matmul(ps_t[:, 0, 0:T], ones, nsq[:, k, :], start=k == 0, stop=k == DC - 1)
                ins.then_inc(sum_ready, 1)
                if n["dest"] == "h":
                    pe.wait_ge(hn_lo, 2 * n["ih"] + 2)

            def do_ln(n):
                i = n["i"]
                pe.wait_ge(conv_tap, CONV_C * CONV_K * (i + 1))
                for k in range(CONV_C):
                    ins = nc.tensor.matmul(ps_t[:, 0, 0:T], ones, cy[:, k, :], start=k == 0, stop=k == CONV_C - 1)
                ins.then_inc(ln_sum, 1)
                for k in range(CONV_C):
                    pe.wait_ge(ln_sq, 2 * i + k // 2 + 1)
                    ins = nc.tensor.matmul(ps_t[:, 1, 0:T], ones, ln_y[:, k, :], start=k == 0, stop=k == CONV_C - 1)
                ins.then_inc(ln_var, 1)

            def do_attn(n):
                a0, is_ctx = NA_H * n["i"], n["ctx"]
                nk = 2 if is_ctx else 4
                pe.wait_ge(q_copied, n["had"]["q"])
                if not is_ctx:
                    pe.wait_ge(q_roped, n["had"]["qr"])
                pe.wait_ge(v_copied, n["had"]["v"])
                for h in range(NA_H + 2):
                    if h < NA_H:
                        wait_up(pe, att_max, a0 + h - 1)
                        c, r = h // 2, HD * (h % 2)
                        for t in range(2):
                            q = dst["q"][r:r + HD, c, t * P:(t + 1) * P]
                            keys = [dst["kc"]] if is_ctx else [dst["k"], dst["kc"]]
                            for n_k, k_ in enumerate(keys):
                                ins = nc.tensor.matmul(pb[h % 2][:, t, T * n_k:T * (n_k + 1)], q, k_[r:r + HD, c, :],
                                                       start=True, stop=True)
                        ins.then_inc(att_s, 1)
                    if 1 <= h <= NA_H:
                        k = h - 1
                        pe.wait_ge(att_prob, a0 + k + 1)
                        wait_up(pe, att_tc, a0 + k)
                        for t in range(2):
                            for j in range(nk):
                                ins = nc.tensor.transpose(ps_t[:, t, j * P:(j + 1) * P],
                                                          att_p[:, k % 2, t, j * P:(j + 1) * P], table("ident"))
                        ins.then_inc(att_t, 1)
                    if h >= 2:
                        k = h - 2
                        c, r = k // 2, HD * (k % 2)
                        pe.wait_ge(att_tc, a0 + k + 1)
                        wait_up(pe, att_lo, a0 + k - 1)
                        for j in range(nk):
                            v = (dst["vc"] if is_ctx else dst["v"])[:, j, HD * k:HD * (k + 1)] if j < 2 else \
                                dst["vc"][:, j - 2, HD * k:HD * (k + 1)]
                            ins = nc.tensor.matmul(ps_o[r:r + HD, k % 2, 0:T], v, att_pt[:, k % 2, j, :],
                                                   start=j == 0, stop=j == nk - 1)
                        ins.then_inc(att_o, 1)
                pe.wait_ge(att_max, a0 + NA_H)

            def do_stick(n):
                pe.wait_ge(q_copied, n["had"]["q"])
                pe.wait_ge(v_copied, n["had"]["v"])
                for h in range(SB_H + 2):
                    if h < SB_H:
                        wait_up(pe, st_sp, 3 * (h - 1))
                        c, r = h // 2, HD * (h % 2)
                        q, k_ = dst["sbq"][r:r + HD, c, :], dst["sbk"][r:r + HD, c, :]
                        nc.tensor.matmul(pb[0][:, h % 2, 0:256], k_[:, 0:P], q, start=True, stop=True)
                        nc.tensor.matmul(pb[0][:, h % 2, 256:384], k_[:, P:T], q[:, P:T], start=True, stop=True)\
                            .then_inc(st_z, 1)
                    if 1 <= h <= SB_H:
                        k = h - 1
                        pe.wait_ge(st_sp, 3 * (k + 1))
                        wait_up(pe, st_v, k - 1)
                        w, o = sb_z[:, k % 2, 0, :], pb[1][:, k % 2, :]
                        nc.tensor.matmul(o[:, 256:384], table("ntri"), w[:, 256:384], start=True, stop=True)
                        nc.tensor.matmul(o[:, 0:128], table("ntri"), w[:, 0:128], start=True, stop=True)
                        nc.tensor.matmul(o[:, 128:256], table("ntri"), w[:, 128:256], start=True, stop=False)
                        nc.tensor.matmul(o[:, 128:256], table("nones"), w[:, 256:384], start=False, stop=True)\
                            .then_inc(st_r, 1)
                    if h >= 2:
                        k = h - 2
                        r = HD * (k % 2)
                        pe.wait_ge(st_w, k + 1)
                        wait_up(pe, st_lo, k - 1)
                        v, w = dst["sbv"], sb_z[:, k % 2, 2, :]
                        v0, v1 = v[:, 0, HD * k:HD * (k + 1)], v[:, 1, HD * k:HD * (k + 1)]
                        o = ps_o[r:r + HD, k % 2, :]
                        nc.tensor.matmul(o[:, 0:128], v0, w[:, 0:128], start=True, stop=True)
                        nc.tensor.matmul(o[:, 128:256], v0, w[:, 128:256], start=True, stop=False)
                        nc.tensor.matmul(o[:, 128:256], v1, w[:, 256:384], start=False, stop=True)\
                            .then_inc(st_o, 1)

            for what, s in plan:
                if what == "slabs":
                    do_slabs(s)
                elif what != "lru":
                    {"norm": do_norm, "ln": do_ln, "attn": do_attn, "stick": do_stick}[what](s)
    return nc


def _pack(w, order, group):
    k, n = w.shape[0] // P, w.shape[1] // P
    t = w.reshape(k, P, n, P).transpose(2, 1, 0, 3)[np.asarray(order)]
    t = t.reshape(len(order) // group, group, P, k * P).transpose(0, 2, 1, 3)
    return np.ascontiguousarray(t.reshape(len(order) // group, P, group * k * P))


def _pack_wide(w):
    k, n = w.shape[0] // P, w.shape[1] // 256
    return np.ascontiguousarray(w.reshape(k, P, n, 256).transpose(2, 1, 0, 3).reshape(n, P, k * 256))


def _pairs(n, off):
    return [c for j in range(n) for c in (j, off + j)]


def _rows(v):
    return v.reshape(-1, P).T


def _taps(w):
    return w.T.reshape(-1, P, w.shape[0]).transpose(1, 0, 2).reshape(P, -1)


def _fmajor(x):
    return np.ascontiguousarray(x.T.reshape(DC, P, T).transpose(1, 0, 2))


def _tables():
    t = np.zeros((P, NTAB), np.float32)

    def put(name, v):
        at, n = TCOL[name]
        t[:, at:at + n] = v

    put("ident", np.eye(P))
    put("ones", 1.0)
    s = np.arange(P)
    put("ntri", -(s[:, None] >= s[None, :]).astype(np.float32))
    put("nones", -1.0)
    half = HD // 2
    freq = (np.float32(10000.0) ** (-np.arange(0, half, 2, dtype=np.float32) / np.float32(half))).astype(np.float32)
    tok = np.arange(T)
    pos = np.stack([tok // GRID_W, tok % GRID_W]).astype(np.float32)
    f = np.arange(P) % HD
    ang = pos[f // half] * freq[f % (half // 2)][:, None]
    put("cos", np.cos(ang))
    put("sin", np.sin(ang) * np.where(f % half < half // 2, -1.0, 1.0)[:, None])
    q = np.concatenate([np.arange(T), np.arange(P)])
    keep = (s[:, None] < q[None, :]).astype(np.float32)
    put("keep", keep)
    put("drop", np.where(keep > 0, 0.0, -1e30))
    return t


def _relative_bias(rpb):
    t = np.arange(T)
    row, col = t // GRID_W, t % GRID_W
    start = np.clip(col - 8, 0, GRID_W - 16)
    inside = (col[None, :] >= start[:, None]) & (col[None, :] < start[:, None] + 16)
    dr = row[None, :] - row[:, None] + 7
    dc = np.where(inside, col[None, :] - col[:, None] + 15, 0)
    b = np.where(inside[None], rpb[:, dr, dc], np.float32(-1e30))
    return np.ascontiguousarray(b.reshape(NA_H, 2, P, T).transpose(0, 2, 1, 3))


def arrays_of(i):
    a = {"x": _fmajor(i["x"][0]), "ctx": _fmajor(i["ctx"][0])}
    par = np.zeros((P, NPARAM), np.float32)

    def put(name, v):
        at, n = PCOL[name]
        par[:, at:at + n] = v

    put("cvec", np.concatenate([_rows(i["c"][0]), _rows(i["c_ctx"]), _rows(i["c_2"][0])], 1))
    mod, bias = [], []
    for l in range(2):
        put(f"b_ada{l}", _rows(i["b_ada"][l]))
        put(f"norm1{l}", _rows(i["norm1_g"][l]))
        put(f"norm2{l}", _rows(i["norm2_g"][l]))
        put(f"conv_w{l}", _taps(i["conv_dw"][l]))
        put(f"conv_b{l}", _rows(i["conv_dw_b"][l]))
        put(f"ln_g{l}", _rows(i["conv_ln_g"][l]))
        put(f"ln_b{l}", _rows(i["conv_ln_b"][l]))
        put(f"ffn_w{l}", _taps(i["ffn_dw"][l]))
        put(f"ffn_b{l}", _rows(i["ffn_dw_b"][l]))
        put(f"mod_b{l}", _rows(i["mod_b_2"][l]))
        put(f"norm_b{l}", _rows(i["norm_g_2"][l].reshape(-1)))
        w = i["w_in"][l]
        a[f"w_glu{l}"] = _pack(w, _pairs(4, 4), 2)
        a[f"w_q{l}"] = _pack(w, range(8, 12), 2)
        a[f"w_k{l}"] = _pack(w, range(12, 16), 2)
        a[f"w_v{l}"] = _pack_wide(w[:, 2048:2560])
        a[f"w_gate{l}"] = _pack(w[:, 2560:], _pairs(8, 8), 2)
        a[f"w_merge{l}"] = np.concatenate([_pack(i["w_conv_out"][l], range(8), 1),
                                           _pack(i["w_na_out"][l], range(8), 1)], 2)
        a[f"w_out{l}"] = _pack(i["w_out"][l], range(8), 2)
        a[f"w_up{l}"] = _pack(i["w_up"][l], _pairs(FC, FC), 2)
        a[f"w_down{l}0"] = _pack(i["w_down"][l][:FA * P], range(8), 1)
        a[f"w_down{l}1"] = _pack(i["w_down"][l][FA * P:], range(8), 1)
        for f in range(2):
            a[f"w_gu{l}{f}"] = _pack(i["ffn_w_gu_2"][l, f], _pairs(FC, FC), 2)
            a[f"w_dn{l}{f}0"] = _pack(i["ffn_w_down_2"][l, f][:FA * P], range(8), 1)
            a[f"w_dn{l}{f}1"] = _pack(i["ffn_w_down_2"][l, f][FA * P:], range(8), 1)
        bias.append(_relative_bias(i["na_rpb"][l]))
    a["w_mod"] = np.concatenate([_pack_wide(i["w_ada"][l]) for l in range(2)]
                                + [_pack_wide(i["mod_w_2"][l]) for l in range(2)], 0)
    qkv = i["sb_w_qkv_2"][0]
    a["w_sbq"] = _pack(qkv, range(8), 2)
    a["w_sbk"] = _pack(qkv, range(8, 16), 2)
    a["w_sbv"] = _pack_wide(qkv[:, 2048:])
    a["w_sbo"] = _pack(i["sb_w_o_2"][0], range(8), 2)
    a["w_lin"] = _pack(i["lru_w_in_2"][0], _pairs(RC, RC), 2)
    a["w_lg"] = np.concatenate([i["lru_w_r_2"][0], i["lru_w_i_2"][0]], 2)
    a["w_lout"] = _pack(i["lru_w_out_2"][0], range(8), 1)
    put("final_a", _rows(i["final_norm_g"]))
    put("final_b", _rows(i["final_norm_g_2"]))
    put("lru_w", _taps(i["lru_conv_w_2"][0]))
    put("lru_b", _rows(i["lru_conv_b_2"][0]))
    put("lru_br", _rows(i["lru_b_r_2"][0]))
    put("lru_bi", _rows(i["lru_b_i_2"][0]))
    put("lru_lam", _rows(i["lru_lambda_2"][0]))
    a["params"], a["tables"], a["rel_bias"] = par, _tables(), np.stack(bias)
    return a


def kernel(**inputs):
    import concourse.bacc as bacc
    from concourse.bass_utils import run_bass_kernel_spmd

    host = arrays_of({k: np.asarray(v) for k, v in inputs.items()})
    nc = bacc.Bacc("TRN2", target_bir_lowering=False, num_devices=1)
    aps = {k: nc.dram_tensor(f"in_{k}", v.shape, F32, kind="ExternalInput").ap() for k, v in host.items()}
    aps["y"] = nc.dram_tensor("y", (P, DC, T), F32, kind="ExternalOutput").ap()
    build(nc, aps)
    r = run_bass_kernel_spmd(nc, [{f"in_{k}": v for k, v in host.items()}], core_ids=[0])
    y = r.results[0]["y"]
    return np.ascontiguousarray(y.transpose(1, 0, 2).reshape(D, T).T).reshape(1, T, D)
```

```python
from contextlib import ExitStack
from dataclasses import dataclass

import numpy as np
import concourse.bass as bass
from concourse import mybir

P = 128
D = 1024
T = 256
DC = D // P
GRID_W = 64
CONV_C, CONV_K = 4, 31
PAD = CONV_K // 2
UW = T + 2 * PAD + 2
HD = 64
NA_H, NA_C = 8, 4
SB_H = 16
FC = 22
FA = 12
RC = 10
SLAB = 16 * P
CONV_PIECES = 11
LN_AT = 6
HALF = SLAB // 2
EPS = 1e-6
N_MOD_A, N_MOD_B = 6 * D // 256, 9 * D // 256
N_MOD = 2 * N_MOD_A + 2 * N_MOD_B
N_FIRST = 8
N_DOUBLE = N_MOD_A + 8
SERIES = 10

F32 = mybir.dt.float32
F32R = mybir.dt.float32r
ALU = mybir.AluOpType
ACT = mybir.ActivationFunctionType
RADD = bass.bass_isa.ReduceOp.add
AXX = mybir.AxisListType.X


def param_columns():
    at, n = {}, 0
    sizes = []
    for l in range(2):
        sizes += [(f"b_ada{l}", 48), (f"norm1{l}", 8), (f"norm2{l}", 8), (f"conv_w{l}", CONV_C * CONV_K),
                  (f"conv_b{l}", 4), (f"ln_g{l}", 4), (f"ln_b{l}", 4), (f"ffn_w{l}", 3 * 44), (f"ffn_b{l}", 44),
                  (f"mod_b{l}", 72), (f"norm_b{l}", 24)]
    sizes += [("final_a", 8), ("final_b", 8), ("lru_w", 40), ("lru_b", 10), ("lru_br", 10), ("lru_bi", 10),
              ("lru_lam", 10)]
    for name, k in sizes:
        at[name] = (n, k)
        n += k
    return at, n


PCOL, NPARAM = param_columns()
TCOL = {"ident": (0, 128), "ones": (128, 128), "ntri": (256, 128), "nones": (384, 128), "cos": (512, 256),
        "sin": (768, 256)}
NTAB = 1024
NMASK = 768


@dataclass
class Stage:
    kind: str
    src: tuple
    width: tuple
    bodies: int
    kc: int = 8
    mods: int = 0
    arg: object = None
    g0: int = 0
    m0: int = 0
    e0: int = 0
    x0: int = 0
    nxt: object = None
    norm_i: object = None
    after: object = None


def build(nc, a):
    plan = []

    def stage(kind, src, width, bodies, **kw):
        src = src if isinstance(src, tuple) else (src, src)
        width = width if isinstance(width, tuple) else (width, width)
        plan.append(("slabs", Stage(kind, src, width, bodies, **kw)))

    def norm(x, kind, l, v, need, dest="h"):
        plan.append(("norm", dict(x=x, kind=kind, l=l, v=v, need=need, dest=dest)))

    def layer_a(l, x):
        dbl = l == 0 and x == "ctx"
        norm(x, "a", l, 0, l * N_MOD_A + 8)
        stage("glu", a[f"w_glu{l}"], SLAB, 2, mods=1)
        rope = x == "x"
        qk = "qr" if rope else "q"
        stage(qk, a[f"w_q{l}"], SLAB, 1, mods=1, arg=dict(dst="q", rope=rope, scale=HD ** -0.5, conv=(l, 0, 2)))
        stage(qk, a[f"w_k{l}"], SLAB, 1, mods=1, arg=dict(dst="k" if rope else "kc", rope=rope, scale=1.0, conv=(l, 2, 4)))
        stage("v", a[f"w_v{l}"], SLAB, 1, mods=1, arg=dict(dst="v" if rope else "vc", conv=(l, 4, 6), heads=NA_H))
        stage("gate", a[f"w_gate{l}"], SLAB, 4, mods=1, arg=dict(l=l, ctx=x == "ctx"))
        stage("merge", a[f"w_merge{l}"], SLAB, 2, mods=1)
        stage("out", a[f"w_out{l}"], SLAB, 2, mods=1 + l,
              arg=dict(x=x, kind="a", l=l, v=2, need=l * N_MOD_A + 12))
        norm(x, "a", l, 3, l * N_MOD_A + 20)
        stage("upa", a[f"w_up{l}"], SLAB, FC // 2, mods=1, arg=dict(l=l))
        for part in range(2):
            stage("down", a[f"w_down{l}{part}"], (FA, FC - FA)[part] * P, 4, kc=(FA, FC - FA)[part], mods=0 if dbl else 1,
                  arg=dict(x=x, kind="a", l=l, v=5, need=(l + 1) * N_MOD_A, part=part))

    def ffn_b(l, f, sub, mods):
        base = 2 * N_MOD_A + l * N_MOD_B + 12 * sub
        norm("x", "b", l, 3 * sub, base + 8)
        stage("upb", a[f"w_gu{l}{f}"], SLAB, FC // 2, mods=mods[0])
        for part in range(2):
            stage("down", a[f"w_dn{l}{f}{part}"], (FA, FC - FA)[part] * P, 4, kc=(FA, FC - FA)[part], mods=mods[1 + part],
                  arg=dict(x="x", kind="b", l=l, v=3 * sub + 2, need=base + 12, part=part, half=True))

    layer_a(0, "ctx")
    layer_a(0, "x")
    norm("ctx", "a", 1, 0, N_MOD_A + 8)
    stage("q", a["w_k1"], SLAB, 1, mods=1, arg=dict(dst="kc", rope=False, scale=1.0, conv=None))
    stage("v", a["w_v1"], SLAB, 1, mods=2, arg=dict(dst="vc", conv=None, heads=NA_H))
    layer_a(1, "x")
    norm("x", "fa", 0, 0, 0, dest="x")
    ffn_b(0, 0, 0, (1, 1, 1))
    norm("x", "b", 0, 3, 2 * N_MOD_A + 20)
    stage("q", a["w_sbq"], SLAB, 2, arg=dict(dst="sbq", rope=False, scale=HD ** -0.5, conv=None))
    stage("q", a["w_sbk"], SLAB, 2, arg=dict(dst="sbk", rope=False, scale=1.0, conv=None))
    stage("v", a["w_sbv"], SLAB, 2, arg=dict(dst="sbv", conv=None, heads=SB_H))
    plan.append(("stick", {}))
    stage("out", a["w_sbo"], SLAB, 2, arg=dict(x="x", kind="b", l=0, v=5, need=2 * N_MOD_A + 24))
    ffn_b(0, 1, 2, (0, 0, 0))
    ffn_b(1, 0, 0, (0, 0, 0))
    norm("x", "b", 1, 3, 2 * N_MOD_A + N_MOD_B + 20)
    stage("lin", a["w_lin"], SLAB, RC // 2)
    stage("lgate", a["w_lg"], 2 * P, RC // 2, kc=1)
    plan.append(("lru", {}))
    stage("down", a["w_lout"], RC * P, 4, kc=RC,
          arg=dict(x="x", kind="b", l=1, v=5, need=2 * N_MOD_A + N_MOD_B + 24, part=2))
    ffn_b(1, 1, 2, (0, 0, 0))
    norm("x", "fb", 0, 0, 0, dest="y")

    g = xn = 0
    m = N_FIRST
    n_out, last_entry, n_attn = 0, None, 0
    of_kind, seen, before, n_h, n_bias, had_x = {}, {}, None, 0, 0, False
    for what, s in plan:
        if what == "slabs":
            s.g0, s.m0, s.e0, s.x0 = g, m, of_kind.get(s.kind, 0), xn
            n = 2 * s.bodies
            g += n
            m += s.mods * s.bodies
            of_kind[s.kind] = s.e0 + n
            if s.kind == "gate":
                s.arg.update(i=n_attn, n_bias=n_bias, had=dict(of_kind))
                n_attn += 1
                n_bias += not s.arg["ctx"]
            if s.kind == "out":
                xn += 2 * n
            if s.kind == "down":
                xn += n
            if before is not None:
                before.nxt = s
            before = s
        else:
            s["i"] = seen.get(what, 0)
            seen[what] = s["i"] + 1
            s["x0"] = xn
            s["had"] = dict(of_kind)
            if what == "norm":
                s["ih"], s["outs"] = n_h, n_out
                n_out += s["dest"] != "h"
                what1, s1 = last_entry if last_entry else ("", None)
                s["fused"] = what1 == "slabs" and s1.kind in ("out", "down") and s1.arg["x"] == s["x"] and s1.kind
                if s["fused"]:
                    s1.norm_i = s["i"]
                n_h += s["dest"] == "h"
                s["first_x"] = s["x"] == "x" and not had_x
                had_x = had_x or s["x"] == "x"
        if what == "slabs" and last_entry and last_entry[0] == "norm":
            s.after = last_entry[1]
        last_entry = (what, s)
    n_mod = m
    assert n_mod <= N_MOD
    first = next(s for what, s in plan if what == "slabs")

    with ExitStack() as ctx:
        def sb(name, shape, dt=F32):
            return ctx.enter_context(nc.sbuf_tensor(name, shape, dt))

        def sem(name):
            return ctx.enter_context(nc.semaphore(name))

        raw = sb("raw", [P, 2, SLAB])
        w_hi = sb("w_hi", [P, 2, SLAB], F32R)
        w_lo = sb("w_lo", [P, 2, SLAB], F32R)
        res = {"x": sb("x_res", [P, DC, T]), "ctx": sb("ctx_res", [P, DC, T])}
        h_hi = sb("h_hi", [P, DC, T], F32R)
        h_lo = sb("h_lo", [P, DC, T], F32R)
        e_at = -(-nc.sbuf_base // 32) * 32
        e_both = sb("e_both", [P, 2, FC, T], F32R)
        e_hi, e_lo = e_both[:, 0], e_both[:, 1]
        e_plain = nc.alloc_sbuf_tensor_at("e_plain", [P, 2, FC, T], F32, offset=e_at)
        modraw = sb("modraw", [P, 2, D])
        modprod = sb("modprod", [P, 2, D])
        cact = sb("cact", [P, 2, D])
        modcol = sb("modcol", [P, 2, 2 * N_MOD])
        par = sb("par", [P, NPARAM])
        tab = sb("tab", [P, NTAB])
        cols = sb("cols", [P, 4, 8])
        small = sb("small", [P, 8, RC])
        arena = sb("arena", [P, 11392])
        bias = sb("bias", [P, 2, 2, 256])
        masks = bias[:].rearrange("p a b c -> p (a b c)")[:, 0:NMASK]

        def view(at, *shape):
            n = int(np.prod(shape))
            v = arena[:, at:at + n]
            if len(shape) == 2:
                return v.rearrange("p (b c) -> p b c", b=shape[0])
            if len(shape) == 3:
                return v.rearrange("p (b c d) -> p b c d", b=shape[0], c=shape[1])
            return v

        dst = {"q": view(0, NA_C, T), "k": view(1024, NA_C, T), "kc": view(3072, NA_C, T),
               "v": view(2048, 2, 512), "vc": view(4096, 2, 512),
               "sbq": view(0, DC, T), "sbk": view(2048, DC, T), "sbv": view(4096, 2, D)}
        u_pad = view(5120, CONV_C, UW)
        cy = view(5120 + CONV_C * UW, CONV_C, T)
        free0 = 5120 + CONV_C * (UW + T)
        att_p = view(free0, 2, 2, 512)
        att_pt = view(free0 + 2048, 2, 4, T)
        gates = e_plain[:, :, 8:16, :]
        ln_y = e_plain[:, 0, 16:20, :]
        ln_r = e_plain[:, 1, 16:21, :]
        diag = e_plain[:, 0, 20:22, :].rearrange("p a (t q) -> p a t q", t=2)
        scr = view(free0, 2, 2, T)
        scr2 = view(free0 + 1024, 2, 2, T)
        nsq = view(0, DC, T)
        nrm = view(2048, 4, T)
        sb_z = view(6144, 2, 3, 384)
        l_gate, l_x, l_r = (view(RC * T * k, RC, T) for k in range(3))
        l_i, l_t = e_plain[:, 0, RC:2 * RC, :], e_plain[:, 1, RC:2 * RC, :]
        assert free0 + 4096 <= 11392 and 3 * RC * T <= 11392 and 6144 + 2304 <= 11392
        mod_first = [e_plain[:, e, DC * k:DC * (k + 1), :].rearrange("p a b -> p (a b)")
                     .rearrange("p (c k) -> p c k", c=2) for e in range(2) for k in range(2)] \
            + [view(9216, 2, D), modraw[:]]
        unused = res["x"][:, 0:4, :].rearrange("p a b -> p (a b)")

        pb = [ctx.enter_context(nc.psum_tensor(f"bank_pair{k}", [P, 2, 512], F32)) for k in range(2)]
        ps_t = ctx.enter_context(nc.psum_tensor("ps_t", [P, 2, 512], F32))
        ps_o = ctx.enter_context(nc.psum_tensor("ps_o", [P, 2, 512], F32))

        def pcol(name, k=0, n=1):
            at = PCOL[name][0] + k
            return par[:, at:at + n]

        def pview(name, k):
            at, n = PCOL[name]
            return par[:, at:at + n].rearrange("p (c k) -> p c k", k=k)

        def table(name):
            at, n = TCOL[name]
            return tab[:, at:at + n]

        raw_in = [sem("raw_in0"), sem("raw_in1")]
        hi_ready, lo_ready = sem("hi_ready"), sem("lo_ready")
        half_done = sem("half_done")
        setup_in = [sem(f"setup_in{k}") for k in range(4)]
        first_in = [sem(f"first_in{k}") for k in range(N_FIRST)]
        mod_in, mod_mul = [sem("mod_in0"), sem("mod_in1")], sem("mod_mul")
        mod_done, mod_ctx_done = sem("mod_done"), sem("mod_ctx_done")
        vec_in = [sem(f"vec_in{k}") for k in range(3)]
        c_ready, masks_in = sem("c_ready"), sem("masks_in")
        dve_chain, act_chain = sem("dve_chain"), sem("act_chain")
        updated = sem("updated")
        sq_ready, sum_ready, ms_ready, std_ready = (sem(k) for k in ("sq_ready", "sum_ready", "ms_ready", "std_ready"))
        norm_ready, hn_hi, hn_lo = sem("norm_ready"), sem("hn_hi"), sem("hn_lo")
        norm_out = sem("norm_out")
        glu_sig, glu_mul = sem("glu_sig"), sem("glu_mul")
        q_copied, r_copied, q_roped, v_copied = (sem(k) for k in ("q_copied", "r_copied", "q_roped", "v_copied"))
        conv_tap = sem("conv_tap")
        ln_sum, ln_centred, ln_sq, ln_var, ln_ms, ln_std = (sem(f"ln_{k}") for k in
                                                            ("sum", "centred", "sq", "var", "ms", "std"))
        ln_scaled, ln_hi, ln_lo = sem("ln_scaled"), sem("ln_hi"), sem("ln_lo")
        bias_in = [sem("bias_in0"), sem("bias_in1")]
        att_s, att_max, att_exp, att_diag = sem("att_s"), sem("att_max"), sem("att_exp"), sem("att_diag")
        att_t, att_tc, att_o, att_hi, att_lo = (sem(f"att_{k}") for k in ("t", "tc", "o", "hi", "lo"))
        gate_copied = sem("gate_copied")
        gm_sig, gm_mul, gm_sum, gm_hi, gm_lo = (sem(f"gm_{k}") for k in ("sig", "mul", "sum", "hi", "lo"))
        up_lin, up_tap, up_silu, up_mul, up_hi, up_lo = (sem(f"up_{k}") for k in
                                                         ("lin", "tap", "silu", "mul", "hi", "lo"))
        upb_silu, upb_mul, upb_hi, upb_lo = (sem(f"upb_{k}") for k in ("silu", "mul", "hi", "lo"))
        st_z, st_ln, st_sp, st_r, st_v, st_w, st_o, st_hi, st_lo = (
            sem(f"st_{k}") for k in ("z", "ln", "sp", "r", "v", "w", "o", "hi", "lo"))
        lin_lin, lin_tap, lin_hi, lin_lo = (sem(f"lin_{k}") for k in ("lin", "tap", "hi", "lo"))
        lru_gates, lru_sq, lru_root, lru_y, lru_hi, lru_lo = (sem(f"lru_{k}") for k in
                                                              ("gates", "sq", "root", "y", "hi", "lo"))
        stored = sem("stored")

        block = ctx.enter_context(nc.Block())

        def sweep(eng, s, body):
            n = s.bodies
            if n <= 3 or s.kind == "lgate":
                for b in range(n):
                    body(b, b == 0, b == n - 1)
            else:
                body(0, True, False)
                with eng.Fori(1, n - 1) as b:
                    body(b, False, False)
                body(n - 1, False, True)

        def following(s, b, p, last):
            if p == 0:
                return s, b, 1
            if last:
                return (s.nxt, 0, 0) if s.nxt is not None else None
            return s, b + 1, 0

        def after_next(s, b, p, last):
            if last:
                return (s.nxt, 0, p) if s.nxt is not None else None
            return s, b + 1, p

        def prepare(split, s, b, p, last):
            split(following(s, b, p, last), 1)
            split(after_next(s, b, p, last), 0)

        def wait_up(eng, s, value):
            if not isinstance(value, int) or value > 0:
                eng.wait_ge(s, value)

        @block.sync
        def _(sp):
            sp.dma_start(cact[:, 1, :], a["vectors"][:, D:2 * D]).then_inc(vec_in[1], 16)
            for k in range(6):
                sp.dma_start(mod_first[k], a["w_mod"][k].rearrange("p (c k) -> p c k", c=2)).then_inc(first_in[k], 16)
                if k == 0:
                    sp.dma_start(cact[:, 0, :], a["vectors"][:, 0:D]).then_inc(vec_in[0], 16)
                if k == 1:
                    sp.dma_start(res["ctx"][:], a["ctx"]).then_inc(setup_in[2], 16)
                if k == 3:
                    sp.dma_start(tab[:], a["tables"]).then_inc(setup_in[1], 16)
                    sp.dma_start(par[:], a["params"]).then_inc(setup_in[0], 16)

            def load(s, b, p):
                g = s.g0 + 2 * b + p
                wait_up(sp, lo_ready, 2 * g - 2)
                j = 2 * b + p
                sp.dma_start(raw[:, p, 0:s.width[p]], s.src[p][j]).then_inc(raw_in[p], 16)

            for k in (6, 7):
                sp.wait_ge(mod_mul, 2 * (k - 5))
                sp.wait_ge(mod_ctx_done, 2 * (k - 5))
                sp.dma_start(mod_first[k - 6], a["w_mod"][k].rearrange("p (c k) -> p c k", c=2))\
                  .then_inc(first_in[k], 16)
            load(first, 0, 0)
            load(first, 0, 1)
            for what, s in plan:
                if what == "norm" and s["kind"] == "fa":
                    sp.wait_ge(att_max, NA_H * n_attn)
                    sp.dma_start(masks, a["masks"]).then_inc(masks_in, 16)
                if what != "slabs":
                    continue

                def body(b, is_first, last, s=s):
                    for p in range(2):
                        if not (s is first and is_first):
                            load(s, b, p)
                sweep(sp, s, body)
            for f in range(2):
                sp.wait_ge(norm_out, DC + 4 * (f + 1))
                sp.dma_start(a["y"][:, 4 * f:4 * f + 4, :], nsq[:, 4 * f:4 * f + 4, :]).then_inc(stored, 16)
            sp.wait_ge(stored, 32)

        @block.gpsimd
        def _(pool):
            def multiply(m, c, tile, vec):
                wait_up(pool, mod_done, 2 * m + c - 1)
                nc.gpsimd.tensor_tensor(modprod[:, c, :], tile[:, c, :], cact[:, vec, :], ALU.mult).then_inc(mod_mul, 1)

            def load_mod(m, c, double):
                pool.wait_ge(mod_mul, 2 * m - 1 + c)
                if double:
                    pool.wait_ge(mod_ctx_done, 2 * m - 1 + c)
                nc.gpsimd.dma_start(modraw[:, c, :], a["w_mod"][m, :, D * c:D * (c + 1)]).then_inc(mod_in[c], 16)

            pool.wait_ge(c_ready, 2)
            for m in range(N_FIRST):
                pool.wait_ge(first_in[m], 16)
                for c in range(2):
                    multiply(m, c, mod_first[m % 6], 0)
            for c in range(2):
                load_mod(N_FIRST, c, True)

            def steps(m0, m1, vec, double):
                if m1 > m0:
                    with pool.Fori(m0, m1) as m:
                        for c in range(2):
                            pool.wait_ge(mod_in[c], 16 * (m - N_FIRST + 1))
                            multiply(m, c, modraw, vec)
                            load_mod(m + 1, c, double)
            top = n_mod - 1
            steps(N_FIRST, min(N_DOUBLE, top), 0, True)
            if top > N_DOUBLE:
                pool.wait_ge(mod_ctx_done, 2 * N_DOUBLE)
                nc.gpsimd.dma_start(res["x"][:], a["x"]).then_inc(setup_in[3], 16)
                nc.gpsimd.dma_start(cact[:, 1, :], a["vectors"][:, 2 * D:3 * D]).then_inc(vec_in[2], 16)
            steps(N_DOUBLE, min(2 * N_MOD_A, top), 0, False)
            if top > 2 * N_MOD_A:
                pool.wait_ge(c_ready, 4)
                steps(2 * N_MOD_A, top, 1, False)
            for c in range(2):
                pool.wait_ge(mod_in[c], 16 * (top - N_FIRST + 1))
                multiply(top, c, modraw, 1 if top >= 2 * N_MOD_A else 0)

        @block.scalar
        def _(act):
            chain = [0]

            def link(ins):
                chain[0] += 1
                ins.then_inc(act_chain, 1)
                act.wait_ge(act_chain, chain[0])

            def split_hi(nx, f):
                if nx is None:
                    return
                s, b, p = nx
                g, w = s.g0 + 2 * b + p, s.width[p] // 2
                if f == 0:
                    act.wait_ge(raw_in[p], 16 * (s.g0 // 2) + 16 + 16 * b)
                wait_up(act, half_done, 2 * g - 3 + f)
                nc.scalar.activation(w_hi[:, p, HALF * f:HALF * f + w], raw[:, p, w * f:w * (f + 1)], ACT.Copy)\
                    .then_inc(hi_ready, 1)

            def sum_products(m):
                for c in range(2):
                    act.wait_ge(mod_mul, 2 * m + c + 1)
                    nc.scalar.activation(modprod[:, c, :], modprod[:, c, :], ACT.Copy,
                                         accum_out=modcol[:, 0, bass.ds(2 * m + c, 1)]).then_inc(mod_done, 1)

            def mods(s, b):
                if s is first and b == 0:
                    for m in range(4, N_FIRST):
                        sum_products(m)
                for q in range(s.mods):
                    sum_products(s.m0 + s.mods * b + q)

            for v in (1, 0):
                act.wait_ge(vec_in[v], 16)
                nc.scalar.activation(cact[:, v, :], cact[:, v, :], ACT.Silu).then_inc(c_ready, 1)
            act.wait_ge(setup_in[0], 16)
            lam = pcol("lru_lam", 0, RC)
            link(nc.scalar.activation(small[:, 0, :], lam, ACT.Abs))
            nc.scalar.activation(small[:, 1, :], small[:, 0, :], ACT.Exp, scale=-1.0).then_inc(c_ready, 1)
            for m in range(4):
                sum_products(m)
            for g, f in ((0, 0), (0, 1), (1, 0)):
                split_hi((first, 0, g), f)

            def do_norm(n):
                i, x = n["i"], res[n["x"]]
                if i == 0:
                    act.wait_ge(setup_in[2], 16)
                if n["first_x"]:
                    act.wait_ge(setup_in[3], 16)
                    act.wait_ge(vec_in[2], 16)
                    nc.scalar.activation(cact[:, 1, :], cact[:, 1, :], ACT.Silu).then_inc(c_ready, 1)
                if not n["fused"]:
                    wait_up(act, updated, n["x0"])
                    wait_up(act, hn_lo, DC * n["ih"])
                    wait_up(act, norm_out, DC * n["outs"])
                    for k in range(DC):
                        nc.scalar.activation(nsq[:, k, :], x[:, k, :], ACT.Square).then_inc(sq_ready, 1)
                act.preload_act_table_set("sqrt_and_others")
                act.wait_ge(ms_ready, i + 1)
                nc.scalar.activation(nrm[:, 1, :], nrm[:, 0, :], ACT.Sqrt).then_inc(std_ready, 1)
                if n["dest"] == "h":
                    for k in range(DC):
                        act.wait_ge(norm_ready, DC * n["ih"] + k + 1)
                        nc.scalar.activation(h_hi[:, k, :], nsq[:, k, :], ACT.Identity, bias=cols[:, 1, k:k + 1])\
                            .then_inc(hn_hi, 1)

            def do_glu(s):
                def body(b, is_first, last):
                    for p in range(2):
                        g, e = s.g0 + 2 * b + p, s.e0 + 2 * b + p
                        prepare(split_hi, s, b, p, last)
                        act.wait_ge(half_done, 2 * g + 2)
                        wait_up(act, glu_mul, e - 1)
                        nc.scalar.activation(scr[:, p, 0, :], pb[p][:, 1, 0:T], ACT.Sigmoid).then_inc(glu_sig, 1)
                    mods(s, b)
                sweep(act, s, body)

            def do_q(s):
                r = s.arg
                def body(b, is_first, last):
                    for p in range(2):
                        g, e = s.g0 + 2 * b + p, s.e0 + 2 * b + p
                        j = 2 * (2 * b + p)
                        prepare(split_hi, s, b, p, last)
                        act.wait_ge(half_done, 2 * g + 2)
                        if r["rope"]:
                            wait_up(act, q_roped, e - 1)
                            o = scr[:, p, :, :]
                        else:
                            o = dst[r["dst"]][:, j:j + 2, :]
                        nc.scalar.activation(o, pb[p][:, :, 0:T], ACT.Copy, scale=r["scale"])\
                            .then_inc(r_copied if r["rope"] else q_copied, 1)
                    mods(s, b)
                sweep(act, s, body)

            def do_v(s):
                def body(b, is_first, last):
                    for p in range(2):
                        g = s.g0 + 2 * b + p
                        j = 256 * (2 * b + p)
                        prepare(split_hi, s, b, p, last)
                        act.wait_ge(half_done, 2 * g + 2)
                        nc.scalar.activation(dst[s.arg["dst"]][:, :, j:j + 256], pb[p][:, :, 0:T], ACT.Copy)\
                            .then_inc(v_copied, 1)
                    mods(s, b)
                sweep(act, s, body)

            def load_bias(l, hd):
                nc.scalar.dma_start(bias[:, hd % 2, :, :], a["rel_bias"][l, hd]).then_inc(bias_in[hd % 2], 16)

            def do_gate(s):
                n = s.arg
                i, l, is_ctx = n["i"], n["l"], n["ctx"]
                a0, keys = NA_H * i, 256 if is_ctx else 512
                if not is_ctx:
                    wait_up(act, att_max, a0)
                    load_bias(l, 0)
                    load_bias(l, 1)
                for h in range(NA_H + 2):
                    if h < NA_H:
                        act.wait_ge(att_max, a0 + h + 1)
                        if not is_ctx and h + 2 < NA_H:
                            load_bias(l, h + 2)
                        for t in range(2):
                            ins = nc.scalar.activation(att_p[:, h % 2, t, 0:keys], att_p[:, h % 2, t, 0:keys], ACT.Exp,
                                                       bias=small[:, 4 + h % 2, t:t + 1],
                                                       accum_out=small[:, 6 + h % 2, t:t + 1])
                        ins.then_inc(att_exp, 1)
                    if 1 <= h <= NA_H:
                        j, k = h - 1, h - 1
                        prepare(split_hi, s, j // 2, j % 2, j // 2 == s.bodies - 1)
                        act.wait_ge(att_t, a0 + k + 1)
                        wait_up(act, att_o, a0 + k - 1)
                        nk = keys // P
                        nc.scalar.activation(
                            att_pt[:, k % 2, 0:nk, :].rearrange("p k (t q) -> p t k q", t=2),
                            ps_t[:, :, 0:keys].rearrange("p t (k q) -> p t k q", q=P), ACT.Copy).then_inc(att_tc, 1)
                        act.wait_ge(half_done, 2 * (s.g0 + j) + 2)
                        nc.scalar.activation(gates[:, :, j, :], pb[j % 2][:, 0, :].rearrange("p (c t) -> p c t", c=2),
                                             ACT.Copy).then_inc(gate_copied, 1)
                    if h >= 2:
                        k = h - 2
                        r = HD * (k % 2)
                        act.wait_ge(att_o, a0 + k + 1)
                        nc.scalar.activation(e_hi[r:r + HD, CONV_C + k // 2, :], ps_o[r:r + HD, k % 2, 0:T],
                                             ACT.Copy).then_inc(att_hi, 1)
                    if h >= 2 and h % 2 == 0:
                        mods(s, h // 2 - 1)
                    if h == LN_AT:
                        for k in range(2):
                            act.wait_ge(ln_centred, 2 * i + k + 1)
                            nc.scalar.activation(ln_y[:, 2 * k:2 * k + 2, :], cy[:, 2 * k:2 * k + 2, :], ACT.Square)\
                                .then_inc(ln_sq, 1)
                    if h == LN_AT + 1:
                        act.wait_ge(ln_ms, i + 1)
                        nc.scalar.activation(ln_r[:, 1, :], ln_r[:, 0, :], ACT.Sqrt).then_inc(ln_std, 1)
                for k in range(CONV_C):
                    act.wait_ge(ln_scaled, CONV_C * i + k + 1)
                    link(nc.scalar.activation(ln_y[:, k, :], cy[:, k, :], ACT.Silu, bias=pcol(f"ln_b{l}", k),
                                              scale=pcol(f"ln_g{l}", k)))
                    nc.scalar.activation(e_hi[:, k, :], ln_y[:, k, :], ACT.Copy).then_inc(ln_hi, 1)
                for f in range(4):
                    nc.scalar.activation(gates[:, :, 2 * f:2 * f + 2, :], gates[:, :, 2 * f:2 * f + 2, :],
                                         ACT.Sigmoid).then_inc(gm_sig, 1)

            def do_merge(s):
                def body(b, is_first, last):
                    for p in range(2):
                        prepare(split_hi, s, b, p, last)
                        for f in range(2):
                            k = 2 * (2 * b + p) + f
                            act.wait_ge(gm_sum, 2 * s.e0 + k + 1)
                            nc.scalar.activation(e_hi[:, 8 + k, :], scr2[:, 0, f, :], ACT.Copy).then_inc(gm_hi, 1)
                    mods(s, b)
                sweep(act, s, body)

            def do_residual(s):
                x = res[s.arg["x"]]
                n = 2 if s.kind == "out" else 1

                def body(b, is_first, last):
                    for p in range(2):
                        prepare(split_hi, s, b, p, last)
                        if s.norm_i is not None:
                            for q in range(n):
                                k = n * (2 * b + p) + q
                                act.wait_ge(updated, s.x0 + k + 1)
                                nc.scalar.activation(nsq[:, k, :], x[:, k, :], ACT.Square).then_inc(sq_ready, 1)
                    mods(s, b)
                sweep(act, s, body)

            def do_upa(s):
                l = s.arg["l"]
                taps, fb = pview(f"ffn_w{l}", 3), pview(f"ffn_b{l}", 1)

                def step(b, p, last, has_tail):
                    j = 2 * b + p
                    g, e = s.g0 + j, s.e0 + j
                    prepare(split_hi, s, b, p, last)
                    if has_tail:
                        act.wait_ge(up_tap, 4 * e)
                        nc.scalar.activation(scr[:, 1 - p, 1, :], scr[:, 1 - p, 1, :], ACT.Silu).then_inc(up_silu, 1)
                    act.wait_ge(half_done, 2 * g + 2)
                    wait_up(act, up_lo, e - 1)
                    nc.scalar.activation(scr[:, p, 0, :], pb[p][:, 0, 0:T], ACT.Identity,
                                         bias=fb[:, j, :], scale=taps[:, j, 1:2])
                    nc.scalar.activation(scr[:, p, 1, :], pb[p][:, 1, 0:T], ACT.Identity,
                                         bias=fb[:, FC + j, :], scale=taps[:, FC + j, 1:2]).then_inc(up_lin, 1)
                    if has_tail:
                        act.wait_ge(up_mul, e)
                        nc.scalar.activation(e_hi[:, j - 1, :], scr[:, 1 - p, 0, :], ACT.Copy).then_inc(up_hi, 1)

                def body(b, is_first, last):
                    step(b, 0, last, not is_first)
                    step(b, 1, last, True)
                    mods(s, b)
                sweep(act, s, body)
                e = s.e0 + FC
                act.wait_ge(up_tap, 4 * e)
                nc.scalar.activation(scr[:, 1, 1, :], scr[:, 1, 1, :], ACT.Silu).then_inc(up_silu, 1)
                act.wait_ge(up_mul, e)
                nc.scalar.activation(e_hi[:, FC - 1, :], scr[:, 1, 0, :], ACT.Copy).then_inc(up_hi, 1)

            def do_upb(s):
                def step(b, p, last, has_tail):
                    j = 2 * b + p
                    g, e = s.g0 + j, s.e0 + j
                    prepare(split_hi, s, b, p, last)
                    if has_tail:
                        act.wait_ge(upb_mul, e)
                        nc.scalar.activation(e_hi[:, j - 1, :], scr[:, 1 - p, 1, :], ACT.Copy).then_inc(upb_hi, 1)
                    act.wait_ge(half_done, 2 * g + 2)
                    nc.scalar.activation(scr[:, p, 0, :], pb[p][:, 0, 0:T], ACT.Silu).then_inc(upb_silu, 1)

                def body(b, is_first, last):
                    step(b, 0, last, not is_first)
                    step(b, 1, last, True)
                    mods(s, b)
                sweep(act, s, body)
                act.wait_ge(upb_mul, s.e0 + FC)
                nc.scalar.activation(e_hi[:, FC - 1, :], scr[:, 1, 1, :], ACT.Copy).then_inc(upb_hi, 1)

            def do_stick(n):
                act.preload_act_table_set("natural_log_exp_and_others")
                for h in range(SB_H + 2):
                    if h < SB_H:
                        act.wait_ge(st_z, h + 1)
                        z, w = pb[0][:, h % 2, 0:384], sb_z[:, h % 2, 0, :]
                        wait_up(act, st_sp, 3 * (h - 1))
                        if h >= 2:
                            act.wait_ge(st_r, h - 1)
                        link(nc.scalar.activation(w, z, ACT.Abs))
                        link(nc.scalar.activation(w, w, ACT.Exp, scale=-1.0))
                        nc.scalar.activation(w, w, ACT.Ln, bias=1.0).then_inc(st_ln, 1)
                    if 1 <= h <= SB_H:
                        k = h - 1
                        act.wait_ge(st_v, k + 1)
                        nc.scalar.activation(sb_z[:, k % 2, 2, :], sb_z[:, k % 2, 1, :], ACT.Exp).then_inc(st_w, 1)
                    if h >= 2:
                        k = h - 2
                        r = HD * (k % 2)
                        act.wait_ge(st_o, k + 1)
                        nc.scalar.activation(e_hi[r:r + HD, k // 2, :], ps_o[r:r + HD, k % 2, 0:T],
                                             ACT.Copy).then_inc(st_hi, 1)

            def do_lin(s):
                w = pview("lru_w", 4)

                def step(b, p, last, has_tail):
                    j = 2 * b + p
                    g, e = s.g0 + j, s.e0 + j
                    prepare(split_hi, s, b, p, last)
                    act.wait_ge(half_done, 2 * g + 2)
                    nc.scalar.activation(l_gate[:, j, :], pb[p][:, 0, 0:T], ACT.Gelu_apprx_tanh)
                    nc.scalar.activation(l_x[:, j, :], pb[p][:, 1, 0:T], ACT.Identity,
                                         bias=pview("lru_b", 1)[:, j, :], scale=w[:, j, 3:4]).then_inc(lin_lin, 1)
                    if has_tail:
                        act.wait_ge(lin_tap, 3 * e)
                        nc.scalar.activation(e_hi[:, j - 1, :], l_x[:, j - 1, :], ACT.Copy).then_inc(lin_hi, 1)

                def body(b, is_first, last):
                    step(b, 0, last, not is_first)
                    step(b, 1, last, True)
                sweep(act, s, body)
                act.wait_ge(lin_tap, 3 * RC)
                nc.scalar.activation(e_hi[:, RC - 1, :], l_x[:, RC - 1, :], ACT.Copy).then_inc(lin_hi, 1)

            def do_lgate(s):
                def body(b, is_first, last):
                    for p in range(2):
                        j = 2 * b + p
                        prepare(split_hi, s, b, p, last)
                        act.wait_ge(half_done, 2 * (s.g0 + j) + 2)
                        nc.scalar.activation(l_r[:, j, :], pb[p][:, 0, 0:T], ACT.Sigmoid, bias=pcol("lru_br", j))
                        nc.scalar.activation(l_i[:, j, :], pb[p][:, 1, 0:T], ACT.Sigmoid, bias=pcol("lru_bi", j))\
                            .then_inc(lru_gates, 1)
                sweep(act, s, body)

            def do_lru(n):
                act.wait_ge(lru_gates, RC)
                for j in range(RC):
                    nc.scalar.activation(l_t[:, j, :], l_r[:, j, :], ACT.Tanh, scale=small[:, 2, j:j + 1])
                    ins = nc.scalar.activation(l_r[:, j, :], l_r[:, j, :], ACT.Exp, scale=small[:, 3, j:j + 1])
                ins.then_inc(lru_sq, 1)
                act.wait_ge(lru_y, 1)
                nc.scalar.activation(l_t, l_t, ACT.Sqrt).then_inc(lru_root, 1)
                act.wait_ge(lru_y, 2)
                nc.scalar.activation(e_hi[:, 0:RC, :], l_gate, ACT.Copy).then_inc(lru_hi, 1)

            kinds = {"glu": do_glu, "q": do_q, "qr": do_q, "v": do_v, "gate": do_gate, "merge": do_merge, "out": do_residual,
                     "down": do_residual,
                     "upa": do_upa, "upb": do_upb, "lin": do_lin, "lgate": do_lgate}
            others = {"norm": do_norm, "stick": do_stick, "lru": do_lru}
            for what, s in plan:
                kinds[s.kind](s) if what == "slabs" else others[what](s)

        @block.vector
        def _(dve):
            chain = [0]

            def link(ins):
                chain[0] += 1
                ins.then_inc(dve_chain, 1)
                dve.wait_ge(dve_chain, chain[0])

            def split_lo(nx, f):
                if nx is None:
                    return
                s, b, p = nx
                g, w = s.g0 + 2 * b + p, s.width[p] // 2
                at = slice(HALF * f, HALF * f + w)
                dve.wait_ge(hi_ready, 2 * g + f + 1)
                nc.vector.tensor_tensor(w_lo[:, p, at], raw[:, p, w * f:w * (f + 1)], w_hi[:, p, at].bitcast(F32),
                                        ALU.subtract).then_inc(lo_ready, 1)

            def mod_ctx(m, tile, arrived):
                for c in range(2):
                    if arrived is not None:
                        dve.wait_ge(mod_in[c], arrived)
                    wait_up(dve, mod_ctx_done, 2 * m + c)
                    ins = nc.vector.scalar_tensor_tensor(out=unused, in0=tile[:, c, :], scalar=1.0, in1=cact[:, 1, :],
                                                         op0=ALU.mult, op1=ALU.mult,
                                                         accum_out=modcol[:, 1, bass.ds(2 * m + c, 1)])
                    ins.then_inc(mod_ctx_done, 1)

            def mods(s, b):
                for q in range(s.mods):
                    if s.m0 + q < N_DOUBLE:
                        m = s.m0 + s.mods * b + q
                        mod_ctx(m, modraw, 16 * (m - N_FIRST + 1))

            def pad_edges():
                link(nc.vector.memset(u_pad[:, :, 0:PAD], 0.0))
                link(nc.vector.memset(u_pad[:, :, PAD + T:UW], 0.0))

            dve.wait_ge(c_ready, 1)
            for m in range(N_FIRST):
                dve.wait_ge(first_in[m], 16)
                mod_ctx(m, mod_first[m % 6], None)
            dve.wait_ge(c_ready, 3)
            e_, u_, v_, p_ = small[:, 1, :], small[:, 2, :], small[:, 3, :], small[:, 0, :]
            link(nc.vector.tensor_scalar(v_, e_, 2.0, None, ALU.add))
            link(nc.vector.reciprocal(u_, v_))
            link(nc.vector.tensor_tensor(u_, u_, e_, ALU.mult))
            link(nc.vector.tensor_tensor(v_, u_, u_, ALU.mult))
            link(nc.vector.memset(p_, 1.0 / (2 * SERIES + 1)))
            for k in range(SERIES - 1, -1, -1):
                link(nc.vector.tensor_tensor(p_, p_, v_, ALU.mult))
                link(nc.vector.tensor_scalar(p_, p_, 1.0 / (2 * k + 1), None, ALU.add))
            link(nc.vector.scalar_tensor_tensor(out=p_, in0=p_, scalar=2.0, in1=u_, op0=ALU.mult, op1=ALU.mult))
            link(nc.vector.tensor_scalar(u_, pcol("lru_lam", 0, RC), -1.0, 0.0, ALU.mult, ALU.max))
            link(nc.vector.tensor_tensor(p_, p_, u_, ALU.add))
            link(nc.vector.tensor_scalar(small[:, 2, :], p_, 8.0, None, ALU.mult))
            link(nc.vector.tensor_scalar(small[:, 3, :], p_, -8.0, None, ALU.mult))
            for g, f in ((0, 0), (0, 1), (1, 0)):
                split_lo((first, 0, g), f)

            def mod_vector(r, v, out, plus):
                if r["kind"] == "a":
                    base, bcol, w = 48 * r["l"], pcol(f"b_ada{r['l']}", 8 * v, 8), 1 if r["x"] == "ctx" else 0
                else:
                    base, bcol, w = 96 + 72 * r["l"], pcol(f"mod_b{r['l']}", 8 * v, 8), 0
                dve.wait_ge(mod_ctx_done if w else mod_done, 2 * r["need"])
                src = modcol[:, w, base + 8 * v:base + 8 * v + 8]
                link(nc.vector.scalar_tensor_tensor(out=cols[:, out, :], in0=src, scalar=plus, in1=bcol,
                                                    op0=ALU.add, op1=ALU.add))

            def newton_rsqrt(ms, std, t, r):
                link(nc.vector.reciprocal(r, std))
                link(nc.vector.tensor_tensor(t, ms, r, ALU.mult))
                link(nc.vector.tensor_tensor(t, t, r, ALU.mult))
                link(nc.vector.tensor_scalar(t, t, -0.5, 1.5, ALU.mult, ALU.add))
                link(nc.vector.tensor_tensor(r, r, t, ALU.mult))

            def do_norm(n):
                i, x, kind, l, v = n["i"], res[n["x"]], n["kind"], n["l"], n["v"]
                if kind in ("a", "b"):
                    mod_vector(n, v, 1, 0.0)
                    mod_vector(n, v + 1, 0, 1.0)
                    gain = {("a", 0): pcol(f"norm1{l}", 0, 8), ("a", 3): pcol(f"norm2{l}", 0, 8)}[(kind, v)] \
                        if kind == "a" else pcol(f"norm_b{l}", 8 * (v // 3), 8)
                    link(nc.vector.tensor_tensor(cols[:, 0, :], cols[:, 0, :], gain, ALU.mult))
                dve.wait_ge(sum_ready, i + 1)
                wait_up(dve, updated, n["x0"])
                nc.vector.tensor_scalar(nrm[:, 0, :], ps_t[:, 0, 0:T], 1.0 / D, EPS, ALU.mult, ALU.add)\
                    .then_inc(ms_ready, 1)
                dve.wait_ge(std_ready, i + 1)
                newton_rsqrt(nrm[:, 0, :], nrm[:, 1, :], nrm[:, 2, :], nrm[:, 3, :])
                if n["dest"] != "h":
                    for k in range(DC):
                        o = x[:, k, :] if n["dest"] == "x" else nsq[:, k, :]
                        nc.vector.scalar_tensor_tensor(out=o, in0=x[:, k, :], scalar=pcol(f"final_{kind[1]}", k),
                                                       in1=nrm[:, 3, :], op0=ALU.mult, op1=ALU.mult)\
                            .then_inc(norm_out, 1)
                    return
                for k in range(DC + 2):
                    if k < DC:
                        nc.vector.scalar_tensor_tensor(out=nsq[:, k, :], in0=x[:, k, :], scalar=cols[:, 0, k:k + 1],
                                                       in1=nrm[:, 3, :], op0=ALU.mult, op1=ALU.mult)\
                            .then_inc(norm_ready, 1)
                    if k >= 2:
                        q = k - 2
                        dve.wait_ge(hn_hi, DC * n["ih"] + q + 1)
                        nc.vector.scalar_tensor_tensor(out=h_lo[:, q, :], in0=nsq[:, q, :], scalar=cols[:, 1, q:q + 1],
                                                       in1=h_hi[:, q, :].bitcast(F32), op0=ALU.add,
                                                       op1=ALU.subtract).then_inc(hn_lo, 1)

            def do_glu(s):
                pad_edges()
                def body(b, is_first, last):
                    for p in range(2):
                        j = 2 * b + p
                        prepare(split_lo, s, b, p, last)
                        dve.wait_ge(glu_sig, s.e0 + j + 1)
                        nc.vector.tensor_tensor(u_pad[:, j, PAD:PAD + T], pb[p][:, 0, 0:T], scr[:, p, 0, :], ALU.mult)\
                            .then_inc(glu_mul, 1)
                    mods(s, b)
                sweep(dve, s, body)

            conv_n = CONV_C * CONV_K

            def conv_piece(piece, i):
                l, k0, _ = piece
                n0, n1 = conv_n * k0 // CONV_PIECES, conv_n * (k0 + 1) // CONV_PIECES
                w = pview(f"conv_w{l}", CONV_K)
                base = conv_n * i
                if k0 == 0:
                    dve.wait_ge(glu_mul, 4 * (i + 1))
                for n in range(n0, n1):
                    t, j = n // CONV_C, n % CONV_C
                    o, u = cy[:, j, :], u_pad[:, j, t:t + T]
                    if t == 0:
                        ins = nc.vector.tensor_scalar(o, u, w[:, j, 0:1], pcol(f"conv_b{l}", j), ALU.mult, ALU.add)
                    else:
                        dve.wait_ge(conv_tap, base + n - CONV_C + 1)
                        ins = nc.vector.scalar_tensor_tensor(out=o, in0=u, scalar=w[:, j, t:t + 1], in1=o,
                                                             op0=ALU.mult, op1=ALU.add)
                    ins.then_inc(conv_tap, 1)

            conv_i = [0]

            def do_q(s):
                r = s.arg
                def body(b, is_first, last):
                    for p in range(2):
                        j = 2 * (2 * b + p)
                        prepare(split_lo, s, b, p, last)
                        if r["rope"]:
                            dve.wait_ge(r_copied, s.e0 + 2 * b + p + 1)
                            q_in, q_sw, o = scr[:, p, :, :], scr2[:, p, :, :], dst[r["dst"]][:, j:j + 2, :]
                            both = lambda name: table(name).unsqueeze(1).broadcast_to([P, 2, T])
                            link(nc.vector.stream_shuffle(q_sw, q_in, [(k + 16) % 32 for k in range(32)]))
                            link(nc.vector.tensor_tensor(o, q_in, both("cos"), ALU.mult))
                            link(nc.vector.tensor_tensor(q_sw, q_sw, both("sin"), ALU.mult))
                            nc.vector.tensor_tensor(o, o, q_sw, ALU.add).then_inc(q_roped, 1)
                        if r["conv"]:
                            conv_piece((r["conv"][0], r["conv"][1] + p, 0), conv_i[0])
                    mods(s, b)
                sweep(dve, s, body)

            def do_v(s):
                def body(b, is_first, last):
                    for p in range(2):
                        prepare(split_lo, s, b, p, last)
                        if s.arg["conv"]:
                            conv_piece((s.arg["conv"][0], s.arg["conv"][1] + p, 0), conv_i[0])
                    mods(s, b)
                sweep(dve, s, body)
                if s.arg["conv"]:
                    conv_i[0] += 1

            def do_gate(s):
                n_ = s.arg
                i, l, is_ctx = n_["i"], n_["l"], n_["ctx"]
                a0, keys, width = NA_H * i, 256 if is_ctx else 512, CONV_C * P
                for h in range(NA_H + 2):
                    if h < NA_H:
                        dve.wait_ge(att_s, a0 + h + 1)
                        wait_up(dve, att_t, a0 + h - 1)
                        for t in range(2):
                            if not is_ctx:
                                if t == 0:
                                    dve.wait_ge(bias_in[h % 2], 16 * (NA_H // 2 * n_["n_bias"] + h // 2 + 1))
                                nc.vector.tensor_tensor(att_p[:, h % 2, t, 0:256], pb[t][:, 1, 0:256],
                                                        bias[:, h % 2, t, :], ALU.add)
                            ins = nc.vector.tensor_copy(att_p[:, h % 2, t, keys - 256:keys],
                                                        pb[t][:, 1, keys - 256:keys])
                        link(ins)
                        link(nc.vector.tensor_reduce(small[:, 4 + h % 2, 2:4], att_p[:, h % 2, :, 0:keys], AXX, ALU.max))
                        nc.vector.tensor_scalar(small[:, 4 + h % 2, 0:2], small[:, 4 + h % 2, 2:4], -1.0, None,
                                                ALU.mult).then_inc(att_max, 1)
                    if 1 <= h <= NA_H:
                        j = h - 1
                        prepare(split_lo, s, j // 2, j % 2, j // 2 == s.bodies - 1)
                    if h < NA_H:
                        dve.wait_ge(att_exp, a0 + h + 1)
                        link(nc.vector.reciprocal(small[:, 6 + h % 2, 2:4], small[:, 6 + h % 2, 0:2]))
                        for t in range(2):
                            ins = nc.vector.tensor_scalar(diag[:, h % 2, t, :], table("ident"),
                                                          small[:, 6 + h % 2, 2 + t:3 + t], None, ALU.mult)
                        ins.then_inc(att_diag, 1)
                    if 1 <= h < LN_AT:
                        conv_piece((l, 5 + h, 0), i)
                    if h >= 2:
                        k = h - 2
                        r = HD * (k % 2)
                        dve.wait_ge(att_hi, a0 + k + 1)
                        nc.vector.tensor_tensor(e_lo[r:r + HD, CONV_C + k // 2, :], ps_o[r:r + HD, k % 2, 0:T],
                                                e_hi[r:r + HD, CONV_C + k // 2, :].bitcast(F32), ALU.subtract)\
                            .then_inc(att_lo, 1)
                    if h == LN_AT:
                        dve.wait_ge(ln_sum, i + 1)
                        dve.wait_ge(conv_tap, conv_n * (i + 1))
                        link(nc.vector.tensor_scalar(ln_r[:, 4, :], ps_o[:, 0, T:2 * T], 1.0 / width, None, ALU.mult))
                        mean = ln_r[:, 4:5, :].broadcast_to([P, 2, T])
                        for k in range(2):
                            nc.vector.tensor_tensor(cy[:, 2 * k:2 * k + 2, :], cy[:, 2 * k:2 * k + 2, :], mean,
                                                    ALU.subtract).then_inc(ln_centred, 1)
                    if h == LN_AT + 1:
                        dve.wait_ge(ln_var, i + 1)
                        nc.vector.tensor_scalar(ln_r[:, 0, :], ps_o[:, 1, T:2 * T], 1.0 / width, EPS, ALU.mult, ALU.add)\
                            .then_inc(ln_ms, 1)
                    if h == LN_AT + 2:
                        dve.wait_ge(ln_std, i + 1)
                        dve.wait_ge(ln_centred, 2 * (i + 1))
                        newton_rsqrt(ln_r[:, 0, :], ln_r[:, 1, :], ln_r[:, 2, :], ln_r[:, 3, :])
                        for k in range(CONV_C):
                            nc.vector.tensor_tensor(cy[:, k, :], cy[:, k, :], ln_r[:, 3, :], ALU.mult)\
                                .then_inc(ln_scaled, 1)
                    if h % 2 == 0 and h >= 2:
                        mods(s, h // 2 - 1)
                for k in range(CONV_C):
                    dve.wait_ge(ln_hi, CONV_C * i + k + 1)
                    nc.vector.tensor_tensor(e_lo[:, k, :], ln_y[:, k, :], e_hi[:, k, :].bitcast(F32), ALU.subtract)\
                        .then_inc(ln_lo, 1)

            def do_merge(s):
                def body(b, is_first, last):
                    for p in range(2):
                        j = 2 * b + p
                        g = s.g0 + j
                        prepare(split_lo, s, b, p, last)
                        for f in range(2):
                            k = 2 * j + f
                            dve.wait_ge(half_done, 2 * g + f + 1)
                            dve.wait_ge(gm_sig, s.e0 + j + 1)
                            wait_up(dve, gm_hi, 2 * s.e0 + k - 1)
                            nc.vector.tensor_tensor(scr[:, f, :, :], pb[p][:, f, :].rearrange("p (c t) -> p c t", c=2),
                                                    gates[:, :, k, :], ALU.mult).then_inc(gm_mul, 1)
                            dve.wait_ge(gm_mul, 2 * s.e0 + k + 1)
                            nc.vector.tensor_tensor(scr2[:, 0, f, :], scr[:, f, 0, :], scr[:, f, 1, :], ALU.add)\
                                .then_inc(gm_sum, 1)
                        for f in range(2):
                            k = 2 * j + f
                            dve.wait_ge(gm_hi, 2 * s.e0 + k + 1)
                            nc.vector.tensor_tensor(e_lo[:, 8 + k, :], scr2[:, 0, f, :], e_hi[:, 8 + k, :].bitcast(F32),
                                                    ALU.subtract).then_inc(gm_lo, 1)
                    mods(s, b)
                sweep(dve, s, body)

            def gate_columns(r, x0):
                half = r.get("half")
                wait_up(dve, updated, x0)
                mod_vector(r, r["v"], 2, 0.0 if r["kind"] == "a" else 1.0)
                if half:
                    link(nc.vector.tensor_scalar(cols[:, 2, :], cols[:, 2, :], 0.5, None, ALU.mult))

            def do_out(s):
                r = s.arg
                x = res[r["x"]]
                gate_columns(r, s.x0)

                def body(b, is_first, last):
                    for p in range(2):
                        g = s.g0 + 2 * b + p
                        prepare(split_lo, s, b, p, last)
                        dve.wait_ge(half_done, 2 * g + 2)
                        for q in range(2):
                            k = 2 * (2 * b + p) + q
                            nc.vector.scalar_tensor_tensor(out=x[:, k, :], in0=pb[p][:, q, 0:T],
                                                           scalar=cols[:, 2, k:k + 1], in1=x[:, k, :],
                                                           op0=ALU.mult, op1=ALU.add).then_inc(updated, 1)
                    mods(s, b)
                sweep(dve, s, body)

            def do_down(s):
                r = s.arg
                x = res[r["x"]]
                if r["part"] != 1:
                    gate_columns(r, s.x0)
                gate = cols[:, 2, :].unsqueeze(2)
                def body(b, is_first, last):
                    for p in range(2):
                        j = 2 * b + p
                        prepare(split_lo, s, b, p, last)
                        dve.wait_ge(half_done, 2 * (s.g0 + j) + 2)
                        if r["part"] == 1:
                            dve.wait_ge(updated, s.x0 - 8 + j + 1)
                        nc.vector.scalar_tensor_tensor(out=x[:, j, :], in0=pb[p][:, 0, 0:T], scalar=gate[:, j, :],
                                                       in1=x[:, j, :], op0=ALU.mult, op1=ALU.add)\
                            .then_inc(updated, 1)
                    mods(s, b)
                sweep(dve, s, body)

            def do_upa(s):
                taps = pview(f"ffn_w{s.arg['l']}", 3)

                def tail_mul(e, q):
                    dve.wait_ge(up_silu, e)
                    nc.vector.tensor_tensor(scr[:, q, 0, :], scr[:, q, 0, :], scr[:, q, 1, :], ALU.mult)\
                        .then_inc(up_mul, 1)

                def tail_lo(e, q, j):
                    dve.wait_ge(up_hi, e)
                    nc.vector.tensor_tensor(e_lo[:, j, :], scr[:, q, 0, :], e_hi[:, j, :].bitcast(F32), ALU.subtract)\
                        .then_inc(up_lo, 1)

                def step(b, p, last, has_tail):
                    j = 2 * b + p
                    e = s.e0 + j
                    prepare(split_lo, s, b, p, last)
                    if has_tail:
                        tail_mul(e, 1 - p)
                    dve.wait_ge(up_lin, e + 1)
                    for n, (q, left) in enumerate(((0, 1), (1, 1), (0, 0), (1, 0))):
                        o = scr[:, p, q, 1:T] if left else scr[:, p, q, 0:T - 1]
                        i_ = pb[p][:, q, 0:T - 1] if left else pb[p][:, q, 1:T]
                        if n >= 2:
                            dve.wait_ge(up_tap, 4 * e + n - 1)
                        nc.vector.scalar_tensor_tensor(out=o, in0=i_, scalar=taps[:, FC * q + j, 0:1] if left else
                                                       taps[:, FC * q + j, 2:3], in1=o, op0=ALU.mult, op1=ALU.add)\
                            .then_inc(up_tap, 1)
                    if has_tail:
                        tail_lo(e, 1 - p, j - 1)

                def body(b, is_first, last):
                    step(b, 0, last, not is_first)
                    step(b, 1, last, True)
                    mods(s, b)
                sweep(dve, s, body)
                tail_mul(s.e0 + FC, 1)
                tail_lo(s.e0 + FC, 1, FC - 1)

            def do_upb(s):
                def tail_lo(e, q, j):
                    dve.wait_ge(upb_hi, e)
                    nc.vector.tensor_tensor(e_lo[:, j, :], scr[:, q, 1, :], e_hi[:, j, :].bitcast(F32), ALU.subtract)\
                        .then_inc(upb_lo, 1)

                def step(b, p, last, has_tail):
                    j = 2 * b + p
                    e = s.e0 + j
                    prepare(split_lo, s, b, p, last)
                    if has_tail:
                        tail_lo(e, 1 - p, j - 1)
                    dve.wait_ge(upb_silu, e + 1)
                    nc.vector.tensor_tensor(scr[:, p, 1, :], pb[p][:, 1, 0:T], scr[:, p, 0, :], ALU.mult)\
                        .then_inc(upb_mul, 1)

                def body(b, is_first, last):
                    step(b, 0, last, not is_first)
                    step(b, 1, last, True)
                    mods(s, b)
                sweep(dve, s, body)
                tail_lo(s.e0 + FC, 1, FC - 1)

            def do_stick(n):
                dve.wait_ge(masks_in, 16)
                for h in range(SB_H + 2):
                    if 1 <= h <= SB_H:
                        k = h - 1
                        dve.wait_ge(st_r, k + 1)
                        nc.vector.tensor_tensor(sb_z[:, k % 2, 1, :], pb[1][:, k % 2, 0:384], sb_z[:, k % 2, 1, :],
                                                ALU.add).then_inc(st_v, 1)
                    if h < SB_H:
                        z, w, zm = pb[0][:, h % 2, 0:384], sb_z[:, h % 2, 0, :], sb_z[:, h % 2, 1, :]
                        dve.wait_ge(st_ln, h + 1)
                        wait_up(dve, st_w, h - 1)
                        nc.vector.tensor_tensor(zm, z, masks[:, 384:768], ALU.add).then_inc(st_sp, 1)
                        nc.vector.scalar_tensor_tensor(out=w, in0=z, scalar=0.0, in1=w, op0=ALU.max, op1=ALU.add)\
                            .then_inc(st_sp, 1)
                        dve.wait_ge(st_sp, 3 * h + 2)
                        nc.vector.tensor_tensor(w, w, masks[:, 0:384], ALU.mult).then_inc(st_sp, 1)
                    if h >= 2:
                        k = h - 2
                        r = HD * (k % 2)
                        dve.wait_ge(st_hi, k + 1)
                        nc.vector.tensor_tensor(e_lo[r:r + HD, k // 2, :], ps_o[r:r + HD, k % 2, 0:T],
                                                e_hi[r:r + HD, k // 2, :].bitcast(F32), ALU.subtract)\
                            .then_inc(st_lo, 1)

            def do_lin(s):
                w = pview("lru_w", 4)

                def tail_lo(j):
                    dve.wait_ge(lin_hi, j + 1)
                    nc.vector.tensor_tensor(e_lo[:, j, :], l_x[:, j, :], e_hi[:, j, :].bitcast(F32), ALU.subtract)\
                        .then_inc(lin_lo, 1)

                def step(b, p, last, has_tail):
                    j = 2 * b + p
                    prepare(split_lo, s, b, p, last)
                    dve.wait_ge(lin_lin, j + 1)
                    for k in range(1, 4):
                        if k > 1:
                            dve.wait_ge(lin_tap, 3 * j + k - 1)
                        nc.vector.scalar_tensor_tensor(out=l_x[:, j, k:T], in0=pb[p][:, 1, 0:T - k],
                                                       scalar=w[:, j, 3 - k:4 - k], in1=l_x[:, j, k:T],
                                                       op0=ALU.mult, op1=ALU.add).then_inc(lin_tap, 1)
                    if has_tail:
                        tail_lo(j - 1)

                def body(b, is_first, last):
                    step(b, 0, last, not is_first)
                    step(b, 1, last, True)
                    mods(s, b)
                sweep(dve, s, body)
                tail_lo(RC - 1)

            def do_lgate(s):
                def body(b, is_first, last):
                    for p in range(2):
                        prepare(split_lo, s, b, p, last)
                sweep(dve, s, body)

            def do_lru(n):
                dve.wait_ge(lru_sq, 1)
                link(nc.vector.tensor_tensor(l_i, l_i, l_x, ALU.mult))
                link(nc.vector.tensor_tensor(l_x, l_r, l_r, ALU.mult))
                nc.vector.scalar_tensor_tensor(out=l_t, in0=l_x, scalar=1.0, in1=l_t, op0=ALU.add, op1=ALU.mult)\
                    .then_inc(lru_y, 1)
                dve.wait_ge(lru_root, 1)
                link(nc.vector.tensor_tensor(l_i, l_i, l_t, ALU.mult))
                for j in range(RC):
                    ins = nc.vector.tensor_tensor_scan(l_x[:, j, :], l_r[:, j, :], l_i[:, j, :], 0.0,
                                                       ALU.mult, ALU.add)
                link(ins)
                nc.vector.tensor_tensor(l_gate, l_gate, l_x, ALU.mult).then_inc(lru_y, 1)
                dve.wait_ge(lru_hi, 1)
                nc.vector.tensor_tensor(e_lo[:, 0:RC, :], l_gate, e_hi[:, 0:RC, :].bitcast(F32), ALU.subtract)\
                    .then_inc(lru_lo, 1)

            kinds = {"glu": do_glu, "q": do_q, "qr": do_q, "v": do_v, "gate": do_gate, "merge": do_merge, "out": do_out, "down": do_down,
                     "upa": do_upa, "upb": do_upb, "lin": do_lin, "lgate": do_lgate}
            others = {"norm": do_norm, "stick": do_stick, "lru": do_lru}
            for what, s in plan:
                kinds[s.kind](s) if what == "slabs" else others[what](s)

        @block.tensor
        def _(pe):
            ones = table("ones")
            pe.wait_ge(setup_in[1], 16)

            def mm3(out, l, r, start, stop):
                nc.tensor.matmul(out, l[0], r[0], start=start, stop=False)
                nc.tensor.matmul(out, l[0], r[1], start=False, stop=False)
                return nc.tensor.matmul(out, l[1], r[0], start=False, stop=stop)

            def sum_squares(i, k, start, stop):
                pe.wait_ge(sq_ready, DC * i + k + 1)
                return nc.tensor.matmul(ps_t[:, 0, 0:T], ones, nsq[:, k, :], start=start, stop=stop)

            def freed(s, b, p):
                j = 2 * b + p
                return {"glu": lambda: (glu_mul, s.e0 + j + 1), "q": lambda: (q_copied, s.e0 + j + 1),
                        "qr": lambda: (r_copied, s.e0 + j + 1), "v": lambda: (v_copied, s.e0 + j + 1),
                        "gate": lambda: (gate_copied, s.e0 + j + 1), "merge": lambda: (gm_mul, 2 * (s.e0 + j + 1)),
                        "out": lambda: (updated, s.x0 + 2 * j + 2), "down": lambda: (updated, s.x0 + j + 1),
                        "upa": lambda: (up_tap, 4 * (s.e0 + j + 1)), "upb": lambda: (upb_mul, s.e0 + j + 1),
                        "lin": lambda: (lin_tap, 3 * (j + 1)), "lgate": lambda: (lru_gates, j + 1)}[s.kind]()

            def chunks(s, b, p, f):
                part = (s.arg or {}).get("part") if isinstance(s.arg, dict) else None
                if s.kind == "merge":
                    return [(e_hi[:, k, :], e_lo[:, k, :]) for k in range(DC)]
                if s.kind == "out":
                    at = 8 if s.arg["kind"] == "a" else 0
                    return [(e_hi[:, at + k, :], e_lo[:, at + k, :]) for k in range(DC)]
                if s.kind == "down":
                    at, n = FA if part == 1 else 0, s.kc // 2
                    return [(e_hi[:, at + k, :], e_lo[:, at + k, :]) for k in range(n * f, n * (f + 1))]
                if s.kind == "lgate":
                    return [(e_hi[:, 2 * b + p, :], e_lo[:, 2 * b + p, :])]
                return [(h_hi[:, k, :], h_lo[:, k, :]) for k in range(DC)]

            def operands_ready(s, b, p, is_first):
                if s.kind == "merge" and p == 0 and is_first:
                    pe.wait_ge(ln_lo, s.e0 + 4)
                    pe.wait_ge(att_lo, NA_H * (s.e0 // 4 + 1))
                if s.kind == "out" and p == 0 and is_first:
                    if s.arg["kind"] == "a":
                        pe.wait_ge(gm_lo, gm_done[id(s)])
                    else:
                        pe.wait_ge(st_lo, SB_H)
                if s.kind == "down" and p == 0 and is_first:
                    part = s.arg["part"]
                    if part == 2:
                        pe.wait_ge(lru_lo, 1)
                    else:
                        pe.wait_ge(up_lo if s.arg["kind"] == "a" else upb_lo, up_done[id(s)] + (FA if part == 0 else FC))
                if s.kind == "lgate":
                    pe.wait_ge(lin_lo, 2 * b + p + 1)

            gm_done, up_done, had, prior = {}, {}, {}, {}
            before = None
            for what, s in plan:
                if what == "slabs":
                    gm_done[id(s)] = 2 * had.get("merge", 0)
                    up_done[id(s)] = had.get("upa" if isinstance(s.arg, dict) and s.arg.get("kind") == "a" else "upb",
                                             0) - FC
                    had[s.kind] = s.e0 + 2 * s.bodies
                    prior[id(s)] = before
                    before = s

            def free_banks(s, b, p, is_first):
                if not is_first:
                    pe.wait_ge(*freed(s, b - 1, p))
                elif prior[id(s)] is not None:
                    q = prior[id(s)]
                    pe.wait_ge(*freed(q, q.bodies - 1, p))

            def half(s, b, p, f, is_first):
                g = s.g0 + 2 * b + p
                pe.wait_ge(lo_ready, 2 * g + f + 1)
                if s.kind == "v":
                    for k in range(4 * f, 4 * f + 4):
                        for t in range(2):
                            x = [h[:, k, t * P:(t + 1) * P] for h in (h_hi, h_lo)]
                            w = [v[:, p, 256 * k:256 * (k + 1)] for v in (w_hi, w_lo)]
                            ins = mm3(pb[p][:, t, 0:256], x, w, k == 0, k == DC - 1)
                else:
                    xs = chunks(s, b, p, f)
                    n, one = len(xs), s.kind == "down"
                    for k, x in enumerate(xs):
                        if s.after is not None and is_first and p == 0 and f == 0:
                            pe.wait_ge(hn_lo, DC * s.after["ih"] + k + 1)
                        c = HALF * f + P * k
                        if s.kind == "merge":
                            o, start, stop = pb[p][:, f, T * (k // 4):T * (k // 4 + 1)], k % 4 == 0, k % 4 == 3
                        elif s.kind == "gate":
                            o, start, stop = pb[p][:, 0, T * f:T * (f + 1)], k == 0, k == n - 1
                        else:
                            o = pb[p][:, 0 if one else f, 0:T]
                            start, stop = k == 0 and not (one and f), k == n - 1 and not (one and not f)
                        ins = mm3(o, (w_hi[:, p, c:c + P], w_lo[:, p, c:c + P]), x, start, stop)
                ins.then_inc(half_done, 1)

            def do_slabs(s):
                def body(b, is_first, last):
                    for p in range(2):
                        operands_ready(s, b, p, is_first)
                        free_banks(s, b, p, is_first)
                        for f in range(2):
                            half(s, b, p, f, is_first)
                        if s.norm_i is not None and not (is_first and p == 0):
                            n = 2 if s.kind == "out" else 1
                            for q in range(n):
                                sum_squares(s.norm_i, n * (2 * b + p - 1) + q, is_first and p == 1 and q == 0, False)
                sweep(pe, s, body)

            def do_norm(n):
                left = DC if not n["fused"] else (2 if n["fused"] == "out" else 1)
                for k in range(DC - left, DC):
                    ins = sum_squares(n["i"], k, k == 0, k == DC - 1)
                ins.then_inc(sum_ready, 1)

            def do_gate(s):
                n_ = s.arg
                i, is_ctx, a0 = n_["i"], n_["ctx"], NA_H * n_["i"]
                nk = 2 if is_ctx else 4
                pe.wait_ge(q_copied, n_["had"]["q"])
                if not is_ctx:
                    pe.wait_ge(q_roped, n_["had"]["qr"])
                pe.wait_ge(v_copied, n_["had"]["v"])
                for h in range(NA_H + 2):
                    j, k1, k2 = h - 1, h - 1, h - 2
                    slab = 1 <= h <= NA_H
                    if h < NA_H:
                        wait_up(pe, att_max, a0 + h)
                        c, r = h // 2, HD * (h % 2)
                        for t in range(2):
                            q = dst["q"][r:r + HD, c, t * P:(t + 1) * P]
                            keys = [dst["kc"]] if is_ctx else [dst["k"], dst["kc"]]
                            for n_k, k_ in enumerate(keys):
                                ins = nc.tensor.matmul(pb[t][:, 1, T * n_k:T * (n_k + 1)], q, k_[r:r + HD, c, :],
                                                       start=True, stop=True)
                        ins.then_inc(att_s, 1)
                    if slab:
                        free_banks(s, j // 2, j % 2, j < 2)
                        half(s, j // 2, j % 2, 0, j < 2)
                        pe.wait_ge(att_diag, a0 + k1 + 1)
                        wait_up(pe, att_tc, a0 + k1)
                        for t in range(2):
                            for q in range(nk):
                                ins = nc.tensor.matmul(ps_t[:, t, q * P:(q + 1) * P],
                                                       att_p[:, k1 % 2, t, q * P:(q + 1) * P], diag[:, k1 % 2, t, :],
                                                       start=True, stop=True)
                        ins.then_inc(att_t, 1)
                    if h == LN_AT:
                        pe.wait_ge(conv_tap, CONV_C * CONV_K * (i + 1))
                        for k in range(CONV_C):
                            ins = nc.tensor.matmul(ps_o[:, 0, T:2 * T], ones, cy[:, k, :], start=k == 0,
                                                   stop=k == CONV_C - 1)
                        ins.then_inc(ln_sum, 1)
                    if h == LN_AT + 1:
                        for k in range(CONV_C):
                            pe.wait_ge(ln_sq, 2 * i + k // 2 + 1)
                            ins = nc.tensor.matmul(ps_o[:, 1, T:2 * T], ones, ln_y[:, k, :], start=k == 0,
                                                   stop=k == CONV_C - 1)
                        ins.then_inc(ln_var, 1)
                    if slab:
                        half(s, j // 2, j % 2, 1, j < 2)
                    if h >= 2:
                        c, r = k2 // 2, HD * (k2 % 2)
                        pe.wait_ge(att_tc, a0 + k2 + 1)
                        wait_up(pe, att_lo, a0 + k2 - 1)
                        for q in range(nk):
                            v = (dst["vc"] if is_ctx else dst["v"])[:, q, HD * k2:HD * (k2 + 1)] if q < 2 else \
                                dst["vc"][:, q - 2, HD * k2:HD * (k2 + 1)]
                            ins = nc.tensor.matmul(ps_o[r:r + HD, k2 % 2, 0:T], v, att_pt[:, k2 % 2, q, :],
                                                   start=q == 0, stop=q == nk - 1)
                        ins.then_inc(att_o, 1)
                pe.wait_ge(att_max, a0 + NA_H)

            def do_stick(n):
                pe.wait_ge(q_copied, n["had"]["q"])
                pe.wait_ge(v_copied, n["had"]["v"])
                for h in range(SB_H + 2):
                    if h < SB_H:
                        wait_up(pe, st_sp, 3 * (h - 1))
                        c, r = h // 2, HD * (h % 2)
                        q, k_ = dst["sbq"][r:r + HD, c, :], dst["sbk"][r:r + HD, c, :]
                        nc.tensor.matmul(pb[0][:, h % 2, 0:256], k_[:, 0:P], q, start=True, stop=True)
                        nc.tensor.matmul(pb[0][:, h % 2, 256:384], k_[:, P:T], q[:, P:T], start=True, stop=True)\
                            .then_inc(st_z, 1)
                    if 1 <= h <= SB_H:
                        k = h - 1
                        pe.wait_ge(st_sp, 3 * (k + 1))
                        wait_up(pe, st_v, k - 1)
                        w, o = sb_z[:, k % 2, 0, :], pb[1][:, k % 2, :]
                        nc.tensor.matmul(o[:, 256:384], table("ntri"), w[:, 256:384], start=True, stop=True)
                        nc.tensor.matmul(o[:, 0:128], table("ntri"), w[:, 0:128], start=True, stop=True)
                        nc.tensor.matmul(o[:, 128:256], table("ntri"), w[:, 128:256], start=True, stop=False)
                        nc.tensor.matmul(o[:, 128:256], table("nones"), w[:, 256:384], start=False, stop=True)\
                            .then_inc(st_r, 1)
                    if h >= 2:
                        k = h - 2
                        r = HD * (k % 2)
                        pe.wait_ge(st_w, k + 1)
                        wait_up(pe, st_lo, k - 1)
                        v, w = dst["sbv"], sb_z[:, k % 2, 2, :]
                        v0, v1 = v[:, 0, HD * k:HD * (k + 1)], v[:, 1, HD * k:HD * (k + 1)]
                        o = ps_o[r:r + HD, k % 2, :]
                        nc.tensor.matmul(o[:, 0:128], v0, w[:, 0:128], start=True, stop=True)
                        nc.tensor.matmul(o[:, 128:256], v0, w[:, 128:256], start=True, stop=False)
                        nc.tensor.matmul(o[:, 128:256], v1, w[:, 256:384], start=False, stop=True)\
                            .then_inc(st_o, 1)

            for what, s in plan:
                if what == "slabs":
                    (do_gate if s.kind == "gate" else do_slabs)(s)
                elif what != "lru":
                    {"norm": do_norm, "stick": do_stick}[what](s)
    return nc


def _pack(w, order, group):
    k, n = w.shape[0] // P, w.shape[1] // P
    t = w.reshape(k, P, n, P).transpose(2, 1, 0, 3)[np.asarray(order)]
    t = t.reshape(len(order) // group, group, P, k * P).transpose(0, 2, 1, 3)
    return np.ascontiguousarray(t.reshape(len(order) // group, P, group * k * P))


def _pack_wide(w):
    k, n = w.shape[0] // P, w.shape[1] // 256
    return np.ascontiguousarray(w.reshape(k, P, n, 256).transpose(2, 1, 0, 3).reshape(n, P, k * 256))


def _pack_rows(w):
    return np.ascontiguousarray(w.T.reshape(-1, 2, P, w.shape[0]).transpose(0, 2, 1, 3).reshape(-1, P, 2 * w.shape[0]))


def _pairs(n, off):
    return [c for j in range(n) for c in (j, off + j)]


def _rows(v):
    return v.reshape(-1, P).T


def _taps(w):
    return w.T.reshape(-1, P, w.shape[0]).transpose(1, 0, 2).reshape(P, -1)


def _fmajor(x):
    return np.ascontiguousarray(x.T.reshape(DC, P, T).transpose(1, 0, 2))


def _tables():
    t = np.zeros((P, NTAB), np.float32)

    def put(name, v):
        at, n = TCOL[name]
        t[:, at:at + n] = v

    put("ident", np.eye(P))
    put("ones", 1.0)
    s = np.arange(P)
    put("ntri", -(s[:, None] >= s[None, :]).astype(np.float32))
    put("nones", -1.0)
    half = HD // 2
    freq = (np.float32(10000.0) ** (-np.arange(0, half, 2, dtype=np.float32) / np.float32(half))).astype(np.float32)
    tok = np.arange(T)
    pos = np.stack([tok // GRID_W, tok % GRID_W]).astype(np.float32)
    f = np.arange(P) % HD
    ang = pos[f // half] * freq[f % (half // 2)][:, None]
    put("cos", np.cos(ang))
    put("sin", np.sin(ang) * np.where(f % half < half // 2, -1.0, 1.0)[:, None])
    return t


def _masks():
    q = np.concatenate([np.arange(T), np.arange(P)])
    keep = (np.arange(P)[:, None] < q[None, :]).astype(np.float32)
    return np.concatenate([keep, np.where(keep > 0, 0.0, -1e30).astype(np.float32)], 1)


def _relative_bias(rpb):
    t = np.arange(T)
    row, col = t // GRID_W, t % GRID_W
    start = np.clip(col - 8, 0, GRID_W - 16)
    inside = (col[None, :] >= start[:, None]) & (col[None, :] < start[:, None] + 16)
    dr = row[None, :] - row[:, None] + 7
    dc = np.where(inside, col[None, :] - col[:, None] + 15, 0)
    b = np.where(inside[None], rpb[:, dr, dc], np.float32(-1e30))
    return np.ascontiguousarray(b.reshape(NA_H, 2, P, T).transpose(0, 2, 1, 3))


def arrays_of(i):
    a = {"x": _fmajor(i["x"][0]), "ctx": _fmajor(i["ctx"][0])}
    par = np.zeros((P, NPARAM), np.float32)

    def put(name, v):
        at, n = PCOL[name]
        par[:, at:at + n] = v

    mod, bias = [], []
    for l in range(2):
        put(f"b_ada{l}", _rows(i["b_ada"][l]))
        put(f"norm1{l}", _rows(i["norm1_g"][l]))
        put(f"norm2{l}", _rows(i["norm2_g"][l]))
        put(f"conv_w{l}", _taps(i["conv_dw"][l]))
        put(f"conv_b{l}", _rows(i["conv_dw_b"][l]))
        put(f"ln_g{l}", _rows(i["conv_ln_g"][l]))
        put(f"ln_b{l}", _rows(i["conv_ln_b"][l]))
        put(f"ffn_w{l}", _taps(i["ffn_dw"][l]))
        put(f"ffn_b{l}", _rows(i["ffn_dw_b"][l]))
        put(f"mod_b{l}", _rows(i["mod_b_2"][l]))
        put(f"norm_b{l}", _rows(i["norm_g_2"][l].reshape(-1)))
        w = i["w_in"][l]
        a[f"w_glu{l}"] = _pack(w, _pairs(4, 4), 2)
        a[f"w_q{l}"] = _pack(w, range(8, 12), 2)
        a[f"w_k{l}"] = _pack(w, range(12, 16), 2)
        a[f"w_v{l}"] = _pack_wide(w[:, 2048:2560])
        a[f"w_gate{l}"] = _pack(w[:, 2560:], _pairs(8, 8), 2)
        a[f"w_merge{l}"] = np.concatenate([_pack(i["w_conv_out"][l], range(8), 1),
                                           _pack(i["w_na_out"][l], range(8), 1)], 2)\
            .reshape(4, 2, P, HALF).transpose(0, 2, 1, 3).reshape(4, P, SLAB)
        a[f"w_out{l}"] = _pack(i["w_out"][l], range(8), 2)
        a[f"w_up{l}"] = _pack(i["w_up"][l], _pairs(FC, FC), 2)
        a[f"w_down{l}0"] = _pack(i["w_down"][l][:FA * P], range(8), 1)
        a[f"w_down{l}1"] = _pack(i["w_down"][l][FA * P:], range(8), 1)
        for f in range(2):
            a[f"w_gu{l}{f}"] = _pack(i["ffn_w_gu_2"][l, f], _pairs(FC, FC), 2)
            a[f"w_dn{l}{f}0"] = _pack(i["ffn_w_down_2"][l, f][:FA * P], range(8), 1)
            a[f"w_dn{l}{f}1"] = _pack(i["ffn_w_down_2"][l, f][FA * P:], range(8), 1)
        bias.append(_relative_bias(i["na_rpb"][l]))
    a["w_mod"] = np.concatenate([_pack_rows(i["w_ada"][l]) for l in range(2)]
                                + [_pack_rows(i["mod_w_2"][l]) for l in range(2)], 0)
    vectors = np.concatenate([i["c"][0], i["c_ctx"], i["c_2"][0]])
    a["vectors"] = np.ascontiguousarray(np.broadcast_to(vectors, (P, 3 * D)))
    qkv = i["sb_w_qkv_2"][0]
    a["w_sbq"] = _pack(qkv, range(8), 2)
    a["w_sbk"] = _pack(qkv, range(8, 16), 2)
    a["w_sbv"] = _pack_wide(qkv[:, 2048:])
    a["w_sbo"] = _pack(i["sb_w_o_2"][0], range(8), 2)
    a["w_lin"] = _pack(i["lru_w_in_2"][0], _pairs(RC, RC), 2)
    a["w_lg"] = np.concatenate([i["lru_w_r_2"][0], i["lru_w_i_2"][0]], 2)
    a["w_lout"] = _pack(i["lru_w_out_2"][0], range(8), 1)
    put("final_a", _rows(i["final_norm_g"]))
    put("final_b", _rows(i["final_norm_g_2"]))
    put("lru_w", _taps(i["lru_conv_w_2"][0]))
    put("lru_b", _rows(i["lru_conv_b_2"][0]))
    put("lru_br", _rows(i["lru_b_r_2"][0]))
    put("lru_bi", _rows(i["lru_b_i_2"][0]))
    put("lru_lam", _rows(i["lru_lambda_2"][0]))
    a["params"], a["tables"], a["rel_bias"] = par, _tables(), np.stack(bias)
    a["masks"] = _masks()
    return a


def kernel(**inputs):
    import concourse.bacc as bacc
    from concourse.bass_utils import run_bass_kernel_spmd

    host = arrays_of({k: np.asarray(v) for k, v in inputs.items()})
    nc = bacc.Bacc("TRN2", target_bir_lowering=False, num_devices=1)
    aps = {k: nc.dram_tensor(f"in_{k}", v.shape, F32, kind="ExternalInput").ap() for k, v in host.items()}
    aps["y"] = nc.dram_tensor("y", (P, DC, T), F32, kind="ExternalOutput").ap()
    build(nc, aps)
    r = run_bass_kernel_spmd(nc, [{f"in_{k}": v for k, v in host.items()}], core_ids=[0])
    y = r.results[0]["y"]
    return np.ascontiguousarray(y.transpose(1, 0, 2).reshape(D, T).T).reshape(1, T, D)
```

```python
from contextlib import ExitStack
from dataclasses import dataclass

import numpy as np
import concourse.bass as bass
from concourse import mybir

P = 128
D = 1024
T = 256
DC = D // P
GRID_W = 64
CONV_C, CONV_K = 4, 31
PAD = CONV_K // 2
UW = T + 2 * PAD + 2
HD = 64
NA_H, NA_C = 8, 4
SB_H = 16
FC = 22
FA = 12
RC = 10
LRU_SLAB = (3, 2)
LRU_PARTS = (range(0, 6), range(6, RC))
SLAB = 16 * P
CONV_SLAB = 10
CONV_AT = np.cumsum([0] + [CONV_SLAB] * 6 + [8] + [8, 3] * 4 + [8]).tolist() + [CONV_K * CONV_C]
ADDS = DC - 2
LN_AT = 6
HALF = SLAB // 2
EPS = 1e-6
N_MOD_A, N_MOD_B = 6 * D // 256, 9 * D // 256
N_MOD = 2 * N_MOD_A + 2 * N_MOD_B
N_FIRST = 8
N_DOUBLE = N_MOD_A + 9
SERIES = 10

F32 = mybir.dt.float32
F32R = mybir.dt.float32r
ALU = mybir.AluOpType
ACT = mybir.ActivationFunctionType
RADD = bass.bass_isa.ReduceOp.add
AXX = mybir.AxisListType.X


def param_columns():
    at, n = {}, 0
    sizes = []
    for l in range(2):
        sizes += [(f"b_ada{l}", 48), (f"norm1{l}", 8), (f"norm2{l}", 8), (f"conv_w{l}", CONV_C * CONV_K),
                  (f"conv_b{l}", 4), (f"ln_g{l}", 4), (f"ln_b{l}", 4), (f"ffn_w{l}", 3 * 44), (f"ffn_b{l}", 44),
                  (f"mod_b{l}", 72), (f"norm_b{l}", 24)]
    sizes += [("final_a", 8), ("final_b", 8), ("lru_w", 40), ("lru_b", 10), ("lru_br", 10), ("lru_bi", 10),
              ("lru_lam", 10)]
    for name, k in sizes:
        at[name] = (n, k)
        n += k
    return at, n


PCOL, NPARAM = param_columns()
TCOL = {"ident": (0, 128), "ones": (128, 128), "ntri": (256, 128), "nones": (384, 128), "cos": (512, 256),
        "sin": (768, 256)}
NTAB = 1024
NMASK = 768


@dataclass
class Stage:
    kind: str
    src: tuple
    width: tuple
    bodies: int
    kc: int = 8
    arg: object = None
    mods: int = 0
    g0: int = 0
    m0: int = 0
    e0: int = 0
    x0: int = 0
    nxt: object = None
    norm_i: object = None
    fused_i: int = 0
    after: object = None


def build(nc, a):
    plan = []

    def stage(kind, src, width, bodies, **kw):
        src = src if isinstance(src, tuple) else (src, src)
        width = width if isinstance(width, tuple) else (width, width)
        plan.append(("slabs", Stage(kind, src, width, bodies, **kw)))

    def norm(x, kind, l, v, need, dest="h"):
        plan.append(("norm", dict(x=x, kind=kind, l=l, v=v, need=need, dest=dest)))

    def layer_a(l, x):
        dbl = l == 0 and x == "ctx"
        norm(x, "a", l, 0, l * N_MOD_A + 8)
        early = l == 0 and x == "ctx"
        stage("glu", a[f"w_glu{l}"], SLAB, 2, mods=1)
        rope = x == "x"
        qk = "qr" if rope else "q"
        stage(qk, a[f"w_q{l}"], SLAB, 1, mods=int(l == 0), arg=dict(dst="q", rope=rope, scale=HD ** -0.5, conv=(l, 0, 2)))
        stage(qk, a[f"w_k{l}"], SLAB, 1, mods=int(early), arg=dict(dst="k" if rope else "kc", rope=rope, scale=1.0, conv=(l, 2, 4)))
        stage("v", a[f"w_v{l}"], SLAB, 1, mods=int(early), arg=dict(dst="v" if rope else "vc", conv=(l, 4, 6), heads=NA_H))
        stage("gate", a[f"w_gate{l}"], SLAB, 4, mods=int(l == 0), arg=dict(l=l, ctx=x == "ctx"))
        stage("merge", a[f"w_merge{l}"], SLAB, 2, mods=1 + (l == 0))
        stage("out", a[f"w_out{l}"], SLAB, 2, mods=1 + (l == 0),
              arg=dict(x=x, kind="a", l=l, v=2, need=l * N_MOD_A + 12))
        norm(x, "a", l, 3, l * N_MOD_A + 20)
        stage("upa", a[f"w_up{l}"], SLAB, FC // 2, mods=l, arg=dict(l=l))
        for part in range(2):
            stage("down", a[f"w_down{l}{part}"], (FA, FC - FA)[part] * P, 4, kc=(FA, FC - FA)[part], mods=int(early),
                  arg=dict(x=x, kind="a", l=l, v=5, need=(l + 1) * N_MOD_A, part=part))

    def ffn_b(l, f, sub, mods=1):
        base = 2 * N_MOD_A + l * N_MOD_B + 12 * sub
        norm("x", "b", l, 3 * sub, base + 8)
        stage("upb", a[f"w_gu{l}{f}"], SLAB, FC // 2, mods=mods)
        for part in range(2):
            stage("down", a[f"w_dn{l}{f}{part}"], (FA, FC - FA)[part] * P, 4, kc=(FA, FC - FA)[part],
                  arg=dict(x="x", kind="b", l=l, v=3 * sub + 2, need=base + 12, part=part, half=True))

    layer_a(0, "ctx")
    layer_a(0, "x")
    norm("ctx", "a", 1, 0, N_MOD_A + 8)
    stage("q", a["w_k1"], SLAB, 1, mods=1, arg=dict(dst="kc", rope=False, scale=1.0, conv=None))
    stage("v", a["w_v1"], SLAB, 1, arg=dict(dst="vc", conv=None, heads=NA_H))
    layer_a(1, "x")
    norm("x", "fa", 0, 0, 0, dest="x")
    ffn_b(0, 0, 0)
    norm("x", "b", 0, 3, 2 * N_MOD_A + 20)
    stage("q", a["w_sbq"], SLAB, 2, mods=1, arg=dict(dst="sbq", rope=False, scale=HD ** -0.5, conv=None))
    stage("q", a["w_sbk"], SLAB, 2, mods=1, arg=dict(dst="sbk", rope=False, scale=1.0, conv=None))
    stage("v", a["w_sbv"], SLAB, 2, mods=1, arg=dict(dst="sbv", conv=None, heads=SB_H))
    plan.append(("stick", {}))
    stage("out", a["w_sbo"], SLAB, 2, mods=1, arg=dict(x="x", kind="b", l=0, v=5, need=2 * N_MOD_A + 24))
    ffn_b(0, 1, 2)
    ffn_b(1, 0, 0)
    norm("x", "b", 1, 3, 2 * N_MOD_A + N_MOD_B + 20)
    stage("lin", a["w_lin"], SLAB, RC // 2, mods=1)
    stage("lgate", (a["w_lg0"], a["w_lg1"]), tuple(2 * P * n for n in LRU_SLAB), RC // sum(LRU_SLAB))
    plan.append(("lru", {}))
    stage("down", a["w_lout"], RC * P, 4, kc=RC,
          arg=dict(x="x", kind="b", l=1, v=5, need=2 * N_MOD_A + N_MOD_B + 24, part=2))
    ffn_b(1, 1, 2, 0)
    norm("x", "fb", 0, 0, 0, dest="y")

    g = xn = 0
    n_out, last_entry, n_attn, n_fused = 0, None, 0, 0
    m = N_FIRST
    of_kind, seen, before, n_h, n_bias, had_x = {}, {}, None, 0, 0, False
    for what, s in plan:
        if what == "slabs":
            s.g0, s.m0, s.e0, s.x0 = g, m, of_kind.get(s.kind, 0), xn
            m += s.mods * s.bodies
            n = 2 * s.bodies
            g += n
            of_kind[s.kind] = s.e0 + n
            if s.kind == "gate":
                s.arg.update(i=n_attn, n_bias=n_bias, had=dict(of_kind))
                n_attn += 1
                n_bias += not s.arg["ctx"]
            if s.kind == "out":
                xn += 2 * n
            if s.kind == "down":
                xn += n
            if before is not None:
                before.nxt = s
            before = s
        else:
            if what == "stick":
                s["m0"] = m
                m += SB_H // 2
            s["i"] = seen.get(what, 0)
            seen[what] = s["i"] + 1
            s["x0"] = xn
            s["had"] = dict(of_kind)
            if what == "norm":
                s["ih"], s["outs"] = n_h, n_out
                n_out += s["dest"] != "h"
                what1, s1 = last_entry if last_entry else ("", None)
                s["fused"] = what1 == "slabs" and s1.kind in ("out", "down") and s1.arg["x"] == s["x"] and s1.kind
                s["before"] = s1 if s["fused"] else None
                if s["fused"]:
                    s1.norm_i, s1.fused_i = s["i"], n_fused
                    n_fused += 1
                    s["fused_i"] = s1.fused_i
                n_h += s["dest"] == "h"
                s["first_x"] = s["x"] == "x" and not had_x
                had_x = had_x or s["x"] == "x"
        if what == "slabs" and last_entry and last_entry[0] == "norm":
            s.after = last_entry[1]
        last_entry = (what, s)
    assert m == N_MOD, m
    first = next(s for what, s in plan if what == "slabs")

    with ExitStack() as ctx:
        def sb(name, shape, dt=F32):
            return ctx.enter_context(nc.sbuf_tensor(name, shape, dt))

        def sem(name):
            return ctx.enter_context(nc.semaphore(name))

        raw = sb("raw", [P, 2, SLAB])
        w_hi = sb("w_hi", [P, 2, SLAB], F32R)
        w_lo = sb("w_lo", [P, 2, SLAB], F32R)
        res = {"x": sb("x_res", [P, DC, T]), "ctx": sb("ctx_res", [P, DC, T])}
        h_hi = sb("h_hi", [P, DC, T], F32R)
        h_lo = sb("h_lo", [P, DC, T], F32R)
        e_at = -(-nc.sbuf_base // 32) * 32
        e_both = sb("e_both", [P, 2, FC, T], F32R)
        e_hi, e_lo = e_both[:, 0], e_both[:, 1]
        e_plain = nc.alloc_sbuf_tensor_at("e_plain", [P, 2, FC, T], F32, offset=e_at)
        modraw = sb("modraw", [P, 2, D])
        cact = sb("cact", [P, 2, D])
        modcol = sb("modcol", [P, 2, 2 * N_MOD])
        par = sb("par", [P, NPARAM])
        tab = sb("tab", [P, NTAB])
        cols = sb("cols", [P, 4, 8])
        small = sb("small", [P, 8, RC])
        arena = sb("arena", [P, 11392])
        bias = sb("bias", [P, 2, 2, 256])
        masks = bias[:].rearrange("p a b c -> p (a b c)")[:, 0:NMASK]

        def view(at, *shape):
            n = int(np.prod(shape))
            v = arena[:, at:at + n]
            if len(shape) == 2:
                return v.rearrange("p (b c) -> p b c", b=shape[0])
            if len(shape) == 3:
                return v.rearrange("p (b c d) -> p b c d", b=shape[0], c=shape[1])
            return v

        dst = {"q": view(0, NA_C, T), "k": view(1024, NA_C, T), "kc": view(3072, NA_C, T),
               "v": view(2048, 2, 512), "vc": view(4096, 2, 512),
               "sbq": view(0, DC, T), "sbk": view(2048, DC, T), "sbv": view(4096, 2, D)}
        u_pad = view(5120, CONV_C, UW)
        cy = view(5120 + CONV_C * UW, CONV_C, T)
        free0 = 5120 + CONV_C * (UW + T)
        att_p = view(free0, 2, 2, 512)
        att_pt = view(free0 + 2048, 2, 4, T)
        gates = e_plain[:, :, 8:16, :]
        ln_y = e_plain[:, 0, 16:20, :]
        ln_r = e_plain[:, 1, 16:21, :]
        diag = e_plain[:, 0, 20:22, :].rearrange("p a (t q) -> p a t q", t=2)
        scr = view(free0, 2, 2, T)
        scr2 = view(free0 + 1024, 2, 2, T)
        nsq = view(0, DC, T)
        nrm = view(2048, 4, T)
        sb_z = view(6144, 2, 3, 384)
        l_gate, l_x, l_r = (view(RC * T * k, RC, T) for k in range(3))
        l_i, l_t = e_plain[:, 0, RC:2 * RC, :], e_plain[:, 1, RC:2 * RC, :]
        assert free0 + 4096 <= 11392 and 3 * RC * T <= 11392 and 6144 + 2304 <= 11392
        mod_first = [e_plain[:, e, DC * k:DC * (k + 1), :].rearrange("p a b -> p (a b)")
                     .rearrange("p (c k) -> p c k", c=2) for e in range(2) for k in range(2)] \
            + [view(9216, 2, D), modraw[:]]
        unused = res["x"][:, 0:4, :].rearrange("p a b -> p (a b)")

        pb = [ctx.enter_context(nc.psum_tensor(f"bank_pair{k}", [P, 2, 512], F32)) for k in range(2)]
        ps_t = ctx.enter_context(nc.psum_tensor("ps_t", [P, 2, 512], F32))
        ps_o = ctx.enter_context(nc.psum_tensor("ps_o", [P, 2, 512], F32))

        def pcol(name, k=0, n=1):
            at = PCOL[name][0] + k
            return par[:, at:at + n]

        def pview(name, k):
            at, n = PCOL[name]
            return par[:, at:at + n].rearrange("p (c k) -> p c k", k=k)

        def table(name):
            at, n = TCOL[name]
            return tab[:, at:at + n]

        raw_in = [[sem(f"raw_in{p}{f}") for f in range(2)] for p in range(2)]
        hi_ready, lo_ready = sem("hi_ready"), sem("lo_ready")
        half_done = sem("half_done")
        setup_in = [sem(f"setup_in{k}") for k in range(4)]
        first_in = [sem(f"first_in{k}") for k in range(N_FIRST)]
        mod_in = [sem("mod_in0"), sem("mod_in1")]
        mod_done, mod_ctx_done = sem("mod_done"), sem("mod_ctx_done")
        vec_in = [sem(f"vec_in{k}") for k in range(3)]
        c_ready, masks_in, eps_set = sem("c_ready"), sem("masks_in"), sem("eps_set")
        dve_chain, act_chain = sem("dve_chain"), sem("act_chain")
        updated = sem("updated")
        sq_ready, sq_added, sum_ready, log_ready, std_ready = (
            sem(k) for k in ("sq_ready", "sq_added", "sum_ready", "log_ready", "std_ready"))
        norm_ready, hn_hi, hn_lo = sem("norm_ready"), sem("hn_hi"), sem("hn_lo")
        norm_out = sem("norm_out")
        glu_sig, glu_mul = sem("glu_sig"), sem("glu_mul")
        q_copied, r_copied, q_roped, v_copied = (sem(k) for k in ("q_copied", "r_copied", "q_roped", "v_copied"))
        conv_tap = sem("conv_tap")
        ln_sum, ln_centred, ln_sq, ln_var, ln_ms, ln_std = (sem(f"ln_{k}") for k in
                                                            ("sum", "centred", "sq", "var", "ms", "std"))
        ln_scaled, ln_hi, ln_lo = sem("ln_scaled"), sem("ln_hi"), sem("ln_lo")
        bias_in = [sem("bias_in0"), sem("bias_in1")]
        att_s, att_max, att_exp, att_diag = sem("att_s"), sem("att_max"), sem("att_exp"), sem("att_diag")
        att_t, att_tc, att_o, att_hi, att_lo = (sem(f"att_{k}") for k in ("t", "tc", "o", "hi", "lo"))
        gate_copied = sem("gate_copied")
        gm_sig, gm_mul, gm_sum, gm_hi, gm_lo = (sem(f"gm_{k}") for k in ("sig", "mul", "sum", "hi", "lo"))
        up_lin, up_tap, up_silu, up_mul, up_hi, up_lo = (sem(f"up_{k}") for k in
                                                         ("lin", "tap", "silu", "mul", "hi", "lo"))
        upb_silu, upb_mul, upb_hi, upb_lo = (sem(f"upb_{k}") for k in ("silu", "mul", "hi", "lo"))
        st_z, st_ln, st_sp, st_r, st_v, st_w, st_o, st_hi, st_lo = (
            sem(f"st_{k}") for k in ("z", "ln", "sp", "r", "v", "w", "o", "hi", "lo"))
        lin_lin, lin_tap, lin_hi, lin_lo = (sem(f"lin_{k}") for k in ("lin", "tap", "hi", "lo"))
        lru_gates, lru_exp, lru_sq, lru_root, lru_y, lru_hi, lru_lo = (
            sem(f"lru_{k}") for k in ("gates", "exp", "sq", "root", "y", "hi", "lo"))
        stored = sem("stored")

        block = ctx.enter_context(nc.Block())

        def sweep(eng, s, body):
            n = s.bodies
            if n <= 3:
                for b in range(n):
                    body(b, b == 0, b == n - 1)
            else:
                body(0, True, False)
                with eng.Fori(1, n - 1) as b:
                    body(b, False, False)
                body(n - 1, False, True)

        def following(s, b, p, last):
            if p == 0:
                return s, b, 1
            if last:
                return (s.nxt, 0, 0) if s.nxt is not None else None
            return s, b + 1, 0

        def after_next(s, b, p, last):
            if last:
                return (s.nxt, 0, p) if s.nxt is not None else None
            return s, b + 1, p

        def prepare(split, s, b, p, last):
            split(following(s, b, p, last), 1)
            split(after_next(s, b, p, last), 0)

        def late(n):
            return after_next(n["before"], n["before"].bodies - 1, 1, True)

        def gate_chunks(b, p):
            at = sum(LRU_SLAB) * b + sum(LRU_SLAB[:p])
            return range(at, at + LRU_SLAB[p])

        def gate_sum(p, f, k):
            tile = (pb[0], ps_t)[f] if p == 0 else pb[1]
            return tile[:, k // 2 if p == 0 else f, T * (k % 2):T * (k % 2 + 1)]

        def wait_up(eng, s, value):
            if not isinstance(value, int) or value > 0:
                eng.wait_ge(s, value)

        @block.sync
        def _(sp):
            sp.dma_start(cact[:, 1, :], a["vectors"][:, D:2 * D]).then_inc(vec_in[1], 16)
            for k in range(6):
                sp.dma_start(mod_first[k], a["w_mod"][k].rearrange("p (c k) -> p c k", c=2)).then_inc(first_in[k], 16)
                if k == 0:
                    sp.dma_start(cact[:, 0, :], a["vectors"][:, 0:D]).then_inc(vec_in[0], 16)
                if k == 1:
                    sp.dma_start(res["ctx"][:], a["ctx"]).then_inc(setup_in[2], 16)
                if k == 3:
                    sp.dma_start(tab[:], a["tables"]).then_inc(setup_in[1], 16)
                    sp.dma_start(par[:], a["params"]).then_inc(setup_in[0], 16)

            def load(s, b, p):
                g, w = s.g0 + 2 * b + p, s.width[p] // 2
                j = b if s.kind == "lgate" else 2 * b + p
                for f in range(2):
                    wait_up(sp, lo_ready, 2 * g - 3 + f)
                    sp.dma_start(raw[:, p, HALF * f:HALF * f + w], s.src[p][j, :, w * f:w * (f + 1)])\
                      .then_inc(raw_in[p][f], 16)

            for k in (6, 7):
                sp.wait_ge(mod_done, 2 * (k - 5))
                sp.dma_start(mod_first[k - 6], a["w_mod"][k].rearrange("p (c k) -> p c k", c=2))\
                  .then_inc(first_in[k], 16)
            load(first, 0, 0)
            load(first, 0, 1)
            for what, s in plan:
                if what == "norm" and s["kind"] == "fa":
                    sp.wait_ge(att_max, NA_H * n_attn)
                    sp.dma_start(masks, a["masks"]).then_inc(masks_in, 16)
                if what != "slabs":
                    continue

                def body(b, is_first, last, s=s):
                    for p in range(2):
                        if not (s is first and is_first):
                            load(s, b, p)
                sweep(sp, s, body)
            for f in range(2):
                sp.wait_ge(norm_out, DC + 4 * (f + 1))
                sp.dma_start(a["y"][:, 4 * f:4 * f + 4, :], nsq[:, 4 * f:4 * f + 4, :]).then_inc(stored, 16)
            sp.wait_ge(stored, 32)

        @block.gpsimd
        def _(pool):
            def load_mod(m, c, used):
                pool.wait_ge(mod_done, used)
                nc.gpsimd.dma_start(modraw[:, c, :], a["w_mod"][m, :, D * c:D * (c + 1)]).then_inc(mod_in[c], 16)

            for c in range(2):
                load_mod(N_FIRST, c, 2 * 5 + c + 1)
            with pool.Fori(N_FIRST + 1, N_DOUBLE) as m:
                for c in range(2):
                    load_mod(m, c, 2 * m - 1 + c)
            pool.wait_ge(mod_ctx_done, 2 * N_DOUBLE)
            nc.gpsimd.dma_start(res["x"][:], a["x"]).then_inc(setup_in[3], 16)
            nc.gpsimd.dma_start(cact[:, 1, :], a["vectors"][:, 2 * D:3 * D]).then_inc(vec_in[2], 16)
            with pool.Fori(N_DOUBLE, N_MOD) as m:
                for c in range(2):
                    load_mod(m, c, 2 * m - 1 + c)

        @block.scalar
        def _(act):
            chain = [0]

            def link(ins):
                chain[0] += 1
                ins.then_inc(act_chain, 1)
                act.wait_ge(act_chain, chain[0])

            def split_hi(nx, f):
                if nx is None:
                    return
                s, b, p = nx
                g, w = s.g0 + 2 * b + p, s.width[p] // 2
                act.wait_ge(raw_in[p][f], 16 * (s.g0 // 2) + 16 + 16 * b)
                wait_up(act, half_done, 2 * g - 3 + f)
                nc.scalar.activation(w_hi[:, p, HALF * f:HALF * f + w], raw[:, p, HALF * f:HALF * f + w], ACT.Copy)\
                    .then_inc(hi_ready, 1)

            for v in (1, 0):
                act.wait_ge(vec_in[v], 16)
                nc.scalar.activation(cact[:, v, :], cact[:, v, :], ACT.Silu).then_inc(c_ready, 1)
            act.wait_ge(setup_in[0], 16)
            lam = pcol("lru_lam", 0, RC)
            link(nc.scalar.activation(small[:, 0, :], lam, ACT.Abs))
            nc.scalar.activation(small[:, 1, :], small[:, 0, :], ACT.Exp, scale=-1.0).then_inc(c_ready, 1)
            for g, f in ((0, 0), (0, 1), (1, 0)):
                split_hi((first, 0, g), f)

            def do_norm(n):
                i, x = n["i"], res[n["x"]]
                if i == 0:
                    act.wait_ge(eps_set, 1)
                    act.wait_ge(setup_in[2], 16)
                if n["first_x"]:
                    act.wait_ge(setup_in[3], 16)
                if not n["fused"]:
                    wait_up(act, updated, n["x0"])
                    wait_up(act, hn_lo, DC * n["ih"])
                    wait_up(act, norm_out, DC * n["outs"])
                    for k in range(DC):
                        nc.scalar.activation(nsq[:, k, :], x[:, k, :], ACT.Square).then_inc(sq_ready, 1)
                if n["x"] == "x" and n["kind"] == "a" and (n["l"], n["v"]) == (0, 3):
                    act.wait_ge(vec_in[2], 16)
                    nc.scalar.activation(cact[:, 1, :], cact[:, 1, :], ACT.Silu).then_inc(c_ready, 1)
                if not n["fused"]:
                    act.preload_act_table_set("natural_log_exp_and_others")
                act.wait_ge(sum_ready, i + 1)
                nc.scalar.activation(nrm[:, 2, :], ps_t[:, 0, 0:T], ACT.Ln, bias=small[:, 0, 0:1], scale=1.0 / D)\
                    .then_inc(log_ready, 1)
                act.wait_ge(log_ready, i + 1)
                nc.scalar.activation(nrm[:, 1, :], nrm[:, 2, :], ACT.Exp, scale=-0.5).then_inc(std_ready, 1)
                if n["dest"] == "h":
                    for k in range(DC):
                        act.wait_ge(norm_ready, DC * n["ih"] + k + 1)
                        nc.scalar.activation(h_hi[:, k, :], nsq[:, k, :], ACT.Identity, bias=cols[:, 1, k:k + 1])\
                            .then_inc(hn_hi, 1)
                if n["before"] is not None:
                    split_hi(late(n), 0)

            def do_glu(s):
                def body(b, is_first, last):
                    for p in range(2):
                        g, e = s.g0 + 2 * b + p, s.e0 + 2 * b + p
                        prepare(split_hi, s, b, p, last)
                        act.wait_ge(half_done, 2 * g + 2)
                        wait_up(act, glu_mul, e - 1)
                        nc.scalar.activation(scr[:, p, 0, :], pb[p][:, 1, 0:T], ACT.Sigmoid).then_inc(glu_sig, 1)
                sweep(act, s, body)

            def do_q(s):
                r = s.arg
                def body(b, is_first, last):
                    for p in range(2):
                        g, e = s.g0 + 2 * b + p, s.e0 + 2 * b + p
                        j = 2 * (2 * b + p)
                        prepare(split_hi, s, b, p, last)
                        act.wait_ge(half_done, 2 * g + 2)
                        if r["rope"]:
                            wait_up(act, q_roped, e - 1)
                            o = scr[:, p, :, :]
                        else:
                            o = dst[r["dst"]][:, j:j + 2, :]
                        nc.scalar.activation(o, pb[p][:, :, 0:T], ACT.Copy, scale=r["scale"])\
                            .then_inc(r_copied if r["rope"] else q_copied, 1)
                sweep(act, s, body)

            def do_v(s):
                def body(b, is_first, last):
                    for p in range(2):
                        g = s.g0 + 2 * b + p
                        j = 256 * (2 * b + p)
                        prepare(split_hi, s, b, p, last)
                        act.wait_ge(half_done, 2 * g + 2)
                        nc.scalar.activation(dst[s.arg["dst"]][:, :, j:j + 256], pb[p][:, :, 0:T], ACT.Copy)\
                            .then_inc(v_copied, 1)
                sweep(act, s, body)

            def load_bias(l, hd):
                nc.scalar.dma_start(bias[:, hd % 2, :, :], a["rel_bias"][l, hd]).then_inc(bias_in[hd % 2], 16)

            def do_gate(s):
                n = s.arg
                i, l, is_ctx = n["i"], n["l"], n["ctx"]
                a0, keys = NA_H * i, 256 if is_ctx else 512
                act.preload_act_table_set("natural_log_exp_and_others")
                if not is_ctx:
                    wait_up(act, att_max, a0)
                    load_bias(l, 0)
                    load_bias(l, 1)
                for h in range(NA_H + 2):
                    if h < NA_H:
                        act.wait_ge(att_max, a0 + h + 1)
                        if not is_ctx and h + 2 < NA_H:
                            load_bias(l, h + 2)
                        for t in range(2):
                            ins = nc.scalar.activation(att_p[:, h % 2, t, 0:keys], att_p[:, h % 2, t, 0:keys], ACT.Exp,
                                                       bias=small[:, 4 + h % 2, t:t + 1],
                                                       accum_out=small[:, 6 + h % 2, t:t + 1])
                        ins.then_inc(att_exp, 1)
                    if 1 <= h <= NA_H:
                        j, k = h - 1, h - 1
                        prepare(split_hi, s, j // 2, j % 2, j // 2 == s.bodies - 1)
                        act.wait_ge(att_t, a0 + k + 1)
                        wait_up(act, att_o, a0 + k - 1)
                        nk = keys // P
                        nc.scalar.activation(
                            att_pt[:, k % 2, 0:nk, :].rearrange("p k (t q) -> p t k q", t=2),
                            ps_t[:, :, 0:keys].rearrange("p t (k q) -> p t k q", q=P), ACT.Copy).then_inc(att_tc, 1)
                        act.wait_ge(half_done, 2 * (s.g0 + j) + 2)
                        nc.scalar.activation(gates[:, :, j, :], pb[j % 2][:, 0, :].rearrange("p (c t) -> p c t", c=2),
                                             ACT.Copy).then_inc(gate_copied, 1)
                    if h >= 2:
                        k = h - 2
                        r = HD * (k % 2)
                        act.wait_ge(att_o, a0 + k + 1)
                        nc.scalar.activation(e_hi[r:r + HD, CONV_C + k // 2, :], ps_o[r:r + HD, k % 2, 0:T],
                                             ACT.Copy).then_inc(att_hi, 1)
                    if h == LN_AT:
                        for k in range(2):
                            act.wait_ge(ln_centred, 2 * i + k + 1)
                            nc.scalar.activation(ln_y[:, 2 * k:2 * k + 2, :], cy[:, 2 * k:2 * k + 2, :], ACT.Square)\
                                .then_inc(ln_sq, 1)
                    if h == LN_AT + 1:
                        act.wait_ge(ln_ms, i + 1)
                        link(nc.scalar.activation(ln_r[:, 2, :], ln_r[:, 0, :], ACT.Ln))
                        nc.scalar.activation(ln_r[:, 1, :], ln_r[:, 2, :], ACT.Exp, scale=-0.5).then_inc(ln_std, 1)
                for k in range(CONV_C):
                    act.wait_ge(ln_scaled, CONV_C * i + k + 1)
                    link(nc.scalar.activation(ln_y[:, k, :], cy[:, k, :], ACT.Silu, bias=pcol(f"ln_b{l}", k),
                                              scale=pcol(f"ln_g{l}", k)))
                    nc.scalar.activation(e_hi[:, k, :], ln_y[:, k, :], ACT.Copy).then_inc(ln_hi, 1)
                for f in range(4):
                    nc.scalar.activation(gates[:, :, 2 * f:2 * f + 2, :], gates[:, :, 2 * f:2 * f + 2, :],
                                         ACT.Sigmoid).then_inc(gm_sig, 1)

            def do_merge(s):
                def body(b, is_first, last):
                    for p in range(2):
                        prepare(split_hi, s, b, p, last)
                        for f in range(2):
                            k = 2 * (2 * b + p) + f
                            act.wait_ge(gm_sum, 2 * s.e0 + k + 1)
                            nc.scalar.activation(e_hi[:, 8 + k, :], scr2[:, 0, f, :], ACT.Copy).then_inc(gm_hi, 1)
                sweep(act, s, body)

            def do_residual(s):
                x = res[s.arg["x"]]
                n = 2 if s.kind == "out" else 1

                def squares(j):
                    for q in range(n):
                        k = n * j + q
                        act.wait_ge(updated, s.x0 + k + 1)
                        nc.scalar.activation(nsq[:, k, :], x[:, k, :], ACT.Square).then_inc(sq_ready, 1)

                def body(b, is_first, last):
                    for p in range(2):
                        if s.norm_i is None:
                            prepare(split_hi, s, b, p, last)
                        elif last and p == 1:
                            squares(2 * b + p)
                            split_hi(following(s, b, p, last), 1)
                        else:
                            prepare(split_hi, s, b, p, last)
                            if last:
                                act.preload_act_table_set("natural_log_exp_and_others")
                            squares(2 * b + p)
                sweep(act, s, body)

            def do_upa(s):
                l = s.arg["l"]
                taps, fb = pview(f"ffn_w{l}", 3), pview(f"ffn_b{l}", 1)

                def step(b, p, last, has_tail):
                    j = 2 * b + p
                    g, e = s.g0 + j, s.e0 + j
                    prepare(split_hi, s, b, p, last)
                    if has_tail:
                        act.wait_ge(up_tap, 4 * e)
                        nc.scalar.activation(scr[:, 1 - p, 1, :], scr[:, 1 - p, 1, :], ACT.Silu).then_inc(up_silu, 1)
                    act.wait_ge(half_done, 2 * g + 2)
                    wait_up(act, up_lo, e - 1)
                    nc.scalar.activation(scr[:, p, 0, :], pb[p][:, 0, 0:T], ACT.Identity,
                                         bias=fb[:, j, :], scale=taps[:, j, 1:2])
                    nc.scalar.activation(scr[:, p, 1, :], pb[p][:, 1, 0:T], ACT.Identity,
                                         bias=fb[:, FC + j, :], scale=taps[:, FC + j, 1:2]).then_inc(up_lin, 1)
                    if has_tail:
                        act.wait_ge(up_mul, e)
                        nc.scalar.activation(e_hi[:, j - 1, :], scr[:, 1 - p, 0, :], ACT.Copy).then_inc(up_hi, 1)

                def body(b, is_first, last):
                    step(b, 0, last, not is_first)
                    step(b, 1, last, True)
                sweep(act, s, body)
                e = s.e0 + FC
                act.wait_ge(up_tap, 4 * e)
                nc.scalar.activation(scr[:, 1, 1, :], scr[:, 1, 1, :], ACT.Silu).then_inc(up_silu, 1)
                act.wait_ge(up_mul, e)
                nc.scalar.activation(e_hi[:, FC - 1, :], scr[:, 1, 0, :], ACT.Copy).then_inc(up_hi, 1)

            def do_upb(s):
                def step(b, p, last, has_tail):
                    j = 2 * b + p
                    g, e = s.g0 + j, s.e0 + j
                    prepare(split_hi, s, b, p, last)
                    if has_tail:
                        act.wait_ge(upb_mul, e)
                        nc.scalar.activation(e_hi[:, j - 1, :], scr[:, 1 - p, 1, :], ACT.Copy).then_inc(upb_hi, 1)
                    act.wait_ge(half_done, 2 * g + 2)
                    nc.scalar.activation(scr[:, p, 0, :], pb[p][:, 0, 0:T], ACT.Silu).then_inc(upb_silu, 1)

                def body(b, is_first, last):
                    step(b, 0, last, not is_first)
                    step(b, 1, last, True)
                sweep(act, s, body)
                act.wait_ge(upb_mul, s.e0 + FC)
                nc.scalar.activation(e_hi[:, FC - 1, :], scr[:, 1, 1, :], ACT.Copy).then_inc(upb_hi, 1)

            def do_stick(n):
                act.preload_act_table_set("natural_log_exp_and_others")
                for h in range(SB_H + 2):
                    if h < SB_H:
                        act.wait_ge(st_z, h + 1)
                        z, w = pb[0][:, h % 2, 0:384], sb_z[:, h % 2, 0, :]
                        wait_up(act, st_sp, 3 * (h - 1))
                        if h >= 2:
                            act.wait_ge(st_r, h - 1)
                        link(nc.scalar.activation(w, z, ACT.Abs))
                        link(nc.scalar.activation(w, w, ACT.Exp, scale=-1.0))
                        nc.scalar.activation(w, w, ACT.Ln, bias=1.0).then_inc(st_ln, 1)
                    if 1 <= h <= SB_H:
                        k = h - 1
                        act.wait_ge(st_v, k + 1)
                        nc.scalar.activation(sb_z[:, k % 2, 2, :], sb_z[:, k % 2, 1, :], ACT.Exp).then_inc(st_w, 1)
                    if h >= 2:
                        k = h - 2
                        r = HD * (k % 2)
                        act.wait_ge(st_o, k + 1)
                        nc.scalar.activation(e_hi[r:r + HD, k // 2, :], ps_o[r:r + HD, k % 2, 0:T],
                                             ACT.Copy).then_inc(st_hi, 1)

            def do_lin(s):
                w = pview("lru_w", 4)

                def step(b, p, last, has_tail):
                    j = 2 * b + p
                    g, e = s.g0 + j, s.e0 + j
                    prepare(split_hi, s, b, p, last)
                    act.wait_ge(half_done, 2 * g + 2)
                    nc.scalar.activation(l_gate[:, j, :], pb[p][:, 0, 0:T], ACT.Gelu_apprx_tanh)
                    nc.scalar.activation(l_x[:, j, :], pb[p][:, 1, 0:T], ACT.Identity,
                                         bias=pview("lru_b", 1)[:, j, :], scale=w[:, j, 3:4]).then_inc(lin_lin, 1)
                    if has_tail:
                        act.wait_ge(lin_tap, 3 * e)
                        nc.scalar.activation(e_hi[:, j - 1, :], l_x[:, j - 1, :], ACT.Copy).then_inc(lin_hi, 1)

                def body(b, is_first, last):
                    step(b, 0, last, not is_first)
                    step(b, 1, last, True)
                sweep(act, s, body)
                act.wait_ge(lin_tap, 3 * RC)
                nc.scalar.activation(e_hi[:, RC - 1, :], l_x[:, RC - 1, :], ACT.Copy).then_inc(lin_hi, 1)

            def lru_exps(j):
                act.wait_ge(lru_gates, j + 1)
                nc.scalar.activation(l_t[:, j, :], l_r[:, j, :], ACT.Tanh, scale=small[:, 2, j:j + 1])
                nc.scalar.activation(l_r[:, j, :], l_r[:, j, :], ACT.Exp, scale=small[:, 3, j:j + 1])\
                    .then_inc(lru_exp, 1)

            def lru_roots(f):
                part = LRU_PARTS[f]
                act.wait_ge(lru_sq, part.stop)
                t = l_t[:, part.start:part.stop, :]
                nc.scalar.activation(t, t, ACT.Sqrt).then_inc(lru_root, 1)

            def lru_highs(f):
                for j in LRU_PARTS[f]:
                    act.wait_ge(lru_y, j + 1)
                    nc.scalar.activation(e_hi[:, j, :], l_gate[:, j, :], ACT.Copy).then_inc(lru_hi, 1)

            def do_lgate(s):
                def body(b, is_first, last):
                    for p in range(2):
                        prepare(split_hi, s, b, p, last)
                        act.wait_ge(half_done, 2 * (s.g0 + 2 * b + p) + 1)
                        for k, j in enumerate(gate_chunks(b, p)):
                            nc.scalar.activation(l_r[:, j, :], gate_sum(p, 0, k), ACT.Sigmoid, bias=pcol("lru_br", j))
                        act.wait_ge(half_done, 2 * (s.g0 + 2 * b + p) + 2)
                        for k, j in enumerate(gate_chunks(b, p)):
                            nc.scalar.activation(l_i[:, j, :], gate_sum(p, 1, k), ACT.Sigmoid, bias=pcol("lru_bi", j))\
                                .then_inc(lru_gates, 1)
                sweep(act, s, body)

            def do_lru(n):
                early = LRU_PARTS[0].stop + 1
                for k in range(early):
                    lru_exps(k)
                lru_roots(0)
                for k in range(early, RC):
                    lru_exps(k)
                lru_roots(1)
                lru_highs(0)
                lru_highs(1)

            kinds = {"glu": do_glu, "q": do_q, "qr": do_q, "v": do_v, "gate": do_gate, "merge": do_merge, "out": do_residual,
                     "down": do_residual,
                     "upa": do_upa, "upb": do_upb, "lin": do_lin, "lgate": do_lgate}
            others = {"norm": do_norm, "stick": do_stick, "lru": do_lru}
            for what, s in plan:
                kinds[s.kind](s) if what == "slabs" else others[what](s)

        @block.vector
        def _(dve):
            chain = [0]

            def link(ins):
                chain[0] += 1
                ins.then_inc(dve_chain, 1)
                dve.wait_ge(dve_chain, chain[0])

            def split_lo(nx, f):
                if nx is None:
                    return
                s, b, p = nx
                g, w = s.g0 + 2 * b + p, s.width[p] // 2
                at = slice(HALF * f, HALF * f + w)
                dve.wait_ge(hi_ready, 2 * g + f + 1)
                nc.vector.tensor_tensor(w_lo[:, p, at], raw[:, p, HALF * f:HALF * f + w], w_hi[:, p, at].bitcast(F32),
                                        ALU.subtract).then_inc(lo_ready, 1)

            def columns(m, tile, v, vec, in_place, arrived=None, halves=(0, 1)):
                done = (mod_done, mod_ctx_done)[v]
                for c in halves:
                    if arrived is not None:
                        dve.wait_ge(mod_in[c], arrived)
                    if not in_place:
                        wait_up(dve, done, 2 * m + c)
                    nc.vector.scalar_tensor_tensor(out=tile[:, c, :] if in_place else unused, in0=tile[:, c, :],
                                                   scalar=1.0, in1=cact[:, vec, :], op0=ALU.mult, op1=ALU.mult,
                                                   accum_out=modcol[:, v, bass.ds(2 * m + c, 1)]).then_inc(done, 1)

            def mods(s, b, p):
                if s is first and b == 0:
                    for m in range(2 + 3 * p, 5 + 3 * p):
                        columns(m, mod_first[m % 6], 0, 0, True)
                    if p == 1:
                        one_mod(s.m0, s.m0)
                    return
                if s.mods == 2:
                    one_mod(s.m0 + 2 * b + p, s.m0)
                if s.mods == 1:
                    one_mod(s.m0 + b, s.m0, (p,))

            def one_mod(m, m0, halves=(0, 1)):
                at = m if isinstance(m, int) else m0
                if at < N_DOUBLE:
                    columns(m, modraw, 1, 1, False, 16 * (m - N_FIRST + 1), halves)
                if at >= 2 * N_MOD_A:
                    dve.wait_ge(c_ready, 4)
                columns(m, modraw, 0, int(at >= 2 * N_MOD_A), True, 16 * (m - N_FIRST + 1), halves)

            def pad_edges():
                link(nc.vector.memset(u_pad[:, :, 0:PAD], 0.0))
                link(nc.vector.memset(u_pad[:, :, PAD + T:UW], 0.0))

            dve.wait_ge(c_ready, 1)
            for m in range(N_FIRST):
                dve.wait_ge(first_in[m], 16)
                columns(m, mod_first[m % 6], 1, 1, False)
                if m < 2:
                    dve.wait_ge(c_ready, 2)
                    columns(m, mod_first[m % 6], 0, 0, True)
            dve.wait_ge(c_ready, 3)
            e_, u_, v_, p_ = small[:, 1, :], small[:, 2, :], small[:, 3, :], small[:, 0, :]
            link(nc.vector.tensor_scalar(v_, e_, 2.0, None, ALU.add))
            link(nc.vector.reciprocal(u_, v_))
            link(nc.vector.tensor_tensor(u_, u_, e_, ALU.mult))
            link(nc.vector.tensor_tensor(v_, u_, u_, ALU.mult))
            link(nc.vector.memset(p_, 1.0 / (2 * SERIES + 1)))
            for k in range(SERIES - 1, -1, -1):
                link(nc.vector.tensor_tensor(p_, p_, v_, ALU.mult))
                link(nc.vector.tensor_scalar(p_, p_, 1.0 / (2 * k + 1), None, ALU.add))
            link(nc.vector.scalar_tensor_tensor(out=p_, in0=p_, scalar=2.0, in1=u_, op0=ALU.mult, op1=ALU.mult))
            link(nc.vector.tensor_scalar(u_, pcol("lru_lam", 0, RC), -1.0, 0.0, ALU.mult, ALU.max))
            link(nc.vector.tensor_tensor(p_, p_, u_, ALU.add))
            link(nc.vector.tensor_scalar(small[:, 2, :], p_, 8.0, None, ALU.mult))
            link(nc.vector.tensor_scalar(small[:, 3, :], p_, -8.0, None, ALU.mult))
            nc.vector.memset(small[:, 0, :], EPS).then_inc(eps_set, 1)
            for g, f in ((0, 0), (0, 1), (1, 0)):
                split_lo((first, 0, g), f)

            def mod_vector(r, v, out, plus):
                if r["kind"] == "a":
                    base, bcol, w = 48 * r["l"], pcol(f"b_ada{r['l']}", 8 * v, 8), 1 if r["x"] == "ctx" else 0
                else:
                    base, bcol, w = 96 + 72 * r["l"], pcol(f"mod_b{r['l']}", 8 * v, 8), 0
                dve.wait_ge(mod_ctx_done if w else mod_done, 2 * r["need"])
                src = modcol[:, w, base + 8 * v:base + 8 * v + 8]
                link(nc.vector.scalar_tensor_tensor(out=cols[:, out, :], in0=src, scalar=plus, in1=bcol,
                                                    op0=ALU.add, op1=ALU.add))

            def newton_rsqrt(ms, rough, t, r):
                link(nc.vector.tensor_tensor(t, ms, rough, ALU.mult))
                link(nc.vector.scalar_tensor_tensor(out=t, in0=t, scalar=-0.5, in1=rough, op0=ALU.mult, op1=ALU.mult))
                link(nc.vector.scalar_tensor_tensor(out=r, in0=t, scalar=1.5, in1=rough, op0=ALU.add, op1=ALU.mult))

            def do_norm(n):
                i, x, kind, l, v = n["i"], res[n["x"]], n["kind"], n["l"], n["v"]
                if kind in ("a", "b"):
                    mod_vector(n, v, 1, 0.0)
                    mod_vector(n, v + 1, 0, 1.0)
                    gain = {("a", 0): pcol(f"norm1{l}", 0, 8), ("a", 3): pcol(f"norm2{l}", 0, 8)}[(kind, v)] \
                        if kind == "a" else pcol(f"norm_b{l}", 8 * (v // 3), 8)
                    link(nc.vector.tensor_tensor(cols[:, 0, :], cols[:, 0, :], gain, ALU.mult))
                dve.wait_ge(log_ready, i + 1)
                wait_up(dve, updated, n["x0"])
                link(nc.vector.tensor_scalar(nrm[:, 0, :], ps_t[:, 0, 0:T], 1.0 / D, EPS, ALU.mult, ALU.add))
                dve.wait_ge(std_ready, i + 1)
                newton_rsqrt(nrm[:, 0, :], nrm[:, 1, :], nrm[:, 2, :], nrm[:, 3, :])
                if n["dest"] != "h":
                    for k in range(DC):
                        o = x[:, k, :] if n["dest"] == "x" else nsq[:, k, :]
                        nc.vector.scalar_tensor_tensor(out=o, in0=x[:, k, :], scalar=pcol(f"final_{kind[1]}", k),
                                                       in1=nrm[:, 3, :], op0=ALU.mult, op1=ALU.mult)\
                            .then_inc(norm_out, 1)
                    if n["before"] is not None:
                        split_lo(late(n), 0)
                    return
                for k in range(DC + 2):
                    if k < DC:
                        nc.vector.scalar_tensor_tensor(out=nsq[:, k, :], in0=x[:, k, :], scalar=cols[:, 0, k:k + 1],
                                                       in1=nrm[:, 3, :], op0=ALU.mult, op1=ALU.mult)\
                            .then_inc(norm_ready, 1)
                    if k >= 2:
                        q = k - 2
                        dve.wait_ge(hn_hi, DC * n["ih"] + q + 1)
                        nc.vector.scalar_tensor_tensor(out=h_lo[:, q, :], in0=nsq[:, q, :], scalar=cols[:, 1, q:q + 1],
                                                       in1=h_hi[:, q, :].bitcast(F32), op0=ALU.add,
                                                       op1=ALU.subtract).then_inc(hn_lo, 1)
                if n["before"] is not None:
                    split_lo(late(n), 0)

            def do_glu(s):
                pad_edges()
                def body(b, is_first, last):
                    for p in range(2):
                        j = 2 * b + p
                        prepare(split_lo, s, b, p, last)
                        dve.wait_ge(glu_sig, s.e0 + j + 1)
                        nc.vector.tensor_tensor(u_pad[:, j, PAD:PAD + T], pb[p][:, 0, 0:T], scr[:, p, 0, :], ALU.mult)\
                            .then_inc(glu_mul, 1)
                        mods(s, b, p)
                sweep(dve, s, body)

            conv_n = CONV_C * CONV_K

            def conv_piece(l, k0, i):
                n0, n1 = CONV_AT[k0:k0 + 2]
                w = pview(f"conv_w{l}", CONV_K)
                base = conv_n * i
                if k0 == 0:
                    dve.wait_ge(glu_mul, 4 * (i + 1))
                for n in range(n0, n1):
                    t, j = n // CONV_C, n % CONV_C
                    o, u = cy[:, j, :], u_pad[:, j, t:t + T]
                    if t == 0:
                        ins = nc.vector.tensor_scalar(o, u, w[:, j, 0:1], pcol(f"conv_b{l}", j), ALU.mult, ALU.add)
                    else:
                        dve.wait_ge(conv_tap, base + n - CONV_C + 1)
                        ins = nc.vector.scalar_tensor_tensor(out=o, in0=u, scalar=w[:, j, t:t + 1], in1=o,
                                                             op0=ALU.mult, op1=ALU.add)
                    ins.then_inc(conv_tap, 1)

            conv_i = [0]

            def do_q(s):
                r = s.arg
                def body(b, is_first, last):
                    for p in range(2):
                        j = 2 * (2 * b + p)
                        prepare(split_lo, s, b, p, last)
                        if r["rope"]:
                            dve.wait_ge(r_copied, s.e0 + 2 * b + p + 1)
                            q_in, q_sw, o = scr[:, p, :, :], scr2[:, p, :, :], dst[r["dst"]][:, j:j + 2, :]
                            both = lambda name: table(name).unsqueeze(1).broadcast_to([P, 2, T])
                            link(nc.vector.stream_shuffle(q_sw, q_in, [(k + 16) % 32 for k in range(32)]))
                            link(nc.vector.tensor_tensor(o, q_in, both("cos"), ALU.mult))
                            link(nc.vector.tensor_tensor(q_sw, q_sw, both("sin"), ALU.mult))
                            nc.vector.tensor_tensor(o, o, q_sw, ALU.add).then_inc(q_roped, 1)
                        if r["conv"]:
                            conv_piece(r["conv"][0], r["conv"][1] + p, conv_i[0])
                        mods(s, b, p)
                sweep(dve, s, body)

            def do_v(s):
                def body(b, is_first, last):
                    for p in range(2):
                        prepare(split_lo, s, b, p, last)
                        if s.arg["conv"]:
                            conv_piece(s.arg["conv"][0], s.arg["conv"][1] + p, conv_i[0])
                        mods(s, b, p)
                sweep(dve, s, body)
                if s.arg["conv"]:
                    conv_i[0] += 1

            def do_gate(s):
                n_ = s.arg
                i, l, is_ctx = n_["i"], n_["l"], n_["ctx"]
                a0, keys, width = NA_H * i, 256 if is_ctx else 512, CONV_C * P
                for h in range(NA_H + 2):
                    if h < NA_H:
                        dve.wait_ge(att_s, a0 + h + 1)
                        wait_up(dve, att_t, a0 + h - 1)
                        for t in range(2):
                            if not is_ctx:
                                if t == 0:
                                    dve.wait_ge(bias_in[h % 2], 16 * (NA_H // 2 * n_["n_bias"] + h // 2 + 1))
                                nc.vector.tensor_tensor(att_p[:, h % 2, t, 0:256], pb[t][:, 1, 0:256],
                                                        bias[:, h % 2, t, :], ALU.add)
                            ins = nc.vector.tensor_copy(att_p[:, h % 2, t, keys - 256:keys],
                                                        pb[t][:, 1, keys - 256:keys])
                        link(ins)
                        link(nc.vector.tensor_reduce(small[:, 4 + h % 2, 2:4], att_p[:, h % 2, :, 0:keys], AXX, ALU.max))
                        nc.vector.tensor_scalar(small[:, 4 + h % 2, 0:2], small[:, 4 + h % 2, 2:4], -1.0, None,
                                                ALU.mult).then_inc(att_max, 1)
                    if h < LN_AT:
                        conv_piece(l, max(2 * h + 5, 6), i)
                    if 1 <= h <= NA_H:
                        j = h - 1
                        prepare(split_lo, s, j // 2, j % 2, j // 2 == s.bodies - 1)
                    if h < NA_H:
                        dve.wait_ge(att_exp, a0 + h + 1)
                        link(nc.vector.reciprocal(small[:, 6 + h % 2, 2:4], small[:, 6 + h % 2, 0:2]))
                        for t in range(2):
                            ins = nc.vector.tensor_scalar(diag[:, h % 2, t, :], table("ident"),
                                                          small[:, 6 + h % 2, 2 + t:3 + t], None, ALU.mult)
                        ins.then_inc(att_diag, 1)
                    if 1 <= h < LN_AT:
                        conv_piece(l, 2 * h + 6, i)
                    if h >= 2:
                        k = h - 2
                        r = HD * (k % 2)
                        dve.wait_ge(att_hi, a0 + k + 1)
                        nc.vector.tensor_tensor(e_lo[r:r + HD, CONV_C + k // 2, :], ps_o[r:r + HD, k % 2, 0:T],
                                                e_hi[r:r + HD, CONV_C + k // 2, :].bitcast(F32), ALU.subtract)\
                            .then_inc(att_lo, 1)
                    if h == LN_AT:
                        dve.wait_ge(ln_sum, i + 1)
                        dve.wait_ge(conv_tap, conv_n * (i + 1))
                        link(nc.vector.tensor_scalar(ln_r[:, 4, :], ps_o[:, 0, T:2 * T], 1.0 / width, None, ALU.mult))
                        mean = ln_r[:, 4:5, :].broadcast_to([P, 2, T])
                        for k in range(2):
                            nc.vector.tensor_tensor(cy[:, 2 * k:2 * k + 2, :], cy[:, 2 * k:2 * k + 2, :], mean,
                                                    ALU.subtract).then_inc(ln_centred, 1)
                    if h == LN_AT + 1:
                        dve.wait_ge(ln_var, i + 1)
                        nc.vector.tensor_scalar(ln_r[:, 0, :], ps_o[:, 1, T:2 * T], 1.0 / width, EPS, ALU.mult, ALU.add)\
                            .then_inc(ln_ms, 1)
                    if h == LN_AT + 2:
                        dve.wait_ge(ln_std, i + 1)
                        dve.wait_ge(ln_centred, 2 * (i + 1))
                        newton_rsqrt(ln_r[:, 0, :], ln_r[:, 1, :], ln_r[:, 2, :], ln_r[:, 3, :])
                        for k in range(CONV_C):
                            nc.vector.tensor_tensor(cy[:, k, :], cy[:, k, :], ln_r[:, 3, :], ALU.mult)\
                                .then_inc(ln_scaled, 1)
                    if 1 <= h <= 2 * s.bodies:
                        mods(s, (h - 1) // 2, (h - 1) % 2)
                for k in range(CONV_C):
                    dve.wait_ge(ln_hi, CONV_C * i + k + 1)
                    nc.vector.tensor_tensor(e_lo[:, k, :], ln_y[:, k, :], e_hi[:, k, :].bitcast(F32), ALU.subtract)\
                        .then_inc(ln_lo, 1)

            def do_merge(s):
                def body(b, is_first, last):
                    for p in range(2):
                        j = 2 * b + p
                        g = s.g0 + j
                        prepare(split_lo, s, b, p, last)
                        for f in range(2):
                            k = 2 * j + f
                            dve.wait_ge(half_done, 2 * g + f + 1)
                            dve.wait_ge(gm_sig, s.e0 + j + 1)
                            wait_up(dve, gm_hi, 2 * s.e0 + k - 1)
                            nc.vector.tensor_tensor(scr[:, f, :, :], pb[p][:, f, :].rearrange("p (c t) -> p c t", c=2),
                                                    gates[:, :, k, :], ALU.mult).then_inc(gm_mul, 1)
                            dve.wait_ge(gm_mul, 2 * s.e0 + k + 1)
                            nc.vector.tensor_tensor(scr2[:, 0, f, :], scr[:, f, 0, :], scr[:, f, 1, :], ALU.add)\
                                .then_inc(gm_sum, 1)
                        for f in range(2):
                            k = 2 * j + f
                            dve.wait_ge(gm_hi, 2 * s.e0 + k + 1)
                            nc.vector.tensor_tensor(e_lo[:, 8 + k, :], scr2[:, 0, f, :], e_hi[:, 8 + k, :].bitcast(F32),
                                                    ALU.subtract).then_inc(gm_lo, 1)
                        mods(s, b, p)
                sweep(dve, s, body)

            def gate_columns(r, x0):
                half = r.get("half")
                wait_up(dve, updated, x0)
                mod_vector(r, r["v"], 2, 0.0 if r["kind"] == "a" else 1.0)
                if half:
                    link(nc.vector.tensor_scalar(cols[:, 2, :], cols[:, 2, :], 0.5, None, ALU.mult))

            def add_squares(s, k):
                dve.wait_ge(sq_ready, DC * s.norm_i + k + 1)
                wait_up(dve, sq_added, ADDS * s.fused_i + k - 1)
                nc.vector.tensor_tensor(nsq[:, 0, :], nsq[:, 0, :], nsq[:, k, :], ALU.add).then_inc(sq_added, 1)

            def do_out(s):
                r = s.arg
                x = res[r["x"]]
                gate_columns(r, s.x0)

                def body(b, is_first, last):
                    for p in range(2):
                        g = s.g0 + 2 * b + p
                        urgent = last and p == 1 and s.norm_i is not None
                        if not urgent:
                            prepare(split_lo, s, b, p, last)
                        dve.wait_ge(half_done, 2 * g + 2)
                        for q in range(2):
                            k = 2 * (2 * b + p) + q
                            nc.vector.scalar_tensor_tensor(out=x[:, k, :], in0=pb[p][:, q, 0:T],
                                                           scalar=cols[:, 2, k:k + 1], in1=x[:, k, :],
                                                           op0=ALU.mult, op1=ALU.add).then_inc(updated, 1)
                        if s.norm_i is not None:
                            for k in (2 * (2 * b + p) - 2, 2 * (2 * b + p) - 1):
                                if k > 0:
                                    add_squares(s, k)
                        mods(s, b, p)
                sweep(dve, s, body)
                if s.norm_i is not None:
                    add_squares(s, ADDS)
                    split_lo(following(s, s.bodies - 1, 1, True), 1)

            def do_down(s):
                r = s.arg
                x = res[r["x"]]
                if r["part"] != 1:
                    gate_columns(r, s.x0)
                gate = cols[:, 2, :].unsqueeze(2)
                def body(b, is_first, last):
                    for p in range(2):
                        j = 2 * b + p
                        urgent = last and p == 1 and s.norm_i is not None
                        if not urgent:
                            prepare(split_lo, s, b, p, last)
                        dve.wait_ge(half_done, 2 * (s.g0 + j) + 2)
                        if r["part"] == 1:
                            dve.wait_ge(updated, s.x0 - 8 + j + 1)
                        nc.vector.scalar_tensor_tensor(out=x[:, j, :], in0=pb[p][:, 0, 0:T], scalar=gate[:, j, :],
                                                       in1=x[:, j, :], op0=ALU.mult, op1=ALU.add)\
                            .then_inc(updated, 1)
                        if s.norm_i is not None and not (is_first):
                            add_squares(s, j - 1)
                        if urgent:
                            split_lo(following(s, b, p, last), 1)
                        mods(s, b, p)
                sweep(dve, s, body)

            def do_upa(s):
                taps = pview(f"ffn_w{s.arg['l']}", 3)

                def tail_mul(e, q):
                    dve.wait_ge(up_silu, e)
                    nc.vector.tensor_tensor(scr[:, q, 0, :], scr[:, q, 0, :], scr[:, q, 1, :], ALU.mult)\
                        .then_inc(up_mul, 1)

                def tail_lo(e, q, j):
                    dve.wait_ge(up_hi, e)
                    nc.vector.tensor_tensor(e_lo[:, j, :], scr[:, q, 0, :], e_hi[:, j, :].bitcast(F32), ALU.subtract)\
                        .then_inc(up_lo, 1)

                def step(b, p, last, has_tail):
                    j = 2 * b + p
                    e = s.e0 + j
                    prepare(split_lo, s, b, p, last)
                    if has_tail:
                        tail_mul(e, 1 - p)
                    dve.wait_ge(up_lin, e + 1)
                    for n, (q, left) in enumerate(((0, 1), (1, 1), (0, 0), (1, 0))):
                        o = scr[:, p, q, 1:T] if left else scr[:, p, q, 0:T - 1]
                        i_ = pb[p][:, q, 0:T - 1] if left else pb[p][:, q, 1:T]
                        if n >= 2:
                            dve.wait_ge(up_tap, 4 * e + n - 1)
                        nc.vector.scalar_tensor_tensor(out=o, in0=i_, scalar=taps[:, FC * q + j, 0:1] if left else
                                                       taps[:, FC * q + j, 2:3], in1=o, op0=ALU.mult, op1=ALU.add)\
                            .then_inc(up_tap, 1)
                    if has_tail:
                        tail_lo(e, 1 - p, j - 1)

                def body(b, is_first, last):
                    step(b, 0, last, not is_first)
                    mods(s, b, 0)
                    step(b, 1, last, True)
                    mods(s, b, 1)
                sweep(dve, s, body)
                tail_mul(s.e0 + FC, 1)
                tail_lo(s.e0 + FC, 1, FC - 1)

            def do_upb(s):
                def tail_lo(e, q, j):
                    dve.wait_ge(upb_hi, e)
                    nc.vector.tensor_tensor(e_lo[:, j, :], scr[:, q, 1, :], e_hi[:, j, :].bitcast(F32), ALU.subtract)\
                        .then_inc(upb_lo, 1)

                def step(b, p, last, has_tail):
                    j = 2 * b + p
                    e = s.e0 + j
                    prepare(split_lo, s, b, p, last)
                    if has_tail:
                        tail_lo(e, 1 - p, j - 1)
                    dve.wait_ge(upb_silu, e + 1)
                    nc.vector.tensor_tensor(scr[:, p, 1, :], pb[p][:, 1, 0:T], scr[:, p, 0, :], ALU.mult)\
                        .then_inc(upb_mul, 1)

                def body(b, is_first, last):
                    step(b, 0, last, not is_first)
                    mods(s, b, 0)
                    step(b, 1, last, True)
                    mods(s, b, 1)
                sweep(dve, s, body)
                tail_lo(s.e0 + FC, 1, FC - 1)

            def do_stick(n):
                dve.wait_ge(masks_in, 16)
                for h in range(SB_H + 2):
                    if 1 <= h <= SB_H:
                        k = h - 1
                        dve.wait_ge(st_r, k + 1)
                        nc.vector.tensor_tensor(sb_z[:, k % 2, 1, :], pb[1][:, k % 2, 0:384], sb_z[:, k % 2, 1, :],
                                                ALU.add).then_inc(st_v, 1)
                    if h < SB_H:
                        z, w, zm = pb[0][:, h % 2, 0:384], sb_z[:, h % 2, 0, :], sb_z[:, h % 2, 1, :]
                        dve.wait_ge(st_ln, h + 1)
                        wait_up(dve, st_w, h - 1)
                        nc.vector.tensor_tensor(zm, z, masks[:, 384:768], ALU.add).then_inc(st_sp, 1)
                        nc.vector.scalar_tensor_tensor(out=w, in0=z, scalar=0.0, in1=w, op0=ALU.max, op1=ALU.add)\
                            .then_inc(st_sp, 1)
                        dve.wait_ge(st_sp, 3 * h + 2)
                        nc.vector.tensor_tensor(w, w, masks[:, 0:384], ALU.mult).then_inc(st_sp, 1)
                    if h >= 2:
                        k = h - 2
                        r = HD * (k % 2)
                        dve.wait_ge(st_hi, k + 1)
                        nc.vector.tensor_tensor(e_lo[r:r + HD, k // 2, :], ps_o[r:r + HD, k % 2, 0:T],
                                                e_hi[r:r + HD, k // 2, :].bitcast(F32), ALU.subtract)\
                            .then_inc(st_lo, 1)
                    if h < SB_H:
                        one_mod(n["m0"] + h // 2, n["m0"], (h % 2,))

            def do_lin(s):
                w = pview("lru_w", 4)

                def tail_lo(j):
                    dve.wait_ge(lin_hi, j + 1)
                    nc.vector.tensor_tensor(e_lo[:, j, :], l_x[:, j, :], e_hi[:, j, :].bitcast(F32), ALU.subtract)\
                        .then_inc(lin_lo, 1)

                def step(b, p, last, has_tail):
                    j = 2 * b + p
                    prepare(split_lo, s, b, p, last)
                    dve.wait_ge(lin_lin, j + 1)
                    for k in range(1, 4):
                        if k > 1:
                            dve.wait_ge(lin_tap, 3 * j + k - 1)
                        nc.vector.scalar_tensor_tensor(out=l_x[:, j, k:T], in0=pb[p][:, 1, 0:T - k],
                                                       scalar=w[:, j, 3 - k:4 - k], in1=l_x[:, j, k:T],
                                                       op0=ALU.mult, op1=ALU.add).then_inc(lin_tap, 1)
                    if has_tail:
                        tail_lo(j - 1)

                def body(b, is_first, last):
                    step(b, 0, last, not is_first)
                    mods(s, b, 0)
                    step(b, 1, last, True)
                    mods(s, b, 1)
                sweep(dve, s, body)
                tail_lo(RC - 1)

            def lru_square(j):
                dve.wait_ge(lru_exp, j + 1)
                link(nc.vector.tensor_tensor(l_x[:, j, :], l_r[:, j, :], l_r[:, j, :], ALU.mult))
                nc.vector.scalar_tensor_tensor(out=l_t[:, j, :], in0=l_x[:, j, :], scalar=1.0, in1=l_t[:, j, :],
                                               op0=ALU.add, op1=ALU.mult).then_inc(lru_sq, 1)

            def lru_scan(f):
                part = LRU_PARTS[f]
                at = slice(part.start, part.stop)
                dve.wait_ge(lru_root, f + 1)
                link(nc.vector.tensor_tensor(l_i[:, at, :], l_i[:, at, :], l_t[:, at, :], ALU.mult))
                for j in part:
                    ins = nc.vector.tensor_tensor_scan(l_x[:, j, :], l_r[:, j, :], l_i[:, j, :], 0.0,
                                                       ALU.mult, ALU.add)
                link(ins)
                for j in part:
                    nc.vector.tensor_tensor(l_gate[:, j, :], l_gate[:, j, :], l_x[:, j, :], ALU.mult)\
                        .then_inc(lru_y, 1)

            def lru_lows(f):
                for j in LRU_PARTS[f]:
                    dve.wait_ge(lru_hi, j + 1)
                    nc.vector.tensor_tensor(e_lo[:, j, :], l_gate[:, j, :], e_hi[:, j, :].bitcast(F32), ALU.subtract)\
                        .then_inc(lru_lo, 1)

            def lru_input(j):
                dve.wait_ge(lru_gates, j + 1)
                link(nc.vector.tensor_tensor(l_i[:, j, :], l_i[:, j, :], l_x[:, j, :], ALU.mult))

            def do_lgate(s):
                def body(b, is_first, last):
                    for p in range(2):
                        prepare(split_lo, s, b, p, last)
                        if b or p:
                            for j in gate_chunks(b - (p == 0), 1 - p):
                                lru_input(j)
                sweep(dve, s, body)
                for j in gate_chunks(s.bodies - 1, 1):
                    lru_input(j)

            def do_lru(n):
                early = LRU_PARTS[0].stop + 1
                for k in range(early):
                    lru_square(k)
                lru_scan(0)
                for k in range(early, RC):
                    lru_square(k)
                lru_lows(0)
                lru_scan(1)
                lru_lows(1)

            kinds = {"glu": do_glu, "q": do_q, "qr": do_q, "v": do_v, "gate": do_gate, "merge": do_merge, "out": do_out, "down": do_down,
                     "upa": do_upa, "upb": do_upb, "lin": do_lin, "lgate": do_lgate}
            others = {"norm": do_norm, "stick": do_stick, "lru": do_lru}
            for what, s in plan:
                kinds[s.kind](s) if what == "slabs" else others[what](s)

        @block.tensor
        def _(pe):
            ones = table("ones")
            pe.wait_ge(setup_in[1], 16)

            def mm3(out, l, r, start, stop):
                nc.tensor.matmul(out, l[0], r[0], start=start, stop=False)
                nc.tensor.matmul(out, l[0], r[1], start=False, stop=False)
                return nc.tensor.matmul(out, l[1], r[0], start=False, stop=stop)

            def sum_squares(i, k, start, stop):
                pe.wait_ge(sq_ready, DC * i + k + 1)
                return nc.tensor.matmul(ps_t[:, 0, 0:T], ones, nsq[:, k, :], start=start, stop=stop)

            def freed(s, b, p):
                j = 2 * b + p
                return {"glu": lambda: (glu_mul, s.e0 + j + 1), "q": lambda: (q_copied, s.e0 + j + 1),
                        "qr": lambda: (r_copied, s.e0 + j + 1), "v": lambda: (v_copied, s.e0 + j + 1),
                        "gate": lambda: (gate_copied, s.e0 + j + 1), "merge": lambda: (gm_mul, 2 * (s.e0 + j + 1)),
                        "out": lambda: (updated, s.x0 + 2 * j + 2), "down": lambda: (updated, s.x0 + j + 1),
                        "upa": lambda: (up_tap, 4 * (s.e0 + j + 1)), "upb": lambda: (upb_mul, s.e0 + j + 1),
                        "lin": lambda: (lin_tap, 3 * (j + 1)), "lgate": lambda: (lru_gates, gate_chunks(b, p).stop)}[s.kind]()

            def chunks(s, b, p, f):
                part = (s.arg or {}).get("part") if isinstance(s.arg, dict) else None
                if s.kind == "merge":
                    return [(e_hi[:, k, :], e_lo[:, k, :]) for k in range(DC)]
                if s.kind == "out":
                    at = 8 if s.arg["kind"] == "a" else 0
                    return [(e_hi[:, at + k, :], e_lo[:, at + k, :]) for k in range(DC)]
                if s.kind == "down":
                    at, n = FA if part == 1 else 0, s.kc // 2
                    return [(e_hi[:, at + k, :], e_lo[:, at + k, :]) for k in range(n * f, n * (f + 1))]
                if s.kind == "lgate":
                    return [(e_hi[:, j, :], e_lo[:, j, :]) for j in gate_chunks(b, p)]
                return [(h_hi[:, k, :], h_lo[:, k, :]) for k in range(DC)]

            def operands_ready(s, b, p, is_first):
                if s.kind == "merge" and p == 0 and is_first:
                    pe.wait_ge(ln_lo, s.e0 + 4)
                if s.kind == "out" and p == 0 and is_first:
                    if s.arg["kind"] == "b":
                        pe.wait_ge(st_lo, SB_H)
                if s.kind == "down" and p == 0 and is_first:
                    part = s.arg["part"]
                    if part < 2:
                        pe.wait_ge(up_lo if s.arg["kind"] == "a" else upb_lo, up_done[id(s)] + (FA if part == 0 else FC))
                if s.kind == "lgate":
                    pe.wait_ge(lin_lo, gate_chunks(b, p).stop)

            after_lru = next(s for what, s in plan if what == "slabs" and s.kind == "down" and s.arg["part"] == 2)
            gm_done, up_done, had, prior = {}, {}, {}, {}
            before = None
            for what, s in plan:
                if what == "slabs":
                    gm_done[id(s)] = 2 * had.get("merge", 0)
                    up_done[id(s)] = had.get("upa" if isinstance(s.arg, dict) and s.arg.get("kind") == "a" else "upb",
                                             0) - FC
                    had[s.kind] = s.e0 + 2 * s.bodies
                    prior[id(s)] = before
                    before = s

            def free_banks(s, b, p, is_first):
                if not is_first:
                    pe.wait_ge(*freed(s, b - 1, p))
                elif prior[id(s)] is not None:
                    q = prior[id(s)]
                    pe.wait_ge(*freed(q, q.bodies - 1, p))

            def half(s, b, p, f, is_first):
                g = s.g0 + 2 * b + p
                pe.wait_ge(lo_ready, 2 * g + f + 1)
                if s.kind == "v":
                    for k in range(4 * f, 4 * f + 4):
                        for t in range(2):
                            x = [h[:, k, t * P:(t + 1) * P] for h in (h_hi, h_lo)]
                            w = [v[:, p, 256 * k:256 * (k + 1)] for v in (w_hi, w_lo)]
                            ins = mm3(pb[p][:, t, 0:256], x, w, k == 0, k == DC - 1)
                else:
                    xs = chunks(s, b, p, f)
                    n, one = len(xs), s.kind == "down"
                    for k, x in enumerate(xs):
                        if s.after is not None and is_first and p == 0 and f == 0:
                            pe.wait_ge(hn_lo, DC * s.after["ih"] + k + 1)
                        if is_first and p == 0 and f == 0:
                            if s.kind == "merge" and k == 4:
                                pe.wait_ge(att_lo, NA_H * (s.e0 // 4 + 1))
                            if s.kind == "out" and s.arg["kind"] == "a":
                                pe.wait_ge(gm_lo, gm_done[id(s)] - DC + k + 1)
                        if s is after_lru and is_first and p == 0:
                            pe.wait_ge(lru_lo, n * f + k + 1)
                        c = HALF * f + P * k
                        if s.kind == "merge":
                            o, start, stop = pb[p][:, f, T * (k // 4):T * (k // 4 + 1)], k % 4 == 0, k % 4 == 3
                        elif s.kind == "lgate":
                            o, start, stop = gate_sum(p, f, k), True, True
                        elif s.kind == "gate":
                            o, start, stop = pb[p][:, 0, T * f:T * (f + 1)], k == 0, k == n - 1
                        else:
                            o = pb[p][:, 0 if one else f, 0:T]
                            start, stop = k == 0 and not (one and f), k == n - 1 and not (one and not f)
                        ins = mm3(o, (w_hi[:, p, c:c + P], w_lo[:, p, c:c + P]), x, start, stop)
                ins.then_inc(half_done, 1)

            def do_slabs(s):
                def body(b, is_first, last):
                    for p in range(2):
                        operands_ready(s, b, p, is_first)
                        free_banks(s, b, p, is_first)
                        for f in range(2):
                            half(s, b, p, f, is_first)
                sweep(pe, s, body)

            def do_norm(n):
                if n["fused"]:
                    pe.wait_ge(sq_added, ADDS * (n["fused_i"] + 1))
                    sum_squares(n["i"], 0, True, False)
                    ins = sum_squares(n["i"], DC - 1, False, True)
                else:
                    for k in range(DC):
                        ins = sum_squares(n["i"], k, k == 0, k == DC - 1)
                ins.then_inc(sum_ready, 1)

            def do_gate(s):
                n_ = s.arg
                i, is_ctx, a0 = n_["i"], n_["ctx"], NA_H * n_["i"]
                nk = 2 if is_ctx else 4
                pe.wait_ge(q_copied, n_["had"]["q"])
                if not is_ctx:
                    pe.wait_ge(q_roped, n_["had"]["qr"])
                pe.wait_ge(v_copied, n_["had"]["v"])
                for h in range(NA_H + 2):
                    j, k1, k2 = h - 1, h - 1, h - 2
                    slab = 1 <= h <= NA_H
                    if h < NA_H:
                        wait_up(pe, att_max, a0 + h)
                        c, r = h // 2, HD * (h % 2)
                        for t in range(2):
                            q = dst["q"][r:r + HD, c, t * P:(t + 1) * P]
                            keys = [dst["kc"]] if is_ctx else [dst["k"], dst["kc"]]
                            for n_k, k_ in enumerate(keys):
                                ins = nc.tensor.matmul(pb[t][:, 1, T * n_k:T * (n_k + 1)], q, k_[r:r + HD, c, :],
                                                       start=True, stop=True)
                        ins.then_inc(att_s, 1)
                    if slab:
                        free_banks(s, j // 2, j % 2, j < 2)
                        half(s, j // 2, j % 2, 0, j < 2)
                        pe.wait_ge(att_diag, a0 + k1 + 1)
                        wait_up(pe, att_tc, a0 + k1)
                        for t in range(2):
                            for q in range(nk):
                                ins = nc.tensor.matmul(ps_t[:, t, q * P:(q + 1) * P],
                                                       att_p[:, k1 % 2, t, q * P:(q + 1) * P], diag[:, k1 % 2, t, :],
                                                       start=True, stop=True)
                        ins.then_inc(att_t, 1)
                    if h == LN_AT:
                        pe.wait_ge(conv_tap, CONV_C * CONV_K * (i + 1))
                        for k in range(CONV_C):
                            ins = nc.tensor.matmul(ps_o[:, 0, T:2 * T], ones, cy[:, k, :], start=k == 0,
                                                   stop=k == CONV_C - 1)
                        ins.then_inc(ln_sum, 1)
                    if h == LN_AT + 1:
                        for k in range(CONV_C):
                            pe.wait_ge(ln_sq, 2 * i + k // 2 + 1)
                            ins = nc.tensor.matmul(ps_o[:, 1, T:2 * T], ones, ln_y[:, k, :], start=k == 0,
                                                   stop=k == CONV_C - 1)
                        ins.then_inc(ln_var, 1)
                    if slab:
                        half(s, j // 2, j % 2, 1, j < 2)
                    if h >= 2:
                        c, r = k2 // 2, HD * (k2 % 2)
                        pe.wait_ge(att_tc, a0 + k2 + 1)
                        wait_up(pe, att_lo, a0 + k2 - 1)
                        for q in range(nk):
                            v = (dst["vc"] if is_ctx else dst["v"])[:, q, HD * k2:HD * (k2 + 1)] if q < 2 else \
                                dst["vc"][:, q - 2, HD * k2:HD * (k2 + 1)]
                            ins = nc.tensor.matmul(ps_o[r:r + HD, k2 % 2, 0:T], v, att_pt[:, k2 % 2, q, :],
                                                   start=q == 0, stop=q == nk - 1)
                        ins.then_inc(att_o, 1)
                pe.wait_ge(att_max, a0 + NA_H)

            def do_stick(n):
                pe.wait_ge(q_copied, n["had"]["q"])
                pe.wait_ge(v_copied, n["had"]["v"])
                for h in range(SB_H + 2):
                    if h < SB_H:
                        wait_up(pe, st_sp, 3 * (h - 1))
                        c, r = h // 2, HD * (h % 2)
                        q, k_ = dst["sbq"][r:r + HD, c, :], dst["sbk"][r:r + HD, c, :]
                        nc.tensor.matmul(pb[0][:, h % 2, 0:256], k_[:, 0:P], q, start=True, stop=True)
                        nc.tensor.matmul(pb[0][:, h % 2, 256:384], k_[:, P:T], q[:, P:T], start=True, stop=True)\
                            .then_inc(st_z, 1)
                    if 1 <= h <= SB_H:
                        k = h - 1
                        pe.wait_ge(st_sp, 3 * (k + 1))
                        wait_up(pe, st_v, k - 1)
                        w, o = sb_z[:, k % 2, 0, :], pb[1][:, k % 2, :]
                        nc.tensor.matmul(o[:, 256:384], table("ntri"), w[:, 256:384], start=True, stop=True)
                        nc.tensor.matmul(o[:, 0:128], table("ntri"), w[:, 0:128], start=True, stop=True)
                        nc.tensor.matmul(o[:, 128:256], table("ntri"), w[:, 128:256], start=True, stop=False)
                        nc.tensor.matmul(o[:, 128:256], table("nones"), w[:, 256:384], start=False, stop=True)\
                            .then_inc(st_r, 1)
                    if h >= 2:
                        k = h - 2
                        r = HD * (k % 2)
                        pe.wait_ge(st_w, k + 1)
                        wait_up(pe, st_lo, k - 1)
                        v, w = dst["sbv"], sb_z[:, k % 2, 2, :]
                        v0, v1 = v[:, 0, HD * k:HD * (k + 1)], v[:, 1, HD * k:HD * (k + 1)]
                        o = ps_o[r:r + HD, k % 2, :]
                        nc.tensor.matmul(o[:, 0:128], v0, w[:, 0:128], start=True, stop=True)
                        nc.tensor.matmul(o[:, 128:256], v0, w[:, 128:256], start=True, stop=False)
                        nc.tensor.matmul(o[:, 128:256], v1, w[:, 256:384], start=False, stop=True)\
                            .then_inc(st_o, 1)

            for what, s in plan:
                if what == "slabs":
                    (do_gate if s.kind == "gate" else do_slabs)(s)
                elif what != "lru":
                    {"norm": do_norm, "stick": do_stick}[what](s)
    return nc


def _pack(w, order, group):
    k, n = w.shape[0] // P, w.shape[1] // P
    t = w.reshape(k, P, n, P).transpose(2, 1, 0, 3)[np.asarray(order)]
    t = t.reshape(len(order) // group, group, P, k * P).transpose(0, 2, 1, 3)
    return np.ascontiguousarray(t.reshape(len(order) // group, P, group * k * P))


def _pack_wide(w):
    k, n = w.shape[0] // P, w.shape[1] // 256
    return np.ascontiguousarray(w.reshape(k, P, n, 256).transpose(2, 1, 0, 3).reshape(n, P, k * 256))


def _pack_rows(w):
    return np.ascontiguousarray(w.T.reshape(-1, 2, P, w.shape[0]).transpose(0, 2, 1, 3).reshape(-1, P, 2 * w.shape[0]))


def _pairs(n, off):
    return [c for j in range(n) for c in (j, off + j)]


def _rows(v):
    return v.reshape(-1, P).T


def _taps(w):
    return w.T.reshape(-1, P, w.shape[0]).transpose(1, 0, 2).reshape(P, -1)


def _fmajor(x):
    return np.ascontiguousarray(x.T.reshape(DC, P, T).transpose(1, 0, 2))


def _tables():
    t = np.zeros((P, NTAB), np.float32)

    def put(name, v):
        at, n = TCOL[name]
        t[:, at:at + n] = v

    put("ident", np.eye(P))
    put("ones", 1.0)
    s = np.arange(P)
    put("ntri", -(s[:, None] >= s[None, :]).astype(np.float32))
    put("nones", -1.0)
    half = HD // 2
    freq = (np.float32(10000.0) ** (-np.arange(0, half, 2, dtype=np.float32) / np.float32(half))).astype(np.float32)
    tok = np.arange(T)
    pos = np.stack([tok // GRID_W, tok % GRID_W]).astype(np.float32)
    f = np.arange(P) % HD
    ang = pos[f // half] * freq[f % (half // 2)][:, None]
    put("cos", np.cos(ang))
    put("sin", np.sin(ang) * np.where(f % half < half // 2, -1.0, 1.0)[:, None])
    return t


def _masks():
    q = np.concatenate([np.arange(T), np.arange(P)])
    keep = (np.arange(P)[:, None] < q[None, :]).astype(np.float32)
    return np.concatenate([keep, np.where(keep > 0, 0.0, -1e30).astype(np.float32)], 1)


def _relative_bias(rpb):
    t = np.arange(T)
    row, col = t // GRID_W, t % GRID_W
    start = np.clip(col - 8, 0, GRID_W - 16)
    inside = (col[None, :] >= start[:, None]) & (col[None, :] < start[:, None] + 16)
    dr = row[None, :] - row[:, None] + 7
    dc = np.where(inside, col[None, :] - col[:, None] + 15, 0)
    b = np.where(inside[None], rpb[:, dr, dc], np.float32(-1e30))
    return np.ascontiguousarray(b.reshape(NA_H, 2, P, T).transpose(0, 2, 1, 3))


def arrays_of(i):
    a = {"x": _fmajor(i["x"][0]), "ctx": _fmajor(i["ctx"][0])}
    par = np.zeros((P, NPARAM), np.float32)

    def put(name, v):
        at, n = PCOL[name]
        par[:, at:at + n] = v

    mod, bias = [], []
    for l in range(2):
        put(f"b_ada{l}", _rows(i["b_ada"][l]))
        put(f"norm1{l}", _rows(i["norm1_g"][l]))
        put(f"norm2{l}", _rows(i["norm2_g"][l]))
        put(f"conv_w{l}", _taps(i["conv_dw"][l]))
        put(f"conv_b{l}", _rows(i["conv_dw_b"][l]))
        put(f"ln_g{l}", _rows(i["conv_ln_g"][l]))
        put(f"ln_b{l}", _rows(i["conv_ln_b"][l]))
        put(f"ffn_w{l}", _taps(i["ffn_dw"][l]))
        put(f"ffn_b{l}", _rows(i["ffn_dw_b"][l]))
        put(f"mod_b{l}", _rows(i["mod_b_2"][l]))
        put(f"norm_b{l}", _rows(i["norm_g_2"][l].reshape(-1)))
        w = i["w_in"][l]
        a[f"w_glu{l}"] = _pack(w, _pairs(4, 4), 2)
        a[f"w_q{l}"] = _pack(w, range(8, 12), 2)
        a[f"w_k{l}"] = _pack(w, range(12, 16), 2)
        a[f"w_v{l}"] = _pack_wide(w[:, 2048:2560])
        a[f"w_gate{l}"] = _pack(w[:, 2560:], _pairs(8, 8), 2)
        a[f"w_merge{l}"] = np.concatenate([_pack(i["w_conv_out"][l], range(8), 1),
                                           _pack(i["w_na_out"][l], range(8), 1)], 2)\
            .reshape(4, 2, P, HALF).transpose(0, 2, 1, 3).reshape(4, P, SLAB)
        a[f"w_out{l}"] = _pack(i["w_out"][l], range(8), 2)
        a[f"w_up{l}"] = _pack(i["w_up"][l], _pairs(FC, FC), 2)
        a[f"w_down{l}0"] = _pack(i["w_down"][l][:FA * P], range(8), 1)
        a[f"w_down{l}1"] = _pack(i["w_down"][l][FA * P:], range(8), 1)
        for f in range(2):
            a[f"w_gu{l}{f}"] = _pack(i["ffn_w_gu_2"][l, f], _pairs(FC, FC), 2)
            a[f"w_dn{l}{f}0"] = _pack(i["ffn_w_down_2"][l, f][:FA * P], range(8), 1)
            a[f"w_dn{l}{f}1"] = _pack(i["ffn_w_down_2"][l, f][FA * P:], range(8), 1)
        bias.append(_relative_bias(i["na_rpb"][l]))
    a["w_mod"] = np.concatenate([_pack_rows(i["w_ada"][l]) for l in range(2)]
                                + [_pack_rows(i["mod_w_2"][l]) for l in range(2)], 0)
    vectors = np.concatenate([i["c"][0], i["c_ctx"], i["c_2"][0]])
    a["vectors"] = np.ascontiguousarray(np.broadcast_to(vectors, (P, 3 * D)))
    qkv = i["sb_w_qkv_2"][0]
    a["w_sbq"] = _pack(qkv, range(8), 2)
    a["w_sbk"] = _pack(qkv, range(8, 16), 2)
    a["w_sbv"] = _pack_wide(qkv[:, 2048:])
    a["w_sbo"] = _pack(i["sb_w_o_2"][0], range(8), 2)
    a["w_lin"] = _pack(i["lru_w_in_2"][0], _pairs(RC, RC), 2)
    lg = np.stack([i["lru_w_r_2"][0], i["lru_w_i_2"][0]]).reshape(2, -1, sum(LRU_SLAB), P, P)
    for p, at in enumerate((slice(0, LRU_SLAB[0]), slice(LRU_SLAB[0], None))):
        a[f"w_lg{p}"] = np.ascontiguousarray(lg[:, :, at].transpose(1, 3, 0, 2, 4).reshape(lg.shape[1], P, -1))
    a["w_lout"] = _pack(i["lru_w_out_2"][0], range(8), 1)
    put("final_a", _rows(i["final_norm_g"]))
    put("final_b", _rows(i["final_norm_g_2"]))
    put("lru_w", _taps(i["lru_conv_w_2"][0]))
    put("lru_b", _rows(i["lru_conv_b_2"][0]))
    put("lru_br", _rows(i["lru_b_r_2"][0]))
    put("lru_bi", _rows(i["lru_b_i_2"][0]))
    put("lru_lam", _rows(i["lru_lambda_2"][0]))
    a["params"], a["tables"], a["rel_bias"] = par, _tables(), np.stack(bias)
    a["masks"] = _masks()
    return a


def kernel(**inputs):
    import concourse.bacc as bacc
    from concourse.bass_utils import run_bass_kernel_spmd

    host = arrays_of({k: np.asarray(v) for k, v in inputs.items()})
    nc = bacc.Bacc("TRN2", target_bir_lowering=False, num_devices=1)
    aps = {k: nc.dram_tensor(f"in_{k}", v.shape, F32, kind="ExternalInput").ap() for k, v in host.items()}
    aps["y"] = nc.dram_tensor("y", (P, DC, T), F32, kind="ExternalOutput").ap()
    build(nc, aps)
    r = run_bass_kernel_spmd(nc, [{f"in_{k}": v for k, v in host.items()}], core_ids=[0])
    y = r.results[0]["y"]
    return np.ascontiguousarray(y.transpose(1, 0, 2).reshape(D, T).T).reshape(1, T, D)
```
